# Optimizing a Trainium2 kernel written in Bass

```python
import math
import jax, jax.numpy as jnp
from jax import lax
import numpy as np

D_MODEL = 1024
BATCH = 1
SEQ = 256
DEPTH = 2

EPS = 1e-6
ROPE_THETA = 10000.0
D_FF = 2816
CONV_K = 4
BLOCK = 128

D_MIX = 2 * D_MODEL
SSD_WIDTH = D_MIX // 2
SSD_HEAD_DIM = 64
SSD_HEADS = SSD_WIDTH // SSD_HEAD_DIM
SSD_GROUPS = 2
SSD_STATE = 128
SSD_CONV_DIM = SSD_WIDTH + 2 * SSD_GROUPS * SSD_STATE
SSD_CHUNK = 128
ML_WIDTH = D_MIX - SSD_WIDTH
ML_HEADS = 4
ML_V_DIM = ML_WIDTH // ML_HEADS
ML_QK_DIM = ML_V_DIM // 2
ML_CHUNK = 128
HY_SPLITS = (SSD_WIDTH, SSD_CONV_DIM, SSD_HEADS, ML_HEADS * ML_QK_DIM, ML_HEADS * ML_QK_DIM,
             ML_WIDTH, ML_WIDTH, ML_HEADS, ML_HEADS)
HY_IN = sum(HY_SPLITS)

ATT_HEAD_DIM = 64
ATT_HEADS = D_MODEL // ATT_HEAD_DIM
IDX_HEADS = ATT_HEADS // 2
IDX_DIM = ATT_HEAD_DIM
TOPK_MAX = 256
SA_SPLITS = (ATT_HEADS * ATT_HEAD_DIM, ATT_HEAD_DIM, ATT_HEAD_DIM, IDX_HEADS * IDX_DIM, IDX_DIM, IDX_HEADS)
SA_IN = sum(SA_SPLITS)

N_EVEN = (DEPTH + 1) // 2
N_ODD = DEPTH // 2


def split_cols(y, sizes):
    bounds, acc = [], 0
    for s in sizes[:-1]:
        acc += s
        bounds.append(acc)
    return jnp.split(y, bounds, axis=-1)

def rms_norm(x, g):
    xf = x.astype(jnp.float32)
    y = xf * lax.rsqrt(jnp.mean(xf * xf, axis=-1, keepdims=True) + EPS) * g.astype(jnp.float32)
    return y.astype(x.dtype)

def swiglu(h, w_gate, w_up, w_down):
    return (jax.nn.silu(h @ w_gate) * (h @ w_up)) @ w_down

def rope_tables(positions, dim):
    inv = ROPE_THETA ** (-jnp.arange(0, dim, 2, dtype=jnp.float32) / dim)
    ang = positions.astype(jnp.float32)[..., None] * inv
    return jnp.cos(ang), jnp.sin(ang)

def apply_rope(x, cos, sin):
    half = x.shape[-1] // 2
    xf = x.astype(jnp.float32)
    x1, x2 = xf[..., :half], xf[..., half:]
    c, s = cos[:, :, None, :], sin[:, :, None, :]
    return jnp.concatenate([x1 * c - x2 * s, x1 * s + x2 * c], axis=-1).astype(x.dtype)

def causal_dwconv(u, w, bias):
    L, K = u.shape[1], w.shape[0]
    up = jnp.pad(u, ((0, 0), (K - 1, 0), (0, 0)))
    return sum(up[:, k:k + L] * w[k] for k in range(K)) + bias

def ssd_chunked(x, dt, A, B, C, chunk):
    b, L, H, P = x.shape
    G, N = B.shape[-2:]
    E, nc = H // G, L // chunk
    a = (dt * A).reshape(b, nc, chunk, G, E)
    xd = (x * dt[..., None]).reshape(b, nc, chunk, G, E, P)
    B = B.reshape(b, nc, chunk, G, N)
    C = C.reshape(b, nc, chunk, G, N)
    acs = jnp.cumsum(a, axis=2)
    seg = acs[:, :, :, None] - acs[:, :, None, :]
    mask = jnp.tril(jnp.ones((chunk, chunk), bool))[:, :, None, None]
    Lm = jnp.exp(jnp.where(mask, seg, -jnp.inf))
    CB = jnp.einsum('bctgn,bcsgn->bctsg', C, B)
    y_diag = jnp.einsum('bctsg,bctsge,bcsgep->bctgep', CB, Lm, xd)
    decay_end = jnp.exp(acs[:, :, -1:] - acs)
    s_loc = jnp.einsum('bcsgn,bcsge,bcsgep->bcgepn', B, decay_end, xd)
    chunk_decay = jnp.exp(acs[:, :, -1])

    def step(hc, inp):
        dec, s = inp
        return hc * dec[..., None, None] + s, hc

    h0 = jnp.zeros((b, G, E, P, N), jnp.float32)
    _, h_in = lax.scan(step, h0, (jnp.moveaxis(chunk_decay, 1, 0), jnp.moveaxis(s_loc, 1, 0)))
    h_in = jnp.moveaxis(h_in, 0, 1)
    y_off = jnp.einsum('bctgn,bcgepn,bctge->bctgep', C, h_in, jnp.exp(acs))
    return (y_diag + y_off).reshape(b, L, H, P)

def mlstm_chunked(q, k, v, i_pre, f_pre, chunk):
    b, L, H, dk = q.shape
    dv = v.shape[-1]
    nc = L // chunk
    q = (q.astype(jnp.float32) * dk ** -0.5).reshape(b, nc, chunk, H, dk)
    k = k.astype(jnp.float32).reshape(b, nc, chunk, H, dk)
    v = v.astype(jnp.float32).reshape(b, nc, chunk, H, dv)
    li = i_pre.astype(jnp.float32).reshape(b, nc, chunk, H)
    lf = jax.nn.log_sigmoid(f_pre.astype(jnp.float32)).reshape(b, nc, chunk, H)
    bcs = jnp.cumsum(lf, axis=2)
    b_last = bcs[:, :, -1]
    g = b_last[:, :, None] - bcs + li
    m_loc = jnp.max(g, axis=2)
    wg = jnp.exp(g - m_loc[:, :, None])
    c_loc = jnp.einsum('bcsh,bcshv,bcshk->bchvk', wg, v, k)
    n_loc = jnp.einsum('bcsh,bcshk->bchk', wg, k)

    def step(carry, inp):
        Cs, ns, ms = carry
        bl, cl, nl, ml = inp
        m_new = jnp.maximum(bl + ms, ml)
        a = jnp.exp(bl + ms - m_new)
        gg = jnp.exp(ml - m_new)
        new = (a[..., None, None] * Cs + gg[..., None, None] * cl,
               a[..., None] * ns + gg[..., None] * nl, m_new)
        return new, (Cs, ns, ms)

    init = (jnp.zeros((b, H, dv, dk), jnp.float32), jnp.zeros((b, H, dk), jnp.float32),
            jnp.zeros((b, H), jnp.float32))
    xs = tuple(jnp.moveaxis(t, 1, 0) for t in (b_last, c_loc, n_loc, m_loc))
    _, (c_in, n_in, m_in) = lax.scan(step, init, xs)
    c_in, n_in, m_in = (jnp.moveaxis(t, 0, 1) for t in (c_in, n_in, m_in))
    Dm = bcs[:, :, :, None, :] - bcs[:, :, None, :, :] + li[:, :, None, :, :]
    mask = jnp.tril(jnp.ones((chunk, chunk), bool))[:, :, None]
    Dm = jnp.where(mask, Dm, -jnp.inf)
    inter = bcs + m_in[:, :, None, :]
    m_t = jnp.maximum(jnp.max(Dm, axis=3), inter)
    S = jnp.einsum('bcthk,bcshk->bctsh', q, k) * jnp.exp(Dm - m_t[:, :, :, None, :])
    w_inter = jnp.exp(inter - m_t)
    num = jnp.einsum('bctsh,bcshv->bcthv', S, v) + w_inter[..., None] * jnp.einsum('bcthk,bchvk->bcthv', q, c_in)
    den = jnp.sum(S, axis=3) + w_inter * jnp.einsum('bcthk,bchk->bcth', q, n_in)
    h = num / jnp.maximum(jnp.abs(den), jnp.exp(-m_t))[..., None]
    return h.reshape(b, L, H, dv)

def hybrid_mixer(h, w_in, conv_w, conv_b, dt_bias, a_log, d_skip, ssd_norm,
                 igate_bias, fgate_bias, mlstm_norm, w_out):
    b, L, _ = h.shape
    z, xbc, dt_raw, qm, km, vm, om, ig, fg = split_cols(h @ w_in, HY_SPLITS)
    xbc = jax.nn.silu(causal_dwconv(xbc, conv_w, conv_b))
    xs, bm, cm = split_cols(xbc, (SSD_WIDTH, SSD_GROUPS * SSD_STATE, SSD_GROUPS * SSD_STATE))
    xs = xs.reshape(b, L, SSD_HEADS, SSD_HEAD_DIM).astype(jnp.float32)
    dt = jax.nn.softplus(dt_raw.astype(jnp.float32) + dt_bias.astype(jnp.float32))
    A = -jnp.exp(a_log.astype(jnp.float32))
    y = ssd_chunked(xs, dt, A,
                    bm.reshape(b, L, SSD_GROUPS, SSD_STATE).astype(jnp.float32),
                    cm.reshape(b, L, SSD_GROUPS, SSD_STATE).astype(jnp.float32), SSD_CHUNK)
    y = y + xs * d_skip.astype(jnp.float32)[:, None]
    gate = jax.nn.silu(z.astype(jnp.float32)).reshape(b, L, SSD_GROUPS, -1)
    y = rms_norm(y.reshape(b, L, SSD_GROUPS, -1) * gate, ssd_norm.reshape(SSD_GROUPS, -1))
    y = y.reshape(b, L, SSD_WIDTH)
    hm = mlstm_chunked(qm.reshape(b, L, ML_HEADS, ML_QK_DIM), km.reshape(b, L, ML_HEADS, ML_QK_DIM),
                       vm.reshape(b, L, ML_HEADS, ML_V_DIM), ig + igate_bias, fg + fgate_bias, ML_CHUNK)
    hm = rms_norm(hm, mlstm_norm.reshape(ML_HEADS, ML_V_DIM)).reshape(b, L, ML_WIDTH)
    hm = hm * jax.nn.sigmoid(om.astype(jnp.float32))
    return jnp.concatenate([y, hm], axis=-1).astype(h.dtype) @ w_out

def sparse_attention(h, cos, sin, w_in, q_norm, k_norm, w_out, topk):
    b, L, _ = h.shape
    q, k, v, qi, ki, wi = split_cols(h @ w_in, SA_SPLITS)
    q = apply_rope(rms_norm(q.reshape(b, L, ATT_HEADS, ATT_HEAD_DIM), q_norm), cos, sin)
    k = apply_rope(rms_norm(k, k_norm)[:, :, None, :], cos, sin)[:, :, 0]
    qi = apply_rope(qi.reshape(b, L, IDX_HEADS, IDX_DIM), cos, sin)
    ki = apply_rope(ki[:, :, None, :], cos, sin)[:, :, 0]
    kv = jnp.concatenate([k, v], axis=-1)
    nb = L // BLOCK
    key_pos = jnp.arange(L)
    idx_scale = (IDX_HEADS ** -0.5) * (IDX_DIM ** -0.5)
    att_scale = ATT_HEAD_DIM ** -0.5

    def to_blocks(t):
        return jnp.moveaxis(t.reshape(b, nb, BLOCK, *t.shape[2:]), 1, 0)

    def block(args):
        j, qb, qib, wib = args
        q_pos = j * BLOCK + jnp.arange(BLOCK)
        logits = jnp.einsum('bthd,bsd->btsh', qib, ki).astype(jnp.float32)
        score = jnp.einsum('btsh,bth->bts', jax.nn.relu(logits), wib.astype(jnp.float32)) * idx_scale
        causal = key_pos[None, :] <= q_pos[:, None]
        score = jnp.where(causal[None], score, -jnp.inf)
        _, sel = lax.top_k(score, topk)
        valid = sel <= q_pos[None, :, None]
        kv_sel = jax.vmap(lambda kvb, sb: kvb[sb])(kv, sel)
        k_sel, v_sel = kv_sel[..., :ATT_HEAD_DIM], kv_sel[..., ATT_HEAD_DIM:]
        s = jnp.einsum('bthd,btkd->bthk', qb, k_sel).astype(jnp.float32) * att_scale
        s = jnp.where(valid[:, :, None, :], s, -jnp.inf)
        p = jax.nn.softmax(s, axis=-1).astype(v_sel.dtype)
        return jnp.einsum('bthk,btkd->bthd', p, v_sel)

    o = lax.map(block, (jnp.arange(nb), to_blocks(q), to_blocks(qi), to_blocks(wi)))
    o = jnp.moveaxis(o, 0, 1).reshape(b, L, ATT_HEADS * ATT_HEAD_DIM)
    return o @ w_out

def first_inputs(seed: int = 0) -> dict:
    key = jax.random.key(seed)
    ks = jax.random.split(key, 24)
    f32 = jnp.float32

    def nrm(k, shape, scale):
        return jax.random.normal(k, shape, f32) * scale

    def gain(k, shape):
        return 1.0 + 0.02 * jax.random.normal(k, shape, f32)

    x = nrm(ks[0], (BATCH, SEQ, D_MODEL), 1.0)
    positions = (jax.random.randint(ks[1], (BATCH, 1), 0, 4096, jnp.int32)
                 + jnp.arange(SEQ, dtype=jnp.int32)[None, :])
    dt0 = jnp.exp(jax.random.uniform(ks[10], (N_EVEN, SSD_HEADS), f32, math.log(1e-3), math.log(1e-1)))
    return {
        "x": x,
        "positions": positions,
        "ffn_norm": gain(ks[2], (DEPTH, 2, D_MODEL)),
        "ffn_w_gate": nrm(ks[3], (DEPTH, 2, D_MODEL, D_FF), D_MODEL ** -0.5),
        "ffn_w_up": nrm(ks[4], (DEPTH, 2, D_MODEL, D_FF), D_MODEL ** -0.5),
        "ffn_w_down": nrm(ks[5], (DEPTH, 2, D_FF, D_MODEL), D_FF ** -0.5),
        "mix_norm": gain(ks[6], (DEPTH, D_MODEL)),
        "hy_w_in": nrm(ks[7], (N_EVEN, D_MODEL, HY_IN), D_MODEL ** -0.5),
        "hy_conv_w": nrm(ks[8], (N_EVEN, CONV_K, SSD_CONV_DIM), CONV_K ** -0.5),
        "hy_conv_b": nrm(ks[9], (N_EVEN, SSD_CONV_DIM), 0.01),
        "hy_dt_bias": jnp.log(jnp.expm1(dt0)),
        "hy_a_log": jnp.log(jax.random.uniform(ks[11], (N_EVEN, SSD_HEADS), f32, 1.0, 16.0)),
        "hy_d_skip": gain(ks[12], (N_EVEN, SSD_HEADS)),
        "hy_ssd_norm": gain(ks[13], (N_EVEN, SSD_WIDTH)),
        "hy_igate_bias": nrm(ks[14], (N_EVEN, ML_HEADS), 0.1),
        "hy_fgate_bias": jnp.linspace(3.0, 6.0, ML_HEADS, dtype=f32)[None, :] + nrm(ks[15], (N_EVEN, ML_HEADS), 0.1),
        "hy_mlstm_norm": gain(ks[16], (N_EVEN, ML_WIDTH)),
        "hy_w_out": nrm(ks[17], (N_EVEN, D_MIX, D_MODEL), D_MIX ** -0.5),
        "sa_w_in": nrm(ks[18], (N_ODD, D_MODEL, SA_IN), D_MODEL ** -0.5),
        "sa_q_norm": gain(ks[19], (N_ODD, ATT_HEAD_DIM)),
        "sa_k_norm": gain(ks[20], (N_ODD, ATT_HEAD_DIM)),
        "sa_w_out": nrm(ks[21], (N_ODD, ATT_HEADS * ATT_HEAD_DIM, D_MODEL), (ATT_HEADS * ATT_HEAD_DIM) ** -0.5),
    }

def first_block(x, positions, ffn_norm, ffn_w_gate, ffn_w_up, ffn_w_down, mix_norm,
              hy_w_in, hy_conv_w, hy_conv_b, hy_dt_bias, hy_a_log, hy_d_skip, hy_ssd_norm,
              hy_igate_bias, hy_fgate_bias, hy_mlstm_norm, hy_w_out,
              sa_w_in, sa_q_norm, sa_k_norm, sa_w_out):
    cos, sin = rope_tables(positions, ATT_HEAD_DIM)
    topk = min(TOPK_MAX, x.shape[1] // 4)
    for l in range(DEPTH):
        x = x + 0.5 * swiglu(rms_norm(x, ffn_norm[l, 0]), ffn_w_gate[l, 0], ffn_w_up[l, 0], ffn_w_down[l, 0])
        h = rms_norm(x, mix_norm[l])
        if l % 2 == 0:
            e = l // 2
            m = hybrid_mixer(h, hy_w_in[e], hy_conv_w[e], hy_conv_b[e], hy_dt_bias[e], hy_a_log[e],
                             hy_d_skip[e], hy_ssd_norm[e], hy_igate_bias[e], hy_fgate_bias[e],
                             hy_mlstm_norm[e], hy_w_out[e])
        else:
            o = l // 2
            m = sparse_attention(h, cos, sin, sa_w_in[o], sa_q_norm[o], sa_k_norm[o], sa_w_out[o], topk)
        x = x + m
        x = x + 0.5 * swiglu(rms_norm(x, ffn_norm[l, 1]), ffn_w_gate[l, 1], ffn_w_up[l, 1], ffn_w_down[l, 1])
    return x


GRID_W = 64
NA_HEADS = 8
NA_HEAD_DIM = 64
NA_WIN_R = 8
NA_WIN_C = 16
NA_QCOLS = 16
NA_KCOLS = 2 * NA_WIN_C
GLA_HEADS = 4
GLA_DK = 64
GLA_DV = 128
GLA_GATE_RANK = 16
GLA_GATE_TAU = 16.0
GLA_CHUNK = 64
MLA_HEADS = 4
MLA_Q_RANK = 256
MLA_KV_RANK = 256
MLA_NOPE = 128
MLA_ROPE = 64
MLA_V = 128
MLA_QBLOCK = 128
N_BRANCH = 3
NA_W = NA_HEADS * NA_HEAD_DIM
GLA_QK_W = GLA_HEADS * GLA_DK
GLA_V_W = GLA_HEADS * GLA_DV
MLA_QK_HEAD = MLA_NOPE + MLA_ROPE
MLA_V_W = MLA_HEADS * MLA_V
IN_SPLITS = (NA_W, NA_W, NA_W,
             GLA_QK_W, GLA_QK_W, GLA_V_W, GLA_V_W, GLA_GATE_RANK, GLA_GATE_RANK,
             MLA_Q_RANK, MLA_KV_RANK, MLA_ROPE,
             N_BRANCH * D_MODEL)
D_IN = 6752


def rms_norm_2(x, g):
    xf = x.astype(jnp.float32)
    y = xf * lax.rsqrt(jnp.mean(xf * xf, axis=-1, keepdims=True) + EPS)
    return (y * g.astype(jnp.float32)).astype(x.dtype)

def swiglu_2(h, w1, w3, w2):
    return (jax.nn.silu(h @ w1) * (h @ w3)) @ w2

def split_cols_2(z, sizes):
    out, start = [], 0
    for n in sizes:
        out.append(z[..., start:start + n])
        start += n
    return out

def neighborhood_attention(q, k, v, rpb):
    B, S, H, d = q.shape
    rows = S // GRID_W
    win_r = min(NA_WIN_R, rows)
    nj = GRID_W // NA_QCOLS
    r = np.arange(rows)
    r0 = np.clip(r - win_r // 2, 0, rows - win_r)
    ridx = r0[:, None] + np.arange(win_r)
    j = np.arange(nj)
    k0 = np.clip(j * NA_QCOLS - NA_WIN_C // 2, 0, GRID_W - NA_KCOLS)
    cidx = k0[:, None] + np.arange(NA_KCOLS)
    qc = j[:, None] * NA_QCOLS + np.arange(NA_QCOLS)
    c0 = np.clip(qc - NA_WIN_C // 2, 0, GRID_W - NA_WIN_C)
    col_ok = (cidx[:, None, :] >= c0[..., None]) & (cidx[:, None, :] < c0[..., None] + NA_WIN_C)
    mask = np.broadcast_to(col_ok[:, :, None, :], (nj, NA_QCOLS, win_r, NA_KCOLS)).reshape(nj, NA_QCOLS, win_r * NA_KCOLS)
    dr = ridx - r[:, None] + (NA_WIN_R - 1)
    dc = np.clip(cidx[:, None, :] - qc[:, :, None] + (NA_WIN_C - 1), 0, 2 * NA_WIN_C - 2)
    bias = rpb[:, dr[:, None, None, :, None], dc[None, :, :, None, :]]
    bias = bias.reshape(H, rows, nj, NA_QCOLS, win_r * NA_KCOLS)

    ri = ridx[:, None, :, None]
    ci = cidx[None, :, None, :]
    kg = k.reshape(B, rows, GRID_W, H, d)[:, ri, ci].reshape(B, rows, nj, win_r * NA_KCOLS, H, d)
    vg = v.reshape(B, rows, GRID_W, H, d)[:, ri, ci].reshape(B, rows, nj, win_r * NA_KCOLS, H, d)
    qg = q.reshape(B, rows, nj, NA_QCOLS, H, d)
    s = jnp.einsum('brjqhd,brjkhd->bhrjqk', qg, kg).astype(jnp.float32) * (d ** -0.5)
    s = jnp.where(mask, s + bias.astype(jnp.float32), -1e30)
    p = jax.nn.softmax(s, axis=-1).astype(v.dtype)
    o = jnp.einsum('bhrjqk,brjkhd->brjqhd', p, vg)
    return o.reshape(B, S, H * d)

def gla_chunked(q, k, v, g, strict):
    B, H, S, dk = q.shape
    dv = v.shape[-1]
    n = S // GLA_CHUNK
    q = q.reshape(B, H, n, GLA_CHUNK, dk)
    k = k.reshape(B, H, n, GLA_CHUNK, dk)
    g = g.reshape(B, H, n, GLA_CHUNK, dk)
    v = v.reshape(B, H, n, GLA_CHUNK, dv)
    b = jnp.cumsum(g, axis=3)
    b_last = b[:, :, :, -1:, :]
    qe = q * jnp.exp(b)
    ke = k * jnp.exp(-b)
    k_end = k * jnp.exp(b_last - b)
    tri = np.tril(np.ones((GLA_CHUNK, GLA_CHUNK), dtype=bool), -1 if strict else 0)
    a = jnp.where(tri, jnp.einsum('bhnid,bhnjd->bhnij', qe, ke), 0.0)
    o_intra = jnp.einsum('bhnij,bhnjv->bhniv', a, v)
    upd = jnp.einsum('bhncd,bhncv->bhndv', k_end, v)
    decay = jnp.exp(b_last[:, :, :, 0, :])

    def step(state, inp):
        dec, u = inp
        return dec[..., None] * state + u, state

    init = jnp.zeros((B, H, dk, dv), q.dtype)
    _, s_prev = lax.scan(step, init, (jnp.moveaxis(decay, 2, 0), jnp.moveaxis(upd, 2, 0)))
    s_prev = jnp.moveaxis(s_prev, 0, 2)
    o = o_intra + jnp.einsum('bhnid,bhndv->bhniv', qe, s_prev)
    return o.reshape(B, H, S, dv)

def gla_bidirectional(q, k, v, g_fwd, g_bwd):
    t = lambda a: jnp.swapaxes(a.astype(jnp.float32), 1, 2)
    q, k, v, g_fwd, g_bwd = t(q), t(k), t(v), t(g_fwd), t(g_bwd)
    q = q * (GLA_DK ** -0.5)
    flip = lambda a: a[:, :, ::-1]
    o_f = gla_chunked(q, k, v, g_fwd, False)
    o_b = flip(gla_chunked(flip(q), flip(k), flip(v), flip(g_bwd), True))
    return jnp.swapaxes(o_f + o_b, 1, 2)

def rope_tables_2(S):
    half = MLA_ROPE // 2
    inv = ROPE_THETA ** (-jnp.arange(half, dtype=jnp.float32) / half)
    ang = jnp.arange(S, dtype=jnp.float32)[:, None] * inv[None, :]
    return jnp.cos(ang), jnp.sin(ang)

def apply_rope_2(x, cos, sin):
    xf = x.astype(jnp.float32)
    x1, x2 = xf[..., :MLA_ROPE // 2], xf[..., MLA_ROPE // 2:]
    c, s = cos[None, :, None, :], sin[None, :, None, :]
    return jnp.concatenate([x1 * c - x2 * s, x1 * s + x2 * c], axis=-1).astype(x.dtype)

def blocked_softmax_attention(q, k, v, scale):
    B, S, H, dq = q.shape
    nb = S // MLA_QBLOCK
    qb = jnp.moveaxis(q.reshape(B, nb, MLA_QBLOCK, H, dq), 1, 0)

    def one(qblk):
        s = jnp.einsum('bqhd,bkhd->bhqk', qblk, k).astype(jnp.float32) * scale
        p = jax.nn.softmax(s, axis=-1).astype(v.dtype)
        return jnp.einsum('bhqk,bkhd->bqhd', p, v)

    o = lax.map(one, qb)
    return jnp.moveaxis(o, 0, 1).reshape(B, S, H * v.shape[-1])

def mla_attention(c_q, c_kv, k_rope, cq_norm, ckv_norm, w_uq, w_ukv, q_norm, k_norm, cos, sin):
    B, S, _ = c_q.shape
    q = (rms_norm_2(c_q, cq_norm) @ w_uq).reshape(B, S, MLA_HEADS, MLA_QK_HEAD)
    kv = (rms_norm_2(c_kv, ckv_norm) @ w_ukv).reshape(B, S, MLA_HEADS, MLA_NOPE + MLA_V)
    k_nope, v = kv[..., :MLA_NOPE], kv[..., MLA_NOPE:]
    k_r = jnp.broadcast_to(k_rope[:, :, None, :], (B, S, MLA_HEADS, MLA_ROPE))
    k = jnp.concatenate([k_nope, k_r], axis=-1)
    q = rms_norm_2(q, q_norm)
    k = rms_norm_2(k, k_norm)
    q = jnp.concatenate([q[..., :MLA_NOPE], apply_rope_2(q[..., MLA_NOPE:], cos, sin)], axis=-1)
    k = jnp.concatenate([k[..., :MLA_NOPE], apply_rope_2(k[..., MLA_NOPE:], cos, sin)], axis=-1)
    return blocked_softmax_attention(q, k, v, MLA_QK_HEAD ** -0.5)

def second_inputs(seed: int = 0) -> dict:
    key = jax.random.key(seed)
    ks = iter(jax.random.split(key, 32))
    L = DEPTH
    f32 = jnp.float32

    def w(shape, fan_in):
        return jax.random.normal(next(ks), shape, f32) * (fan_in ** -0.5)

    def gain(shape):
        return 1.0 + 0.05 * jax.random.normal(next(ks), shape, f32)

    def small(shape, scale, offset=0.0):
        return offset + scale * jax.random.normal(next(ks), shape, f32)

    return {
        "x": jax.random.normal(next(ks), (BATCH, SEQ, D_MODEL), f32),
        "ffn1_norm": gain((L, D_MODEL)),
        "ffn1_w1": w((L, D_MODEL, D_FF), D_MODEL),
        "ffn1_w3": w((L, D_MODEL, D_FF), D_MODEL),
        "ffn1_w2": w((L, D_FF, D_MODEL), D_FF),
        "mix_norm": gain((L, D_MODEL)),
        "w_in": w((L, D_MODEL, D_IN), D_MODEL),
        "na_q_norm": gain((L, NA_HEAD_DIM)),
        "na_k_norm": gain((L, NA_HEAD_DIM)),
        "na_rpb": small((L, NA_HEADS, 2 * NA_WIN_R - 1, 2 * NA_WIN_C - 1), 0.1),
        "gla_gf_up": w((L, GLA_GATE_RANK, GLA_QK_W), GLA_GATE_RANK),
        "gla_gf_bias": small((L, GLA_QK_W), 0.1, 2.0),
        "gla_gb_up": w((L, GLA_GATE_RANK, GLA_QK_W), GLA_GATE_RANK),
        "gla_gb_bias": small((L, GLA_QK_W), 0.1, 2.0),
        "gla_out_norm": gain((L, GLA_DV)),
        "mla_cq_norm": gain((L, MLA_Q_RANK)),
        "mla_ckv_norm": gain((L, MLA_KV_RANK)),
        "mla_w_uq": w((L, MLA_Q_RANK, MLA_HEADS * MLA_QK_HEAD), MLA_Q_RANK),
        "mla_w_ukv": w((L, MLA_KV_RANK, MLA_HEADS * (MLA_NOPE + MLA_V)), MLA_KV_RANK),
        "mla_q_norm": gain((L, MLA_QK_HEAD)),
        "mla_k_norm": gain((L, MLA_QK_HEAD)),
        "w_br_na": w((L, NA_W, D_MODEL), NA_W),
        "w_br_gla": w((L, GLA_V_W, D_MODEL), GLA_V_W),
        "w_br_mla": w((L, MLA_V_W, D_MODEL), MLA_V_W),
        "w_out": w((L, D_MODEL, D_MODEL), D_MODEL),
        "ffn2_norm": gain((L, D_MODEL)),
        "ffn2_w1": w((L, D_MODEL, D_FF), D_MODEL),
        "ffn2_w3": w((L, D_MODEL, D_FF), D_MODEL),
        "ffn2_w2": w((L, D_FF, D_MODEL), D_FF),
    }

def second_block(x, ffn1_norm, ffn1_w1, ffn1_w3, ffn1_w2, mix_norm, w_in,
              na_q_norm, na_k_norm, na_rpb,
              gla_gf_up, gla_gf_bias, gla_gb_up, gla_gb_bias, gla_out_norm,
              mla_cq_norm, mla_ckv_norm, mla_w_uq, mla_w_ukv, mla_q_norm, mla_k_norm,
              w_br_na, w_br_gla, w_br_mla, w_out,
              ffn2_norm, ffn2_w1, ffn2_w3, ffn2_w2):
    B, S, D = x.shape
    cos, sin = rope_tables_2(S)
    for l in range(DEPTH):
        x = x + 0.5 * swiglu_2(rms_norm_2(x, ffn1_norm[l]), ffn1_w1[l], ffn1_w3[l], ffn1_w2[l])

        h = rms_norm_2(x, mix_norm[l])
        z = h @ w_in[l]
        (na_q, na_k, na_v, gq, gk, gv, gr, gfl, gbl, c_q, c_kv, k_rope, gates) = split_cols_2(z, IN_SPLITS)

        qa = rms_norm_2(na_q.reshape(B, S, NA_HEADS, NA_HEAD_DIM), na_q_norm[l])
        ka = rms_norm_2(na_k.reshape(B, S, NA_HEADS, NA_HEAD_DIM), na_k_norm[l])
        va = na_v.reshape(B, S, NA_HEADS, NA_HEAD_DIM)
        y_na = neighborhood_attention(qa, ka, va, na_rpb[l])

        g_f = jax.nn.log_sigmoid((gfl @ gla_gf_up[l] + gla_gf_bias[l]).astype(jnp.float32)) / GLA_GATE_TAU
        g_b = jax.nn.log_sigmoid((gbl @ gla_gb_up[l] + gla_gb_bias[l]).astype(jnp.float32)) / GLA_GATE_TAU
        o_gla = gla_bidirectional(gq.reshape(B, S, GLA_HEADS, GLA_DK), gk.reshape(B, S, GLA_HEADS, GLA_DK),
                                  gv.reshape(B, S, GLA_HEADS, GLA_DV),
                                  g_f.reshape(B, S, GLA_HEADS, GLA_DK), g_b.reshape(B, S, GLA_HEADS, GLA_DK))
        o_gla = rms_norm_2(o_gla, gla_out_norm[l]).astype(x.dtype).reshape(B, S, GLA_V_W)
        y_gla = o_gla * jax.nn.silu(gr)

        y_mla = mla_attention(c_q, c_kv, k_rope, mla_cq_norm[l], mla_ckv_norm[l], mla_w_uq[l], mla_w_ukv[l],
                              mla_q_norm[l], mla_k_norm[l], cos, sin)

        gt = jax.nn.sigmoid(gates.reshape(B, S, N_BRANCH, D))
        mixed = (gt[:, :, 0] * (y_na @ w_br_na[l])
                 + gt[:, :, 1] * (y_gla @ w_br_gla[l])
                 + gt[:, :, 2] * (y_mla @ w_br_mla[l]))
        x = x + mixed @ w_out[l]

        x = x + 0.5 * swiglu_2(rms_norm_2(x, ffn2_norm[l]), ffn2_w1[l], ffn2_w3[l], ffn2_w2[l])
    return x


def setup_inputs(seed=0):
    out = dict(first_inputs(seed))
    for name, value in second_inputs(seed + 1).items():
        if name != "x":
            out[name + "_2"] = value
    return out


def reference(
    x, positions, ffn_norm, ffn_w_gate, ffn_w_up, ffn_w_down, mix_norm, hy_w_in, hy_conv_w,
    hy_conv_b, hy_dt_bias, hy_a_log, hy_d_skip, hy_ssd_norm, hy_igate_bias, hy_fgate_bias,
    hy_mlstm_norm, hy_w_out, sa_w_in, sa_q_norm, sa_k_norm, sa_w_out, ffn1_norm_2, ffn1_w1_2,
    ffn1_w3_2, ffn1_w2_2, mix_norm_2, w_in_2, na_q_norm_2, na_k_norm_2, na_rpb_2, gla_gf_up_2,
    gla_gf_bias_2, gla_gb_up_2, gla_gb_bias_2, gla_out_norm_2, mla_cq_norm_2, mla_ckv_norm_2,
    mla_w_uq_2, mla_w_ukv_2, mla_q_norm_2, mla_k_norm_2, w_br_na_2, w_br_gla_2, w_br_mla_2,
    w_out_2, ffn2_norm_2, ffn2_w1_2, ffn2_w3_2, ffn2_w2_2,
):
    x = first_block(
        x, positions, ffn_norm, ffn_w_gate, ffn_w_up, ffn_w_down, mix_norm, hy_w_in, hy_conv_w,
        hy_conv_b, hy_dt_bias, hy_a_log, hy_d_skip, hy_ssd_norm, hy_igate_bias, hy_fgate_bias,
        hy_mlstm_norm, hy_w_out, sa_w_in, sa_q_norm, sa_k_norm, sa_w_out,
    )
    return second_block(
        x, ffn1_norm_2, ffn1_w1_2, ffn1_w3_2, ffn1_w2_2, mix_norm_2, w_in_2, na_q_norm_2,
        na_k_norm_2, na_rpb_2, gla_gf_up_2, gla_gf_bias_2, gla_gb_up_2, gla_gb_bias_2,
        gla_out_norm_2, mla_cq_norm_2, mla_ckv_norm_2, mla_w_uq_2, mla_w_ukv_2, mla_q_norm_2,
        mla_k_norm_2, w_br_na_2, w_br_gla_2, w_br_mla_2, w_out_2, ffn2_norm_2, ffn2_w1_2,
        ffn2_w3_2, ffn2_w2_2,
    )


_drawn_inputs = setup_inputs


def setup_inputs(seed=0):
    import zlib

    import numpy as np

    out = dict(_drawn_inputs(seed))
    spreads = {}
    factors = {'hy_conv_b': 2.89,
     'hy_d_skip': 3.611,
     'hy_igate_bias': 64.0,
     'hy_mlstm_norm': 3.438,
     'sa_q_norm': 8.0,
     'sa_k_norm': 8.0,
     'na_q_norm_2': 8.0,
     'na_k_norm_2': 8.0,
     'na_rpb_2': 5.971,
     'gla_gf_up_2': 2.669,
     'gla_gf_bias_2': 22.546,
     'gla_gb_bias_2': 43.04,
     'gla_out_norm_2': 3.886,
     'mla_cq_norm_2': 8.0,
     'mla_ckv_norm_2': 8.0,
     'mla_q_norm_2': 8.0,
     'mla_k_norm_2': 8.0,
     'ffn2_norm_2': 2.696,
     'gla_gb_up_2': 8.0}
    for name, (base, spread) in spreads.items():
        noise = np.random.default_rng([zlib.crc32(name.encode()), seed]).standard_normal(out[name].shape)
        drawn = base * np.exp(spread * noise) if base else spread * noise
        out[name] = __import__('jax').numpy.asarray(drawn.astype(out[name].dtype))
    for name, factor in factors.items():
        out[name] = (out[name] * factor).astype(out[name].dtype)
    return out
```

```python
from contextlib import ExitStack

import concourse.bass as bass
import numpy as np
from concourse import mybir

F32 = mybir.dt.float32
BF16 = mybir.dt.bfloat16
I32 = mybir.dt.int32
ALU = mybir.AluOpType
ACT = mybir.ActivationFunctionType
AX = mybir.AxisListType

P = 128
S = 256
TT = S // P
D = 1024
KD = D // P
FF = 2816
DEPTH = 2
EPS = 1e-6
NEG = -1e30
TAKEN_KEY = -3e38

RING = 6
SLOT = 2048
COLS = 256
CHUNKS = FF // COLS

SSD_W = 1024
SSD_H = 16
SSD_G = 2
SSD_N = 128
CONV_DIM = SSD_W + 2 * SSD_G * SSD_N
CONV_T = CONV_DIM // P
CONV_K = 4
ML_H = 4
ML_V = 256
ML_VA = ML_V + 1
HY_Z, HY_XBC, HY_DT = 0, SSD_W, SSD_W + CONV_DIM
HY_Q = HY_DT + SSD_H
HY_K = HY_Q + 512
HY_V = HY_K + 512
HY_O = HY_V + 1024
HY_IG = HY_O + 1024
HY_FG = HY_IG + ML_H

SA_H, SA_IH, SA_D = 16, 8, 64
SA_IN = SA_H * SA_D + 2 * SA_D + SA_IH * SA_D + SA_D + SA_IH
SA_K, SA_V, SA_QI = 1024, 1088, 1152
SA_KI, SA_WI = SA_QI + SA_IH * SA_D, SA_QI + SA_IH * SA_D + SA_D
TOPK = min(256, S // 4)

GRID_W, WIN_R, WIN_C = 64, 8, 16
ROWS = S // GRID_W
NA_H = 8
RPB_R, RPB_C = 2 * WIN_R - 1, 2 * WIN_C - 1
GLA_H, GLA_DK, GLA_DV, GLA_C = 4, 64, 128, 64
MLA_H, MLA_NOPE, MLA_R, MLA_DV = 4, 128, 64, 128
MLA_QK = MLA_NOPE + MLA_R
Z_NQ, Z_NK, Z_NV = 0, 512, 1024
Z_GQ, Z_GK, Z_GV, Z_GR, Z_GL = 1536, 1792, 2048, 2560, 3072
Z_CQ, Z_CKV, Z_KR, Z_GT = 3104, 3360, 3616, 3680
Z_IN = Z_GT + 3 * D

G_FFN, G_MIX, G_FFN1, G_MIX2, G_FFN2 = 0, 32, 48, 64, 80
G_CW, G_CB, G_SSD, G_ML, G_GLA, G_CQ, G_CKV = 96, 144, 156, 164, 172, 174, 178
N_GA, N_GB = 96, 86

R_DSKIP, R_SAQ, R_SAK, R_NAQ, R_NAK = 0, 16, 80, 144, 272
R_GB, R_MQ, R_MK = 400, 1424, 1808
N_ROW = 2192

C_ID, C_CAUS_T, C_CAUS, C_WIN = 0, 128, 256, 768
C_LE, C_GT, C_GE, C_LT = 832, 960, 1088, 1216
C_INV, C_COS, C_SIN, C_REV = 1344, 1376, 1440, 1504
N_CONST = 1632


def constants():
    c = np.zeros((P, N_CONST), np.float32)
    i, j = np.arange(P)[:, None], np.arange(P)[None, :]
    c[:, C_ID:C_ID + P] = i == j
    c[:, C_CAUS_T:C_CAUS_T + P] = np.where(i <= j, 0, NEG)
    key = np.arange(S)[None, :]
    for t in range(TT):
        c[:, C_CAUS + t * S:C_CAUS + (t + 1) * S] = np.where(key <= i + t * P, 0, NEG)
    c[:, C_REV:C_REV + P] = (i // GRID_W == j // GRID_W) & (i % GRID_W + j % GRID_W == GRID_W - 1)
    cq, ck = GRID_W - 1 - np.arange(P)[:, None] % GRID_W, np.arange(GRID_W)[None, :]
    c0 = np.clip(cq - WIN_C // 2, 0, GRID_W - WIN_C)
    c[:, C_WIN:C_WIN + GRID_W] = np.where((ck >= c0) & (ck < c0 + WIN_C), 0, NEG)
    same = i // GLA_C == j // GLA_C
    for at, m in ((C_LE, i <= j), (C_GT, i > j), (C_GE, i >= j), (C_LT, i < j)):
        c[:, at:at + P] = same & m
    half = MLA_R // 2
    inv = (np.float32(10000.0) ** (-np.arange(half, dtype=np.float32) / np.float32(half))).astype(np.float32)
    c[:, C_INV:C_INV + half] = inv
    ang = np.arange(S, dtype=np.float32)[:, None] * inv[None, :]
    for t in range(TT):
        c[:, C_COS + t * half:C_COS + (t + 1) * half] = np.cos(ang[t * P:(t + 1) * P])
        c[:, C_SIN + t * half:C_SIN + (t + 1) * half] = np.sin(ang[t * P:(t + 1) * P])
    return c


class Tally:

    def __init__(self):
        self.at = {}

    def __call__(self, sem, n=1):
        self.at[sem.name] = self.at.get(sem.name, 0) + n
        return self.at[sem.name]


class Banks:

    def __init__(self):
        self.next, self.uses, self.filled = 0, [0] * 4, [0] * 4

    def take(self, by_piece=False):
        b = self.next
        self.next = (b + 1) % 4
        self.uses[b] += 1
        self.filled[b] += not by_piece
        return b


class Thread:

    def __init__(self, e, step):
        self.e, self.step = e, step
        self.see, self.banks, self.piece = Tally(), Banks(), 0

    def link(self, ins):
        ins.then_inc(self.step, 1)
        self.e.wait_ge(self.step, self.see(self.step))

    def done(self, ins, sem):
        ins.then_inc(sem, 1)
        self.e.wait_ge(sem, self.see(sem))


def two_blocks(nc, A, out):
    with ExitStack() as ctx:
        def sb(name, shape, dt=F32, where=ctx):
            return where.enter_context(nc.sbuf_tensor(name, shape, dt))

        def sem(name):
            return ctx.enter_context(nc.semaphore(name))

        x = sb("x", [P, TT, D])
        hT = sb("hT", [P, KD, S])
        ring = sb("ring", [P, RING, SLOT])
        silu_gate = sb("silu_gate", [P, 2, 512])
        gatedT = sb("gatedT", [P, 2, 512])
        const = sb("const", [P, N_CONST])
        gain = sb("gain", [P, N_GA + N_GB])
        gain_rows = sb("gain_rows", [P, 2, P])
        rows = sb("rows", [P, N_ROW])
        heads_in = sb("heads_in", [SSD_H, 4])
        w_gates = sb("w_gates", [P, KD, 24])
        gate_up = sb("gate_up", [16, DEPTH, 2, 256])
        zeros = sb("zeros", [P, 512], BF16)
        ones = sb("ones", [SSD_H, P])
        pos_i = sb("pos_i", [P, TT], I32)
        pos_f = sb("pos_f", [P, TT])
        rope1 = sb("rope1", [P, 2, TT, 32])
        rope_t = sb("rope_t", [P, 3, TT * 32])
        squares = sb("squares", [P, 2048])
        stat = sb("stat", [P, 3, 32])
        normed = sb("normed", [P, TT, D])
        gdec = sb("gdec", [P, 2, 2, 4])
        heads4 = sb("heads4", [ML_H, 1])
        fg_bias = sb("fg_bias", [ML_H, 1])

        with ExitStack() as m:
            xbc = sb("xbc", [P, CONV_T, CONV_K - 1 + S], where=m)
            conv = sb("conv", [P, CONV_T, S], where=m)
            mq = sb("mq", [P, ML_H, S], where=m)
            mk = sb("mk", [P, ML_H, S], where=m)
            mv = sb("mv", [P, TT, ML_H, ML_VA], where=m)
            og = sb("og", [P, TT, 1024], where=m)
            hrow = sb("hrow", [SSD_H, 10, S], where=m)
            cols = sb("cols", [P, TT, 64], where=m)
            ecols = sb("ecols", [P, SSD_H], where=m)
            xs = sb("xs", [P, TT, SSD_W], where=m)
            xd = sb("xd", [P, TT, SSD_W], where=m)
            wT = sb("wT", [P, SSD_H, S], where=m)
            hden = sb("hden", [P, 2, TT * ML_H], where=m)
            zg = normed
            xde = squares[:, 0:1024]
            state = squares[:, 1024:2048].rearrange("p (g n) -> p g n", g=SSD_G)
            seg = silu_gate
            cb = gatedT[:, 0, :].rearrange("p (g c n) -> p g c n", g=SSD_G, c=TT)
            b_tok = gatedT[:, 1, 0:2 * P].rearrange("p (g n) -> p g n", g=SSD_G)
            flat = xbc[:, :, :].rearrange("p k s -> p (k s)")
            hm = flat[:, 0:TT * ML_H * ML_VA].rearrange("p (c h v) -> p c h v", c=TT, h=ML_H)
            cst = flat[:, TT * ML_H * ML_VA:3 * ML_H * ML_VA].rearrange("p (h v) -> p h v", h=ML_H)
            kw = conv[:, 0:2, :].rearrange("p k (h n) -> p (k h) n", n=P)
            qw = conv[:, 2:4, :].rearrange("p k (h n) -> p (k h) n", n=P)
            yT = wT
        with ExitStack() as m:
            soft_s = sb("soft_s", [P, 2, TT, S], where=m)
            soft_p = sb("soft_p", [P, 2, TT, S], where=m)
            soft_pT = sb("soft_pT", [P, 2, 512], where=m)
            soft_m = sb("soft_m", [P, 2, 2, TT], where=m)
            soft_r = sb("soft_r", [P, 2, TT], where=m)
            with ExitStack() as g:
                sa = sb("sa", [P, TT, SA_IN], where=g)
                sa_kd = sb("sa_kd", [P, TT, 2, P], where=g)
                sa_qT = sb("sa_qT", [P, 8, S], where=g)
                sa_kT = sb("sa_kT", [P, 1, S], where=g)
                sa_qiT = sb("sa_qiT", [P, 4, S], where=g)
                sa_kiT = sb("sa_kiT", [P, 1, S], where=g)
                sa_sc = sb("sa_sc", [P, TT, S], where=g)
                sa_tmp = sb("sa_tmp", [P, TT, S], where=g)
                sa_m8 = sb("sa_m8", [P, 8], where=g)
                sa_bias = sb("sa_bias", [P, TT, S], where=g)
                sa_oT = sb("sa_oT", [P, 8, S], where=g)
                sa_rt = sb("sa_rt", [P, 4, TT, SA_H * 32], where=g)
            z = sb("z", [P, TT, Z_IN], where=m)
            mix = sb("mix", [P, TT, D], where=m)
            mix_t = normed
            brT = silu_gate[:, :, :].rearrange("p a (k s) -> p (a k) s", s=S)
            with ExitStack() as g:
                na_bias = sb("na_bias", [P, NA_H, TT, S], where=g)
                na_qT = sb("na_qT", [P, 4, S], where=g)
                na_kT = gatedT[:, :, :].rearrange("p a (k s) -> p (a k) s", s=S)
            with ExitStack() as g:
                ep = sb("ep", [P, 2, 2, S], where=g)
                em = sb("em", [P, 2, 2, S], where=g)
                gqT = sb("gqT", [P, 2, S], where=g)
                gkT = sb("gkT", [P, 2, S], where=g)
                gst = sb("gst", [P, 2, 2, 3, P], where=g)
                go = sb("go", [P, TT, GLA_H, P], where=g)
                gg = z[:, :, 0:512].rearrange("p a (d n) -> p d a n", d=2)
                ge = z[:, :, 512:1024].rearrange("p a (d n) -> p d a n", d=2)
                ke = z[:, :, 1024:1536].rearrange("p a (d n) -> p d a n", d=2)
                am = squares[:, 0:512].rearrange("p (d a n) -> p d a n", d=2, a=TT)
                glT = squares[0:16, 512:1024].rearrange("p (d s) -> p d s", d=2)
                a_in = squares[:, 1024:2048].rearrange("p (h a n) -> p h a n", h=GLA_H, a=TT)
            with ExitStack() as g:
                cT = sb("cT", [P, 2, 2, S], where=g)
                lqT = sb("lqT", [P, MLA_H, S], where=g)
                lkT = sb("lkT", [P, MLA_H, S], where=g)
                lqrT = sb("lqrT", [64, MLA_H, S], where=g)
                lkrT = sb("lkrT", [64, MLA_H, S], where=g)
                lq = z[:, :, 0:768].rearrange("p a (h d) -> p a h d", h=MLA_H)
                lk = z[:, :, 768:1536].rearrange("p a (h d) -> p a h d", h=MLA_H)
                lkv = z[:, :, 1536:2560].rearrange("p a (h d) -> p a h d", h=MLA_H)
            z_rt = squares[:, :].rearrange("p (n a c) -> p n a c", n=4, a=TT)

        acc = ctx.enter_context(nc.psum_tensor("acc", [P, 4, 512], F32))
        bank = ctx.enter_context(nc.psum_tensor("bank", [P, 4, 512], F32))

        ring_in = [sem(f"ring_in{i}") for i in range(RING)]
        full = [sem(f"bank_full{i}") for i in range(4)]
        taken = [sem(f"bank_taken{i}") for i in range(4)]
        piece_done = sem("piece_done")
        small_in = sem("small_in")
        bias_in = sem("na_bias_in")
        bias_ready = sem("na_bias_ready")
        bias_room = sem("na_bias_room")
        out_done = sem("out_done")
        setup_v, setup_g, setup_a = sem("setup_vector"), sem("setup_gpsimd"), sem("setup_scalar")
        silu_ready, gated_ready = sem("silu_ready"), sem("gated_ready")
        acc_full, acc_taken = sem("acc_full"), sem("acc_taken")
        norm_src, squares_ready, var_ready, root_ready = (
            sem("norm_src"), sem("squares_ready"), sem("var_ready"), sem("root_ready"))
        flip_src = sem("flip_src")
        to_act, to_dve, dve_operand, act_operand = (
            sem("vector_to_scalar"), sem("scalar_to_vector"), sem("vector_operand"), sem("scalar_operand"))
        score_ready, prob_ready, softmax_ready = sem("score_ready"), sem("prob_ready"), sem("softmax_ready")
        x_final = sem("x_final")
        steps = {n: sem(f"{n}_step") for n in ("pe", "act", "dve", "pool", "sp")}

        ident = const[:, C_ID:C_ID + P]
        reverse = const[:, C_REV:C_REV + P]

        def selector(n, h):
            return const[0:n, C_ID + h:C_ID + h + 1].to_broadcast([n, P])

        def bank_of(b):
            return bank[:, b, :]

        def halves(b, w=COLS):
            return bank[:, b, :].rearrange("p (a c) -> p a c", a=2)[:, :, 0:w]

        def acc2():
            return acc[:, :, :].rearrange("p (a b) c -> p a (b c)", a=TT)

        def all_taken(t):
            for b in range(4):
                if t.banks.uses[b]:
                    t.e.wait_ge(taken[b], t.banks.uses[b])

        def claim(t, by_piece=False):
            b = t.banks.take(by_piece)
            if t.banks.uses[b] > 1:
                t.e.wait_ge(taken[b], t.banks.uses[b] - 1)
            return b

        def filled(t):
            b = t.banks.take()
            t.e.wait_ge(full[b], t.banks.filled[b])
            return b

        def load(t, dst, src):
            s = t.piece % RING
            t.e.wait_ge(piece_done, t.piece + 1)
            t.e.dma_start(dst(s), src).then_inc(ring_in[s], 16)
            t.piece += 1

        def slot_cols(s, w=COLS):
            return ring[:, s, :].rearrange("p (k c) -> p k c", k=KD)[:, :, 0:w]

        def slot_rows(s, n=D):
            return ring[:, s, 0:2 * n].rearrange("p (k c) -> p k c", k=2)

        def cols_of(w, c, n=COLS):
            return w.rearrange("(k p) c -> p k c", p=P)[:, :, bass.ds(c, n)]

        def rows_of(w, r, n=D):
            return w.rearrange("(k p) c -> p k c", p=P)[:, bass.ds(r, 2), 0:n]

        def load_cols(t, w, c, n=COLS):
            load(t, lambda s: slot_cols(s, n), cols_of(w, c, n))

        def load_rows(t, w, r, n=D):
            load(t, lambda s: slot_rows(s, n), rows_of(w, r, n))

        def arrived(t):
            s = t.piece % RING
            t.e.wait_ge(ring_in[s], 16 * (t.piece // RING + 1))
            t.piece += 1
            return s

        def ffn_sync(t, wg, wu, wd):
            load_cols(t, wg, 0)
            load_cols(t, wu, 0)
            n0 = t.piece
            with t.e.Fori(0, (CHUNKS - 1) // 2) as i:
                for j in range(2):
                    for n, (w, kind) in enumerate(((wg, 0), (wu, 0), (wd, 1))):
                        o = 3 * j + n
                        s = (n0 + o) % RING
                        t.e.wait_ge(piece_done, i * RING + (n0 + o + 1))
                        if kind:
                            t.e.dma_start(slot_rows(s), rows_of(w, i * 4 + 2 * j)).then_inc(ring_in[s], 16)
                        else:
                            t.e.dma_start(slot_cols(s), cols_of(w, i * 512 + COLS * (1 + j))).then_inc(ring_in[s], 16)
            t.piece += 3 * (CHUNKS - 1)
            load_rows(t, wd, 2 * (CHUNKS - 1))

        def ffn_up(pe, c, s, which):
            for f in range(2):
                for k in range(KD):
                    mm = pe.matmul(bank[:, 2 * (c % 2) + which, f * S:(f + 1) * S],
                                   slot_cols(s)[:, k, f * P:(f + 1) * P], hT[:, k, :],
                                   start=(k == 0), stop=(k == KD - 1))
            mm.then_inc(piece_done, 1)

        def ffn_down(pe, c, s, last=False):
            for f in range(2):
                for a in range(TT):
                    for n in range(2):
                        mm = pe.matmul(acc[:, 2 * a + n, :], gatedT[:, c % 2, f * S + a * P:f * S + (a + 1) * P],
                                       slot_rows(s)[:, f, n * 512:(n + 1) * 512], start=False,
                                       stop=(last and f == 1), skip_group_check=True)
            mm.then_inc(piece_done, 1)

        def ffn_tensor(t, k):
            pe = t.e
            all_taken(t)
            acc_is_free(t)
            for b in range(4):
                pe.matmul(acc[:, b, :], zeros[:, 0:P], zeros[:, :], start=True, stop=False, skip_group_check=True)
            for which in range(2):
                ffn_up(pe, 0, arrived(t), which)
            n0 = t.piece
            with pe.Fori(0, (CHUNKS - 1) // 2) as i:
                for j in range(2):
                    for which in range(2):
                        n = n0 + 3 * j + which
                        pe.wait_ge(ring_in[n % RING], i * 16 + 16 * (n // RING + 1))
                        ffn_up(pe, 1 + j, n % RING, which)
                    n = n0 + 3 * j + 2
                    pe.wait_ge(ring_in[n % RING], i * 16 + 16 * (n // RING + 1))
                    pe.wait_ge(gated_ready, i * 2 + (CHUNKS * k + 1 + j))
                    ffn_down(pe, j, n % RING)
            t.piece += 3 * (CHUNKS - 1)
            s = arrived(t)
            pe.wait_ge(gated_ready, CHUNKS * (k + 1))
            ffn_down(pe, CHUNKS - 1, s, last=True)

        def ffn_scalar(t, k):
            act = t.e
            n0 = t.piece

            def gate(c, done):
                act.wait_ge(piece_done, done)
                act.activation(silu_gate[:, c % 2, :], bank_of(2 * (c % 2)), ACT.Silu).then_inc(silu_ready, 1)

            gate(0, RING + n0 + 1)
            with act.Fori(0, (CHUNKS - 1) // 2) as i:
                for j in range(2):
                    gate(1 + j, i * RING + (RING + n0 + 3 + 3 * j))
            t.piece += 3 * CHUNKS

        def ffn_vector(t, k):
            dve = t.e
            n0 = t.piece

            def gate(c, done, silu):
                dve.wait_ge(piece_done, done)
                dve.wait_ge(silu_ready, silu)
                dve.tensor_tensor(gatedT[:, c % 2, :], bank_of(2 * (c % 2) + 1), silu_gate[:, c % 2, :],
                                  ALU.mult).then_inc(gated_ready, 1)

            gate(0, RING + n0 + 2, CHUNKS * k + 1)
            with dve.Fori(0, (CHUNKS - 1) // 2) as i:
                for j in range(2):
                    gate(1 + j, i * RING + (RING + n0 + 4 + 3 * j), i * 2 + (CHUNKS * k + 2 + j))
            t.piece += 3 * CHUNKS
            add_to_x(t, 0.5)

        def acc_is_free(t):
            if t.acc_uses:
                t.e.wait_ge(acc_taken, t.acc_uses)
            t.acc_uses += 1

        def add_to_x(t, scale):
            t.e.wait_ge(piece_done, RING + t.piece)
            t.done(t.e.scalar_tensor_tensor(x[:, :, :], acc2(), scale, x[:, :, :], ALU.mult, ALU.add), acc_taken)

        def rms_scalar(t, src, n, d):
            act = t.e
            act.wait_ge(norm_src, t.see(norm_src))
            sq = squares[:, 0:n * d]
            if len(src.shape) == 3:
                sq = sq.rearrange("p (n d) -> p n d", n=n)
            else:
                sq = sq.rearrange("p (a n d) -> p a n d", a=TT, d=d)
            act.activation(sq, src, ACT.Square).then_inc(squares_ready, 1)
            act.wait_ge(var_ready, t.see(var_ready))
            t.link(act.activation(stat[:, 1, 0:n], stat[:, 0, 0:n], ACT.Ln))
            act.activation(stat[:, 1, 0:n], stat[:, 1, 0:n], ACT.Exp, scale=-0.5).then_inc(root_ready, 1)

        def rms_vector(t, src, n, d, dst=None):
            dve = t.e
            dst = src if dst is None else dst
            v, y, w = stat[:, 0, 0:n], stat[:, 1, 0:n], stat[:, 2, 0:n]
            dve.sem_inc(norm_src, 1)
            dve.wait_ge(squares_ready, t.see(squares_ready))
            t.link(dve.tensor_reduce(v, squares[:, 0:n * d].rearrange("p (n d) -> p n d", n=n), AX.X, ALU.add))
            t.done(dve.tensor_scalar(v, v, 1.0 / d, EPS, ALU.mult, ALU.add), var_ready)
            dve.wait_ge(root_ready, t.see(root_ready))
            t.link(dve.tensor_tensor(w, y, y, ALU.mult))
            t.link(dve.tensor_tensor(w, w, v, ALU.mult))
            t.link(dve.tensor_scalar(w, w, -0.5, 1.5, ALU.mult, ALU.add))
            t.link(dve.tensor_tensor(y, y, w, ALU.mult))
            if len(src.shape) == 3:
                yb = y.unsqueeze(2).to_broadcast([P, n, d])
            else:
                yb = y.rearrange("p (a n) -> p a n", a=TT).unsqueeze(3).to_broadcast([P, TT, n // TT, d])
            t.link(dve.tensor_tensor(dst, src, yb, ALU.mult))

        def flip_tensor(t, src, n, rows_out=P, order=None):
            pe = t.e
            pe.wait_ge(flip_src, t.see(flip_src))
            for k0 in range(0, n, 2):
                b = claim(t)
                for k in range(k0, min(k0 + 2, n)):
                    for a in range(TT):
                        o = (k - k0) * S + a * P
                        mm = pe.transpose(bank[0:rows_out, b, o:o + P], src(k, a), ident if order is None else order)
                mm.then_inc(full[b], 1)

        def flip_out(t, dst, n, scale, rows_out, mine):
            for k0 in range(0, n, 2):
                if (k0 // 2) % 2 != mine:
                    t.banks.take()
                    continue
                b = filled(t)
                ks = range(k0, min(k0 + 2, n))
                if not callable(scale):
                    parts = [(dst[0:rows_out, k0:k0 + len(ks), :],
                              bank[0:rows_out, b, 0:len(ks) * S].rearrange("p (k s) -> p k s", s=S), scale)]
                else:
                    parts = [(dst[0:rows_out, k, :], bank[0:rows_out, b, (k - k0) * S:(k - k0 + 1) * S], scale(k))
                             for k in ks]
                for o, i, g in parts:
                    if mine == 0:
                        ins = t.e.activation(o, i, ACT.Copy, scale=1.0 if g is None else g)
                    else:
                        ins = t.e.tensor_scalar(o, i, 1.0 if g is None else g, None, ALU.mult)
                ins.then_inc(taken[b], 1)

        def flip_scalar(t, dst, n, scale=None, rows_out=P):
            flip_out(t, dst, n, scale, rows_out, 0)

        def flip_vector(t, dst, n, scale=None, rows_out=P):
            t.e.sem_inc(flip_src, 1)
            flip_out(t, dst, n, scale, rows_out, 1)

        def gain_col(at):
            return lambda k: gain[:, at + k:at + k + 1]

        def pre_tensor(t, at):
            flip_tensor(t, lambda k, a: normed[:, a, k * P:(k + 1) * P], KD)

        def pre_scalar(t, at):
            rms_scalar(t, x[:, :, :], TT, D)
            flip_scalar(t, hT, KD, gain_col(at))

        def pre_vector(t, at):
            rms_vector(t, x[:, :, :], TT, D, normed[:, :, :])
            flip_vector(t, hT, KD, gain_col(at))

        def project_tensor(t, widths, feature_major=False):
            pe = t.e
            all_taken(t)
            for w in widths:
                s = arrived(t)
                b = claim(t, by_piece=True)
                for a in range(2):
                    for k in range(KD):
                        if feature_major:
                            mm = pe.matmul(bank[:, b, a * S:(a + 1) * S], slot_cols(s)[:, k, a * P:(a + 1) * P],
                                           hT[:, k, :], start=(k == 0), stop=(k == KD - 1))
                        else:
                            mm = pe.matmul(bank[:, b, a * COLS:a * COLS + w], hT[:, k, a * P:(a + 1) * P],
                                           slot_cols(s)[:, k, 0:w], start=(k == 0), stop=(k == KD - 1))
                mm.then_inc(piece_done, 1)

        def project_scalar(t, dsts, scale=1.0):
            for dst in dsts:
                b = t.banks.take(by_piece=True)
                t.piece += 1
                t.e.wait_ge(piece_done, RING + t.piece)
                src = halves(b, dst.shape[-1])
                t.e.activation(dst, src, ACT.Copy, scale=scale).then_inc(taken[b], 1)

        def project_vector(t, n):
            for _ in range(n):
                t.banks.take(by_piece=True)
                t.piece += 1

        def down_tensor(t, actT, n):
            pe = t.e
            acc_is_free(t)
            for k in range(n):
                if k % 2 == 0:
                    s = arrived(t)
                for a in range(TT):
                    for h in range(2):
                        mm = pe.matmul(acc[:, 2 * a + h, :], actT[:, k, a * P:(a + 1) * P],
                                       slot_rows(s)[:, k % 2, h * 512:(h + 1) * 512], start=(k == 0), stop=(k == n - 1))
                if k % 2 == 1:
                    mm.then_inc(piece_done, 1)

        def rotate(t, lo, hi, cos, sin, heads, tmp):
            dve = t.e
            c = cos.unsqueeze(2).to_broadcast([P, TT, heads, 32])
            s = sin.unsqueeze(2).to_broadcast([P, TT, heads, 32])
            v = [tmp[:, n, :, 0:heads * 32].rearrange("p a (h c) -> p a h c", c=32) for n in range(4)]
            dve.tensor_tensor(v[0], lo, c, ALU.mult)
            dve.tensor_tensor(v[1], hi, s, ALU.mult)
            dve.tensor_tensor(v[2], lo, s, ALU.mult)
            t.link(dve.tensor_tensor(v[3], hi, c, ALU.mult))
            dve.tensor_tensor(lo, v[0], v[1], ALU.subtract)
            t.link(dve.tensor_tensor(hi, v[2], v[3], ALU.add))

        def attend_tensor(t, heads, parts, value, dv, base, order=None):
            pe = t.e
            all_taken(t)
            for i in range(heads + 2):
                if i < heads:
                    b = claim(t)
                    for a in range(TT):
                        ps = parts(i, a)
                        for n, (q, k) in enumerate(ps):
                            mm = pe.matmul(bank[:, b, a * S:(a + 1) * S], q, k, start=(n == 0), stop=(n == len(ps) - 1))
                    mm.then_inc(full[b], 1)
                if 1 <= i <= heads:
                    pe.wait_ge(softmax_ready, t.see(softmax_ready))
                    b = claim(t)
                    for st in range(TT):
                        for a in range(TT):
                            o = st * S + a * P
                            mm = pe.transpose(bank[:, b, o:o + P], soft_p[:, (i - 1) % 2, a, st * P:(st + 1) * P],
                                              ident if order is None else order)
                    mm.then_inc(full[b], 1)
                if i >= 2:
                    h = i - 2
                    pe.wait_ge(act_operand, t.see(act_operand))
                    b = claim(t)
                    r = base(h)
                    for st in range(TT):
                        mm = pe.matmul(bank[r:r + dv, b, 0:S], value(h, st), soft_pT[:, h % 2, st * S:(st + 1) * S],
                                       start=(st == 0), stop=(st == TT - 1))
                    mm.then_inc(full[b], 1)

        def attend_scalar(t, heads, dst):
            act = t.e
            for i in range(heads + 2):
                if i < heads:
                    t.banks.take()
                    act.wait_ge(score_ready, t.see(score_ready))
                    for a in range(TT):
                        ins = act.activation(soft_p[:, i % 2, a, :], soft_s[:, i % 2, a, :], ACT.Exp,
                                             bias=soft_m[:, i % 2, 0, a:a + 1], accum_out=soft_m[:, i % 2, 1, a:a + 1])
                    ins.then_inc(prob_ready, 1)
                if 1 <= i <= heads:
                    b = filled(t)
                    act.activation(soft_pT[:, (i - 1) % 2, :], bank_of(b), ACT.Copy).then_inc(taken[b], 1)
                    act.wait_ge(taken[b], t.banks.uses[b])
                    act.sem_inc(act_operand, 1)
                if i >= 2:
                    b = filled(t)
                    o, r, dv = dst(i - 2)
                    act.activation(o, bank[r:r + dv, b, 0:S], ACT.Copy).then_inc(taken[b], 1)

        def attend_vector(t, heads, scale, bias):
            dve = t.e
            for i in range(heads + 2):
                if i < heads:
                    b = filled(t)
                    s = soft_s[:, i % 2, :, :]
                    if bias is None:
                        ins = dve.tensor_scalar(s, halves(b), scale, None, ALU.mult)
                    else:
                        ins = dve.scalar_tensor_tensor(s, halves(b), scale, bias(i), ALU.mult, ALU.add)
                    ins.then_inc(taken[b], 1)
                    dve.wait_ge(taken[b], t.banks.uses[b])
                    dve.tensor_reduce(soft_m[:, i % 2, 0, :], s, AX.X, ALU.max, negate=True).then_inc(score_ready, 1)
                if 1 <= i <= heads:
                    t.banks.take()
                    h = i - 1
                    dve.wait_ge(prob_ready, t.see(prob_ready))
                    t.link(dve.reciprocal(soft_r[:, h % 2, :], soft_m[:, h % 2, 1, :]))
                    for a in range(TT):
                        ins = dve.tensor_scalar(soft_p[:, h % 2, a, :], soft_p[:, h % 2, a, :],
                                                soft_r[:, h % 2, a:a + 1], None, ALU.mult)
                    ins.then_inc(softmax_ready, 1)
                if i >= 2:
                    t.banks.take()

        R_DT, R_FG, R_IG, R_T, R_L, R_A, R_ACS, R_DEND, R_B, R_M = range(10)
        HY_FEATURE = ((HY_XBC, 6), (HY_Q, 2), (HY_K, 2))
        HY_TOKEN = ((HY_Z, 4), (HY_V, 4), (HY_O, 4))

        def hybrid_sync(t):
            w = A["hy_w_in"][0]
            for at, n in HY_FEATURE + HY_TOKEN:
                for i in range(n):
                    load_cols(t, w, at + i * COLS)
            for r in range(0, 16, 2):
                load_rows(t, A["hy_w_out"][0], r)

        def hybrid_tensor(t):
            pe = t.e
            all_taken(t)
            b = claim(t)
            for col, n, o in ((0, SSD_H, 0), (16, ML_H, S)):
                for k in range(KD):
                    mm = pe.matmul(bank[0:n, b, o:o + S], w_gates[:, k, col:col + n], hT[:, k, :],
                                   start=(k == 0), stop=(k == KD - 1))
            mm.then_inc(full[b], 1)
            b = claim(t)
            for k in range(KD):
                mm = pe.matmul(bank[0:ML_H, b, 0:S], w_gates[:, k, 20:24], hT[:, k, :],
                               start=(k == 0), stop=(k == KD - 1))
            mm.then_inc(full[b], 1)
            project_tensor(t, [COLS] * 10, feature_major=True)
            project_tensor(t, [COLS] * 12)
            pe.wait_ge(dve_operand, t.see(dve_operand))
            b = claim(t)
            for c in range(TT):
                for row, n, o in ((R_DT, 16, 0), (R_ACS, 16, 16), (R_DEND, 16, 32), (R_B, 4, 48), (R_T, 4, 52),
                                  (R_A, 4, 56)):
                    mm = pe.transpose(bank[:, b, c * 64 + o:c * 64 + o + n], hrow[0:n, row, c * P:(c + 1) * P],
                                      const[0:n, C_ID:C_ID + n])
            mm.then_inc(full[b], 1)
            pe.wait_ge(act_operand, t.see(act_operand))
            b = claim(t)
            for g in range(SSD_G):
                for c in range(TT):
                    o = (g * TT + c) * P
                    mm = pe.matmul(bank[:, b, o:o + P], conv[:, 8 + g, c * P:(c + 1) * P],
                                   conv[:, 10 + g, c * P:(c + 1) * P], start=True, stop=True)
            mm.then_inc(full[b], 1)
            for c in range(TT):
                for h in range(2):
                    b = claim(t)
                    for k in range(4):
                        mm = pe.transpose(bank[:, b, k * P:(k + 1) * P], conv[:, 4 * h + k, c * P:(c + 1) * P], ident)
                    mm.then_inc(full[b], 1)
            b = claim(t)
            for g in range(SSD_G):
                mm = pe.transpose(bank[:, b, g * P:(g + 1) * P], conv[:, 8 + g, 0:P], ident)
            mm.then_inc(full[b], 1)
            for h in range(0, SSD_H, 2):
                b = claim(t)
                for j in range(2):
                    mm = pe.matmul(bank[:, b, j * S:(j + 1) * S], selector(SSD_H, h + j),
                                   hrow[:, R_ACS, :], start=True, stop=True)
                mm.then_inc(full[b], 1)
            pe.wait_ge(dve_operand, t.see(dve_operand))
            all_taken(t)
            for g in range(SSD_G):
                b = claim(t)
                pe.matmul(bank_of(b), b_tok[:, g, :], xde[:, g * 512:(g + 1) * 512], start=True, stop=True)\
                    .then_inc(full[b], 1)
            pe.wait_ge(dve_operand, t.see(dve_operand))
            acc_is_free(t)
            for c in range(TT):
                for h in range(SSD_H):
                    mm = pe.matmul(acc[:, 2 * c + h // 8, (h % 8) * 64:(h % 8 + 1) * 64], wT[:, h, c * P:(c + 1) * P],
                                   xd[:, c, h * 64:(h + 1) * 64], start=True, stop=True)
            mm.then_inc(acc_full, 1)
            all_taken(t)
            for g in range(SSD_G):
                b = claim(t)
                pe.matmul(bank_of(b), conv[:, 10 + g, P:S], state[:, g, :], start=True, stop=True).then_inc(full[b], 1)

            b = claim(t)
            for h in range(ML_H):
                mm = pe.transpose(bank[:, b, h * P:(h + 1) * P], mk[:, h, 0:P], ident)
            mm.then_inc(full[b], 1)
            all_taken(t)
            for h in range(ML_H):
                b = claim(t)
                pe.matmul(bank[:, b, 0:ML_VA], kw[:, h, :], mv[:, 0, h, :], start=True, stop=True).then_inc(full[b], 1)
            for h in range(0, ML_H, 2):
                b = claim(t)
                for j in range(2):
                    mm = pe.matmul(bank[:, b, j * S:(j + 1) * S], selector(ML_H, h + j),
                                   hrow[0:ML_H, R_M, :], start=True, stop=True)
                mm.then_inc(full[b], 1)
                b = claim(t)
                for j in range(2):
                    for c in range(TT):
                        mm = pe.matmul(bank[:, b, j * S + c * P:j * S + (c + 1) * P], mk[:, h + j, c * P:(c + 1) * P],
                                       mq[:, h + j, c * P:(c + 1) * P], start=True, stop=True)
                mm.then_inc(full[b], 1)
            b = claim(t)
            for h in range(ML_H):
                mm = pe.matmul(bank[:, b, h * P:(h + 1) * P], selector(ML_H, h),
                               hrow[0:ML_H, R_L, P:S], start=True, stop=True)
            mm.then_inc(full[b], 1)
            all_taken(t)
            for c in range(TT):
                for h in range(ML_H):
                    b = claim(t)
                    mm = pe.matmul(bank[:, b, 0:ML_VA], wT[:, h, c * P:(c + 1) * P], mv[:, c, h, :],
                                   start=True, stop=(c == 0))
                    if c:
                        mm = pe.matmul(bank[:, b, 0:ML_VA], qw[:, h, :], cst[:, h, :], start=False, stop=True)
                    mm.then_inc(full[b], 1)
            flip_tensor(t, lambda k, a: xs[:, a, k * P:(k + 1) * P], 8)
            flip_tensor(t, lambda k, a: xd[:, a, k * P:(k + 1) * P], 8)
            all_taken(t)
            down_tensor(t, yT, 16)

        def hybrid_scalar(t):
            act = t.e
            t.banks.take(), t.banks.take()
            act.activation(heads_in[:, 3:4], heads_in[:, 1:2], ACT.Exp).then_inc(to_dve, 1)
            act.wait_ge(to_act, t.see(to_act))
            project_scalar(t, [xbc[:, 2 * i:2 * i + 2, CONV_K - 1:] for i in range(6)])
            project_scalar(t, [mq[:, 2 * i:2 * i + 2, :] for i in range(2)], scale=float(P) ** -0.5)
            project_scalar(t, [mk[:, 2 * i:2 * i + 2, :] for i in range(2)])
            t.link(act.activation(hrow[:, R_T:R_T + 2, :], hrow[:, R_T:R_T + 2, :], ACT.Exp))
            act.activation(hrow[:, R_T:R_T + 2, :], hrow[:, R_T:R_T + 2, :], ACT.Ln, bias=1.0).then_inc(to_dve, 1)
            project_scalar(t, [zg[:, :, i * COLS:(i + 1) * COLS] for i in range(4)])
            project_scalar(t, [mv[:, :, i, 0:ML_V] for i in range(4)])
            project_scalar(t, [og[:, :, i * COLS:(i + 1) * COLS] for i in range(4)])
            act.wait_ge(to_act, t.see(to_act))
            act.activation(hrow[:, R_DEND, :], hrow[:, R_DEND, :], ACT.Exp)
            act.activation(hrow[0:ML_H, R_T, :], hrow[0:ML_H, R_T, :], ACT.Exp)
            act.activation(hrow[0:ML_H, R_A, :], hrow[0:ML_H, R_A, :], ACT.Exp)
            act.activation(hrow[0:ML_H, R_L, :], hrow[0:ML_H, R_L, :], ACT.Exp).then_inc(to_dve, 1)
            act.wait_ge(to_act, t.see(to_act))
            t.link(act.activation(conv[:, :, :], conv[:, :, :], ACT.Silu))
            act.sem_inc(act_operand, 1)
            act.activation(zg[:, :, :], zg[:, :, :], ACT.Silu)
            act.activation(og[:, :, :], og[:, :, :], ACT.Sigmoid).then_inc(to_dve, 1)
            b = filled(t)
            act.activation(cols[:, :, :], bank[:, b, 0:TT * 64].rearrange("p (c n) -> p c n", c=TT), ACT.Copy)\
                .then_inc(taken[b], 1)
            act.wait_ge(taken[b], t.banks.uses[b])
            act.activation(ecols[:, :], cols[:, 1, 16:32], ACT.Exp).then_inc(to_dve, 1)
            b = filled(t)
            act.activation(cb[:, :, :, :], bank_of(b).rearrange("p (g c n) -> p g c n", g=2, c=2), ACT.Copy)\
                .then_inc(taken[b], 1)
            for c in range(TT):
                for h in range(2):
                    b = filled(t)
                    act.activation(xs[:, c, h * 512:(h + 1) * 512], bank_of(b), ACT.Copy).then_inc(taken[b], 1)
            b = filled(t)
            act.activation(b_tok[:, :, :], bank[:, b, 0:S].rearrange("p (g n) -> p g n", g=2),
                           ACT.Copy).then_inc(taken[b], 1)
            for h in range(0, SSD_H, 2):
                t.banks.take()
                act.wait_ge(to_act, t.see(to_act))
                act.activation(seg[:, (h // 2) % 2, :], seg[:, (h // 2) % 2, :], ACT.Exp).then_inc(to_dve, 1)
            for g in range(SSD_G):
                b = filled(t)
                act.activation(state[:, g, :], bank_of(b), ACT.Copy).then_inc(taken[b], 1)
            t.banks.take(), t.banks.take()
            rms_scalar(t, xs[:, :, :].rearrange("p a (g d) -> p (a g) d", g=2), 4, 512)
            t.banks.take()
            for h in range(ML_H):
                b = filled(t)
                act.activation(cst[:, h, :], bank[:, b, 0:ML_VA], ACT.Copy).then_inc(taken[b], 1)
            for h in range(0, ML_H, 2):
                t.banks.take(), t.banks.take()
                act.wait_ge(to_act, t.see(to_act))
                act.activation(seg[:, (h // 2) % 2, :], seg[:, (h // 2) % 2, :], ACT.Exp).then_inc(to_dve, 1)
            t.banks.take()
            for c in range(TT):
                for h in range(ML_H):
                    b = filled(t)
                    act.activation(hm[:, c, h, :], bank[:, b, 0:ML_VA], ACT.Copy).then_inc(taken[b], 1)
            rms_scalar(t, xd[:, :, :].rearrange("p a (g d) -> p (a g) d", g=ML_H), 8, 256)
            flip_scalar(t, yT, 8, gain_col(G_SSD))
            flip_scalar(t, yT[:, 8:16, :], 8, gain_col(G_ML))
            t.piece += 8

        def hybrid_vector(t):
            dve = t.e
            r = lambda n, k=SSD_H: hrow[0:k, n, :]
            t.link(dve.memset(hrow[:, :, :], 0.0))
            dve.memset(mv[:, :, :, ML_V:ML_VA], 1.0)
            t.link(dve.memset(xbc[:, :, 0:CONV_K - 1], 0.0))
            b = filled(t)
            dve.tensor_scalar(r(R_DT), bank[0:SSD_H, b, 0:S], heads_in[:, 0:1], None, ALU.add)
            dve.tensor_scalar(r(R_IG, ML_H), bank[0:ML_H, b, S:2 * S], heads_in[0:ML_H, 2:3], None, ALU.add)\
                .then_inc(taken[b], 1)
            dve.wait_ge(taken[b], t.banks.uses[b])
            b = filled(t)
            dve.tensor_scalar(r(R_FG, ML_H), bank[0:ML_H, b, 0:S], fg_bias[:, 0:1], None, ALU.add).then_inc(taken[b], 1)
            dve.wait_ge(taken[b], t.banks.uses[b])
            both, e = hrow[:, R_DT:R_DT + 2, :], hrow[:, R_T:R_T + 2, :]
            dve.wait_ge(to_dve, t.see(to_dve))
            dve.scalar_tensor_tensor(e, both, -1.0, both, ALU.mult, ALU.min).then_inc(to_act, 1)
            project_vector(t, 6)
            for k in range(CONV_T):
                if k == 0:
                    all_taken(t)
                o = conv[:, k, :]
                tap = lambda n: gain[:, G_CW + n * CONV_T + k:G_CW + n * CONV_T + k + 1]
                t.link(dve.tensor_scalar(o, xbc[:, k, 0:S], tap(0), gain[:, G_CB + k:G_CB + k + 1], ALU.mult, ALU.add))
                for n in range(1, CONV_K):
                    t.link(dve.scalar_tensor_tensor(o, xbc[:, k, n:n + S], tap(n), o, ALU.mult, ALU.add))
            project_vector(t, 16)
            dve.wait_ge(to_dve, t.see(to_dve))
            t.link(dve.scalar_tensor_tensor(r(R_DT), r(R_DT), 0.0, r(R_T), ALU.max, ALU.add))
            t.link(dve.scalar_tensor_tensor(r(R_FG), r(R_FG), 0.0, r(R_L), ALU.min, ALU.subtract))
            t.link(dve.tensor_scalar(r(R_A), r(R_DT), heads_in[:, 3:4], -1.0, ALU.mult, ALU.mult))
            for c in range(TT):
                cc = slice(c * P, (c + 1) * P)
                t.link(dve.tensor_tensor_scan(hrow[:, R_ACS, cc], ones[:, :], hrow[:, R_A, cc], 0.0, ALU.mult, ALU.add))
                t.link(dve.tensor_scalar(hrow[:, R_DEND, cc], hrow[:, R_ACS, cc], hrow[:, R_ACS, c * P + P - 1:c * P + P],
                                         -1.0, ALU.subtract, ALU.mult))
            q = ML_H
            for c in range(TT):
                cc = slice(c * P, (c + 1) * P)
                last = c * P + P - 1
                m_in = 0.0 if c == 0 else heads4[:, 0:1]
                t.link(dve.tensor_tensor_scan(hrow[0:q, R_L, cc], ones[0:q, :], hrow[0:q, R_FG, cc], 0.0,
                                              ALU.mult, ALU.add))
                t.link(dve.tensor_tensor(hrow[0:q, R_B, cc], hrow[0:q, R_IG, cc], hrow[0:q, R_L, cc], ALU.subtract))
                t.link(dve.tensor_tensor_scan(hrow[0:q, R_M, cc], hrow[0:q, R_B, cc], hrow[0:q, R_B, cc], m_in,
                                              ALU.max, ALU.max))
                t.link(dve.scalar_tensor_tensor(hrow[0:q, R_T, cc], hrow[0:q, R_L, cc], -1.0, hrow[0:q, R_M, cc],
                                                ALU.mult, ALU.subtract))
                t.link(dve.tensor_scalar(hrow[0:q, R_A, cc], hrow[0:q, R_B, cc], hrow[0:q, R_M, last:last + 1], None,
                                         ALU.subtract))
                if c == 0:
                    t.link(dve.tensor_tensor(heads4[:, 0:1], hrow[0:q, R_L, last:last + 1],
                                             hrow[0:q, R_M, last:last + 1], ALU.add))
                t.link(dve.tensor_scalar(hrow[0:q, R_M, cc], hrow[0:q, R_M, cc], -1.0, None, ALU.mult))
                if c == 0:
                    t.link(dve.memset(hrow[0:q, R_L, cc], 0.0))
                else:
                    t.link(dve.tensor_scalar(hrow[0:q, R_L, cc], hrow[0:q, R_M, cc], m_in, None, ALU.add))
            dve.sem_inc(to_act, 1)
            dve.wait_ge(to_dve, t.see(to_dve))
            dve.sem_inc(dve_operand, 1)
            all_taken(t)
            dve.sem_inc(to_act, 1)
            b_cols = t.banks.take()
            dve.wait_ge(to_dve, t.see(to_dve, 2))
            t.banks.take()
            for _ in range(5):
                t.banks.take()
            all_taken(t)
            v4 = lambda ap: ap.rearrange("p c (h d) -> p c h d", h=SSD_H)
            t.link(dve.tensor_tensor(v4(xd[:, :, :]), v4(xs[:, :, :]),
                                     cols[:, :, 0:16].unsqueeze(3).to_broadcast([P, TT, SSD_H, 64]), ALU.mult))
            caus = const[:, C_CAUS_T:C_CAUS_T + P]

            def weigh(h):
                dve.wait_ge(to_dve, t.see(to_dve))
                g = h // 8
                t.link(dve.tensor_tensor(wT[:, h:h + 2, :].rearrange("p j (c n) -> p j c n", c=TT),
                                         seg[:, (h // 2) % 2, :].rearrange("p (j c n) -> p j c n", j=2, c=TT),
                                         cb[:, g, :, :].unsqueeze(1).to_broadcast([P, 2, TT, P]), ALU.mult))

            for h in range(0, SSD_H, 2):
                b = filled(t)
                s4 = seg[:, (h // 2) % 2, :].rearrange("p (j c n) -> p j c n", j=2, c=TT)
                a4 = cols[:, :, 16 + h:18 + h].rearrange("p c j -> p j c").unsqueeze(3).to_broadcast([P, 2, TT, P])
                dve.tensor_tensor(s4, bank_of(b).rearrange("p (j c n) -> p j c n", j=2, c=TT), a4, ALU.subtract)\
                    .then_inc(taken[b], 1)
                dve.wait_ge(taken[b], t.banks.uses[b])
                s3 = seg[:, (h // 2) % 2, :].rearrange("p (k n) -> p k n", n=P)
                dve.tensor_tensor(s3, s3, caus.unsqueeze(1).to_broadcast([P, 4, P]), ALU.add).then_inc(to_act, 1)
                if h == 0:
                    t.link(dve.tensor_tensor(xde[:, :].rearrange("p (h d) -> p h d", h=SSD_H),
                                             xd[:, 0, :].rearrange("p (h d) -> p h d", h=SSD_H),
                                             cols[:, 0, 32:48].unsqueeze(2).to_broadcast([P, SSD_H, 64]), ALU.mult))
                    dve.sem_inc(dve_operand, 1)
                else:
                    weigh(h - 2)
            weigh(SSD_H - 2)
            dve.sem_inc(dve_operand, 1)
            t.link(dve.tensor_tensor(v4(xs[:, :, :]), v4(xs[:, :, :]),
                                     rows[:, R_DSKIP:R_DSKIP + 16].unsqueeze(1).unsqueeze(3)
                                     .to_broadcast([P, TT, SSD_H, 64]), ALU.mult))
            dve.wait_ge(acc_full, t.see(acc_full))
            t.done(dve.tensor_tensor(xs[:, :, :], xs[:, :, :], acc2(), ALU.add), acc_taken)
            t.banks.take(), t.banks.take()
            for g in range(SSD_G):
                b = filled(t)
                dve.tensor_tensor(seg[:, g, :].rearrange("p (h d) -> p h d", h=8),
                                  bank_of(b).rearrange("p (h d) -> p h d", h=8),
                                  ecols[:, 8 * g:8 * g + 8].unsqueeze(2).to_broadcast([P, 8, 64]), ALU.mult)\
                    .then_inc(taken[b], 1)
                dve.wait_ge(taken[b], t.banks.uses[b])
                t.link(dve.tensor_tensor(xs[:, 1, g * 512:(g + 1) * 512], xs[:, 1, g * 512:(g + 1) * 512],
                                         seg[:, g, :], ALU.add))
            t.link(dve.tensor_tensor(xs[:, :, :], xs[:, :, :], zg[:, :, :], ALU.mult))
            rms_vector(t, xs[:, :, :].rearrange("p a (g d) -> p (a g) d", g=2), 4, 512)
            b = filled(t)
            dve.tensor_tensor(kw[:, :, :], bank_of(b).rearrange("p (h n) -> p h n", h=ML_H),
                              cols[:, 0, 56:60].unsqueeze(2).to_broadcast([P, ML_H, P]), ALU.mult).then_inc(taken[b], 1)
            for h in range(ML_H):
                t.banks.take()
            for h in range(0, ML_H, 2):
                b = filled(t)
                s4 = seg[:, (h // 2) % 2, :].rearrange("p (j c n) -> p j c n", j=2, c=TT)
                a4 = cols[:, :, 48 + h:50 + h].rearrange("p c j -> p j c").unsqueeze(3).to_broadcast([P, 2, TT, P])
                dve.tensor_tensor(s4, bank_of(b).rearrange("p (j c n) -> p j c n", j=2, c=TT), a4, ALU.add)\
                    .then_inc(taken[b], 1)
                dve.wait_ge(taken[b], t.banks.uses[b])
                s3 = seg[:, (h // 2) % 2, :].rearrange("p (k n) -> p k n", n=P)
                dve.tensor_tensor(s3, s3, caus.unsqueeze(1).to_broadcast([P, 4, P]), ALU.add).then_inc(to_act, 1)
                b = filled(t)
                dve.wait_ge(to_dve, t.see(to_dve))
                dve.tensor_tensor(wT[:, h:h + 2, :].rearrange("p j n -> p (j n)"), bank_of(b),
                                  seg[:, (h // 2) % 2, :], ALU.mult).then_inc(taken[b], 1)
            b = filled(t)
            dve.tensor_tensor(qw[:, :, :], bank_of(b).rearrange("p (h n) -> p h n", h=ML_H), mq[:, :, P:S], ALU.mult)\
                .then_inc(taken[b], 1)
            for _ in range(8):
                t.banks.take()
            all_taken(t)
            den = hm[:, :, :, ML_V:ML_VA].rearrange("p c h o -> p c (h o)")
            d0 = hden[:, 0, :].rearrange("p (c h) -> p c h", c=TT)
            t.link(dve.scalar_tensor_tensor(d0, den, -1.0, den, ALU.mult, ALU.max))
            t.link(dve.tensor_tensor(d0, d0, cols[:, :, 52:56], ALU.max))
            t.link(dve.reciprocal(hden[:, 1, :], hden[:, 0, :]))
            h4 = xd[:, :, :].rearrange("p c (h d) -> p c h d", h=ML_H)
            t.link(dve.tensor_tensor(h4, hm[:, :, :, 0:ML_V], hden[:, 1, :].rearrange("p (c h) -> p c h", c=TT)
                                     .unsqueeze(3).to_broadcast([P, TT, ML_H, ML_V]), ALU.mult))
            rms_vector(t, xd[:, :, :].rearrange("p a (g d) -> p (a g) d", g=ML_H), 8, 256)
            t.link(dve.tensor_tensor(xd[:, :, :], xd[:, :, :], og[:, :, :], ALU.mult))
            flip_vector(t, yT, 8, gain_col(G_SSD))
            flip_vector(t, yT[:, 8:16, :], 8, gain_col(G_ML))
            t.piece += 8
            add_to_x(t, 1.0)

        SA_W = [COLS] * 6 + [SA_IN - 6 * COLS]

        def sparse_sync(t):
            for i, w in enumerate(SA_W):
                load_cols(t, A["sa_w_in"][0], i * COLS, w)
            for r in range(0, 8, 2):
                load_rows(t, A["sa_w_out"][0], r)

        def sparse_tensor(t):
            pe = t.e
            project_tensor(t, SA_W)
            flip_tensor(t, lambda k, a: sa[:, a, SA_QI + k * P:SA_QI + (k + 1) * P], 4)
            flip_tensor(t, lambda k, a: sa_kd[:, a, 1, :], 1)
            all_taken(t)
            for h in range(SA_IH):
                b = claim(t)
                r = 64 * (h % 2)
                for a in range(TT):
                    mm = pe.matmul(bank[:, b, a * S:(a + 1) * S], sa_qiT[r:r + 64, h // 2, a * P:(a + 1) * P],
                                   sa_kiT[r:r + 64, 0, :], start=True, stop=True)
                mm.then_inc(full[b], 1)
            flip_tensor(t, lambda k, a: sa[:, a, k * P:(k + 1) * P], 8)
            flip_tensor(t, lambda k, a: sa_kd[:, a, 0, :], 1)
            lo = lambda h: 64 * (h % 2)
            attend_tensor(t, SA_H, lambda h, a: [(sa_qT[lo(h):lo(h) + 64, h // 2, a * P:(a + 1) * P],
                                                  sa_kT[lo(h):lo(h) + 64, 0, :])],
                          lambda h, st: sa[:, st, SA_V:SA_V + SA_D], 64, lo)
            all_taken(t)
            down_tensor(t, sa_oT, 8)

        def head_views(ap, at, heads, d=64):
            v = ap[:, :, at:at + heads * d].rearrange("p a (h d) -> p a h d", d=d)
            return v

        def sparse_scalar(t):
            project_scalar(t, [sa[:, :, i * COLS:i * COLS + w] for i, w in enumerate(SA_W)])
            flip_scalar(t, sa_qiT, 4)
            flip_scalar(t, sa_kiT, 1)
            for h in range(SA_IH):
                t.banks.take()
            rms_scalar(t, head_views(sa, 0, SA_H), TT * SA_H, 64)
            rms_scalar(t, sa[:, :, SA_K:SA_K + 64], TT, 64)
            flip_scalar(t, sa_qT, 8)
            flip_scalar(t, sa_kT, 1)
            attend_scalar(t, SA_H, lambda h: (sa_oT[64 * (h % 2):64 * (h % 2) + 64, h // 2, :], 64 * (h % 2), 64))
            t.piece += 4

        def sparse_vector(t):
            dve = t.e
            cos, sin = rope1[:, 0, :, :], rope1[:, 1, :, :]
            project_vector(t, 7)
            all_taken(t)
            for at, n in ((SA_QI, SA_IH), (SA_KI, 1)):
                v = head_views(sa, at, n)
                rotate(t, v[:, :, :, 0:32], v[:, :, :, 32:64], cos, sin, n, sa_rt)
            t.link(dve.tensor_scalar(sa[:, :, SA_WI:SA_WI + SA_IH], sa[:, :, SA_WI:SA_WI + SA_IH],
                                     float(SA_IH) ** -0.5 * float(SA_D) ** -0.5, None, ALU.mult))
            dve.tensor_copy(sa_kd[:, :, 1, 0:64], sa[:, :, SA_KI:SA_KI + 64])
            t.link(dve.tensor_copy(sa_kd[:, :, 1, 64:128], sa[:, :, SA_KI:SA_KI + 64]))
            flip_vector(t, sa_qiT, 4)
            flip_vector(t, sa_kiT, 1)
            for h in range(SA_IH):
                b = filled(t)
                dst = sa_sc if h == 0 else sa_tmp
                wi = sa[:, :, SA_WI + h:SA_WI + h + 1].to_broadcast([P, TT, S])
                dve.scalar_tensor_tensor(dst[:, :, :], halves(b), 0.0, wi, ALU.max, ALU.mult).then_inc(taken[b], 1)
                dve.wait_ge(taken[b], t.banks.uses[b])
                if h:
                    t.link(dve.tensor_tensor(sa_sc[:, :, :], sa_sc[:, :, :], sa_tmp[:, :, :], ALU.add))
            caus = const[:, C_CAUS:C_CAUS + TT * S].rearrange("p (a s) -> p a s", a=TT)
            t.link(dve.tensor_tensor(sa_sc[:, :, :], sa_sc[:, :, :], caus, ALU.add))
            for a in range(TT):
                for _ in range(TOPK // 8):
                    t.link(dve.max(sa_m8[:, :], sa_sc[:, a, :]))
                    t.link(dve.match_replace(sa_sc[:, a, :], sa_m8[:, :], sa_sc[:, a, :], TAKEN_KEY))
            t.link(dve.tensor_scalar(sa_bias[:, :, :], sa_sc[:, :, :], 0.5 * TAKEN_KEY, NEG, ALU.is_gt, ALU.mult))
            t.link(dve.tensor_tensor(sa_bias[:, :, :], sa_bias[:, :, :], caus, ALU.add))
            for at, n, g in ((0, SA_H, R_SAQ), (SA_K, 1, R_SAK)):
                v = head_views(sa, at, n)
                if n > 1:
                    rms_vector(t, v, TT * n, 64)
                else:
                    rms_vector(t, sa[:, :, at:at + 64], TT, 64)
                t.link(dve.tensor_tensor(v, v, rows[:, g:g + 64].unsqueeze(1).unsqueeze(1).to_broadcast([P, TT, n, 64]),
                                         ALU.mult))
                rotate(t, v[:, :, :, 0:32], v[:, :, :, 32:64], cos, sin, n, sa_rt)
            dve.tensor_copy(sa_kd[:, :, 0, 0:64], sa[:, :, SA_K:SA_K + 64])
            t.link(dve.tensor_copy(sa_kd[:, :, 0, 64:128], sa[:, :, SA_K:SA_K + 64]))
            flip_vector(t, sa_qT, 8)
            flip_vector(t, sa_kT, 1)
            attend_vector(t, SA_H, float(SA_D) ** -0.5, lambda h: sa_bias[:, :, :])
            t.piece += 4
            add_to_x(t, 1.0)

        Z_W = [COLS] * (Z_IN // COLS) + [Z_IN % COLS]

        def triple_sync(t, l):
            for i, w in enumerate(Z_W):
                load_cols(t, A["w_in_2"][l], i * COLS, w)
            for r in (0, 2):
                load_rows(t, A["w_br_na_2"][l], r)
            for r in (0, 2):
                load_rows(t, A["w_br_gla_2"][l], r)
            load_rows(t, A["mla_w_uq_2"][l], 0, MLA_H * MLA_QK)
            load_rows(t, A["mla_w_ukv_2"][l], 0)
            for r in (0, 2):
                load_rows(t, A["w_br_mla_2"][l], r)
            for r in range(0, 8, 2):
                load_rows(t, A["w_out_2"][l], r)

        def na_tensor(t, l):
            flip_tensor(t, lambda k, a: z[:, a, Z_NQ + k * P:Z_NQ + (k + 1) * P], 4, order=reverse)
            flip_tensor(t, lambda k, a: z[:, a, Z_NK + k * P:Z_NK + (k + 1) * P], 4)
            lo = lambda h: 64 * (h % 2)
            attend_tensor(t, NA_H, lambda h, a: [(na_qT[lo(h):lo(h) + 64, h // 2, a * P:(a + 1) * P],
                                                  na_kT[lo(h):lo(h) + 64, h // 2, :])],
                          lambda h, st: z[:, st, Z_NV + h * 64:Z_NV + (h + 1) * 64], 64, lo, order=reverse)
            all_taken(t)
            down_tensor(t, brT, 4)

        def na_scalar(t, l):
            for at in (Z_NQ, Z_NK):
                rms_scalar(t, head_views(z, at, NA_H), TT * NA_H, 64)
            flip_scalar(t, na_qT, 4)
            flip_scalar(t, na_kT, 4)
            attend_scalar(t, NA_H, lambda h: (brT[64 * (h % 2):64 * (h % 2) + 64, h // 2, :], 64 * (h % 2), 64))
            t.piece += 2

        def na_vector(t, l):
            dve = t.e
            for at, g in ((Z_NQ, R_NAQ), (Z_NK, R_NAK)):
                v = head_views(z, at, NA_H)
                rms_vector(t, v, TT * NA_H, 64)
                t.link(dve.tensor_tensor(v, v, rows[:, g + 64 * l:g + 64 * (l + 1)].unsqueeze(1).unsqueeze(1)
                                         .to_broadcast([P, TT, NA_H, 64]), ALU.mult))
            flip_vector(t, na_qT, 4)
            flip_vector(t, na_kT, 4)
            dve.wait_ge(bias_ready, l + 1)
            attend_vector(t, NA_H, 0.125, lambda h: na_bias[:, h, :, :])
            branch_vector(t, 0)

        def branch_vector(t, n):
            dve = t.e
            t.piece += 2
            dve.wait_ge(piece_done, RING + t.piece)
            gt = z[:, :, Z_GT + n * D:Z_GT + (n + 1) * D]
            if n == 0:
                t.done(dve.tensor_tensor(mix[:, :, :], acc2(), gt, ALU.mult), acc_taken)
            else:
                t.done(dve.tensor_tensor(mix_t[:, :, :], acc2(), gt, ALU.mult), acc_taken)
                t.link(dve.tensor_tensor(mix[:, :, :], mix[:, :, :], mix_t[:, :, :], ALU.add))

        def gla_tensor(t, l):
            pe = t.e
            b = claim(t)
            for d in range(2):
                for a in range(TT):
                    mm = pe.transpose(bank[0:16, b, d * S + a * P:d * S + (a + 1) * P],
                                      z[:, a, Z_GL + 16 * d:Z_GL + 16 * d + 16], ident)
            mm.then_inc(full[b], 1)
            flip_tensor(t, lambda k, a: z[:, a, Z_GQ + k * P:Z_GQ + (k + 1) * P], 2)
            flip_tensor(t, lambda k, a: z[:, a, Z_GK + k * P:Z_GK + (k + 1) * P], 2)
            all_taken(t)
            for d in range(2):
                b = claim(t)
                for a in range(TT):
                    mm = pe.matmul(bank[:, b, a * 256:(a + 1) * 256], glT[:, d, a * P:(a + 1) * P],
                                   gate_up[:, l, d, :], start=True, stop=True)
                mm.then_inc(full[b], 1)
            pe.wait_ge(dve_operand, t.see(dve_operand))
            for d, incl, rest in ((0, C_LE, C_GT), (1, C_GE, C_LT)):
                b = claim(t)
                for j in range(2):
                    for a in range(TT):
                        mm = pe.matmul(bank[:, b, j * S + a * P:j * S + (a + 1) * P], gg[:, d, a, j * P:(j + 1) * P],
                                       const[:, incl:incl + P], start=True, stop=True)
                mm.then_inc(full[b], 1)
                b = claim(t)
                for a in range(TT):
                    mm = pe.matmul(bank[:, b, a * 256:(a + 1) * 256], const[:, rest:rest + P], gg[:, d, a, :],
                                   start=True, stop=True)
                mm.then_inc(full[b], 1)
            pe.wait_ge(dve_operand, t.see(dve_operand))
            for h in range(GLA_H):
                b = claim(t)
                r, j = 64 * (h % 2), h // 2
                for d in range(2):
                    for a in range(TT):
                        o = (d * TT + a) * P
                        mm = pe.matmul(bank[:, b, o:o + P], em[r:r + 64, d, j, a * P:(a + 1) * P],
                                       ep[r:r + 64, d, j, a * P:(a + 1) * P], start=True, stop=True)
                mm.then_inc(full[b], 1)
            for d in range(2):
                for half in range(2):
                    b = claim(t)
                    r = 64 * half
                    for n in range(3):
                        c = n if d == 0 else 3 - n
                        if c % 2 != half:
                            continue
                        for h in range(GLA_H):
                            o = (h // 2 * 2 + n // 2) * P
                            mm = pe.matmul(bank[64 * (h % 2):64 * (h % 2) + 64, b, o:o + P],
                                           ke[r:r + 64, d, c // 2, h * 64:(h + 1) * 64],
                                           z[r:r + 64, c // 2, Z_GV + h * P:Z_GV + (h + 1) * P], start=True, stop=True)
                    mm.then_inc(full[b], 1)
            pe.wait_ge(dve_operand, t.see(dve_operand))
            for parity in range(2):
                b = claim(t)
                r = 64 * parity
                for j in range(2):
                    h = 2 * j + parity
                    for a in range(TT):
                        o = (j * TT + a) * P
                        pe.matmul(bank[:, b, o:o + P], a_in[:, h, a, :], z[:, a, Z_GV + h * P:Z_GV + (h + 1) * P],
                                  start=True, stop=False, skip_group_check=True)
                        for c in (2 * a, 2 * a + 1):
                            for d in range(2):
                                n = c - 1 if d == 0 else 2 - c
                                if n < 0:
                                    continue
                                mm = pe.matmul(bank[64 * (c % 2):64 * (c % 2) + 64, b, o:o + P],
                                               ep[r:r + 64, d, j, c * 64:(c + 1) * 64], gst[r:r + 64, d, j, n, :],
                                               start=False, stop=False, skip_group_check=True)
                mm.then_inc(full[b], 1)
            flip_tensor(t, lambda k, a: go[:, a, k, :], 4)
            all_taken(t)
            down_tensor(t, brT, 4)

        def gla_scalar(t, l):
            act = t.e
            b = filled(t)
            act.activation(glT[:, :, :], bank[0:16, b, :].rearrange("p (d s) -> p d s", d=2), ACT.Copy)\
                .then_inc(taken[b], 1)
            flip_scalar(t, gqT, 2, float(GLA_DK) ** -0.5)
            flip_scalar(t, gkT, 2)
            t.banks.take(), t.banks.take()
            act.wait_ge(to_act, t.see(to_act))
            t.link(act.activation(ge[:, :, :, :], ge[:, :, :, :], ACT.Exp))
            act.activation(ge[:, :, :, :], ge[:, :, :, :], ACT.Ln, bias=1.0).then_inc(to_dve, 1)
            tau = 1.0 / 16.0
            for d in range(2):
                b = filled(t)
                act.activation(ep[:, d, :, :], bank_of(b).rearrange("p (j s) -> p j s", j=2), ACT.Exp, scale=tau)
                act.activation(em[:, d, :, :], bank_of(b).rearrange("p (j s) -> p j s", j=2), ACT.Exp, scale=-tau)\
                    .then_inc(taken[b], 1)
                b = filled(t)
                act.activation(ke[:, d, :, :], bank_of(b).rearrange("p (a n) -> p a n", a=TT), ACT.Exp, scale=tau)\
                    .then_inc(taken[b], 1)
            for _ in range(8):
                t.banks.take()
            for parity in range(2):
                b = filled(t)
                act.activation(go[:, :, parity::2, :].rearrange("p a j v -> p j a v"),
                               bank_of(b).rearrange("p (j a v) -> p j a v", j=2, a=TT), ACT.Copy).then_inc(taken[b], 1)
            rms_scalar(t, go[:, :, :, :].rearrange("p a h v -> p (a h) v"), TT * GLA_H, P)
            flip_scalar(t, brT, 4, lambda k: gain[:, G_GLA + l:G_GLA + l + 1])
            t.piece += 2

        def gla_vector(t, l):
            dve = t.e
            t.banks.take()
            flip_vector(t, gqT, 2, float(GLA_DK) ** -0.5)
            flip_vector(t, gkT, 2)
            for d in range(2):
                b = filled(t)
                bias = rows[:, R_GB + (2 * l + d) * 256:R_GB + (2 * l + d + 1) * 256]
                dve.tensor_tensor(gg[:, d, :, :], bank_of(b).rearrange("p (a n) -> p a n", a=TT),
                                  bias.unsqueeze(1).to_broadcast([P, TT, 256]), ALU.add).then_inc(taken[b], 1)
                dve.wait_ge(taken[b], t.banks.uses[b])
            g3, e3 = z[:, :, 0:512], z[:, :, 512:1024]
            dve.scalar_tensor_tensor(e3, g3, -1.0, g3, ALU.mult, ALU.min)\
                .then_inc(to_act, 1)
            dve.wait_ge(to_dve, t.see(to_dve))
            t.done(dve.scalar_tensor_tensor(g3, g3, 0.0, e3, ALU.min, ALU.subtract), dve_operand)
            for _ in range(4):
                t.banks.take()
            all_taken(t)
            t.link(dve.tensor_copy(gdec[:, 0, :, :], ep[:, 0, :, :].rearrange("p j (c n) -> p j c n", n=64)[:, :, :, 63]))
            t.link(dve.tensor_copy(gdec[:, 1, :, :], ep[:, 1, :, :].rearrange("p j (c n) -> p j c n", n=64)[:, :, :, 0]))
            for d in range(2):
                dve.tensor_tensor(ep[:, d, :, :], ep[:, d, :, :], gqT[:, :, :], ALU.mult)
                dve.tensor_tensor(em[:, d, :, :], em[:, d, :, :], gkT[:, :, :], ALU.mult)
                ins = dve.tensor_tensor(ke[:, d, :, :], ke[:, d, :, :], z[:, :, Z_GK:Z_GK + 256], ALU.mult)
            t.done(ins, dve_operand)
            masks = const[:, C_LE:C_LE + 2 * P].rearrange("p (d n) -> p d n", d=2)
            for h in range(GLA_H):
                b = filled(t)
                dve.tensor_tensor(am[:, :, :, :], bank_of(b).rearrange("p (d a n) -> p d a n", d=2, a=TT),
                                  masks.unsqueeze(2).to_broadcast([P, 2, TT, P]), ALU.mult).then_inc(taken[b], 1)
                dve.wait_ge(taken[b], t.banks.uses[b])
                t.link(dve.tensor_tensor(a_in[:, h, :, :], am[:, 0, :, :], am[:, 1, :, :], ALU.add))
            for d in range(2):
                of_half = [filled(t), filled(t)]
                for n in range(3):
                    c = n if d == 0 else 3 - n
                    for j in range(2):
                        o = (2 * j + n // 2) * P
                        added = bank[:, of_half[c % 2], o:o + P]
                        if n == 0:
                            ins = dve.tensor_copy(gst[:, d, j, 0, :], added)
                        else:
                            ins = dve.scalar_tensor_tensor(gst[:, d, j, n, :], gst[:, d, j, n - 1, :],
                                                           gdec[:, d, j, c:c + 1], added, ALU.mult, ALU.add)
                    if n < 2:
                        t.link(ins)
                ins.then_inc(taken[of_half[c % 2]], 1)
                dve.wait_ge(taken[of_half[c % 2]], t.banks.uses[of_half[c % 2]])
                dve.sem_inc(taken[of_half[1 - c % 2]], 1)
            dve.sem_inc(dve_operand, 1)
            t.banks.take(), t.banks.take()
            all_taken(t)
            rms_vector(t, go[:, :, :, :].rearrange("p a h v -> p (a h) v"), TT * GLA_H, P)
            t.link(dve.tensor_tensor(go[:, :, :, :].rearrange("p a h v -> p a (h v)"),
                                     go[:, :, :, :].rearrange("p a h v -> p a (h v)"),
                                     z[:, :, Z_GR:Z_GR + 512], ALU.mult))
            flip_vector(t, brT, 4, lambda k: gain[:, G_GLA + l:G_GLA + l + 1])
            branch_vector(t, 1)

        def mla_tensor(t, l):
            pe = t.e
            flip_tensor(t, lambda k, a: z[:, a, Z_CQ + k * P:Z_CQ + (k + 1) * P], 2)
            flip_tensor(t, lambda k, a: z[:, a, Z_CKV + k * P:Z_CKV + (k + 1) * P], 2)
            all_taken(t)
            for i, n in enumerate((3, 4)):
                s = arrived(t)
                w = slot_rows(s, n * 256)
                for c in range(n):
                    b = claim(t, by_piece=(c == n - 1))
                    for a in range(TT):
                        for k in range(2):
                            mm = pe.matmul(bank[:, b, a * 256:(a + 1) * 256], cT[:, i, k, a * P:(a + 1) * P],
                                           w[:, k, c * 256:(c + 1) * 256], start=(k == 0), stop=(k == 1))
                    mm.then_inc(piece_done if c == n - 1 else full[b], 1)
            flip_tensor(t, lambda h, a: lq[:, a, h, 0:P], 4)
            flip_tensor(t, lambda h, a: lq[:, a, h, P:MLA_QK], 4, 64)
            flip_tensor(t, lambda h, a: lk[:, a, h, 0:P], 4)
            flip_tensor(t, lambda h, a: lk[:, a, h, P:MLA_QK], 4, 64)
            attend_tensor(t, MLA_H, lambda h, a: [(lqT[:, h, a * P:(a + 1) * P], lkT[:, h, :]),
                                                  (lqrT[:, h, a * P:(a + 1) * P], lkrT[:, h, :])],
                          lambda h, st: lkv[:, st, h, P:2 * P], P, lambda h: 0)
            all_taken(t)
            down_tensor(t, brT, 4)

        def mla_scalar(t, l):
            act = t.e
            for at in (Z_CQ, Z_CKV):
                rms_scalar(t, z[:, :, at:at + 256], TT, 256)
            flip_scalar(t, cT[:, 0], 2, gain_col(G_CQ + 2 * l))
            flip_scalar(t, cT[:, 1], 2, gain_col(G_CKV + 2 * l))
            qf = lq[:, :, :, :].rearrange("p a h d -> p a (h d)")
            kf = lkv[:, :, :, :].rearrange("p a h d -> p a (h d)")
            for n, dst in ((3, qf), (4, kf)):
                for c in range(n):
                    if c == n - 1:
                        b = t.banks.take(by_piece=True)
                        t.piece += 1
                        act.wait_ge(piece_done, RING + t.piece)
                    else:
                        b = filled(t)
                    act.activation(dst[:, :, c * 256:(c + 1) * 256], halves(b), ACT.Copy).then_inc(taken[b], 1)
            rms_scalar(t, lq, TT * MLA_H, MLA_QK)
            rms_scalar(t, lk, TT * MLA_H, MLA_QK)
            flip_scalar(t, lqT, 4)
            flip_scalar(t, lqrT, 4, None, 64)
            flip_scalar(t, lkT, 4)
            flip_scalar(t, lkrT, 4, None, 64)
            attend_scalar(t, MLA_H, lambda h: (brT[:, h, :], 0, P))
            t.piece += 2

        def mla_vector(t, l):
            dve = t.e
            for at in (Z_CQ, Z_CKV):
                rms_vector(t, z[:, :, at:at + 256], TT, 256)
            flip_vector(t, cT[:, 0], 2, gain_col(G_CQ + 2 * l))
            flip_vector(t, cT[:, 1], 2, gain_col(G_CKV + 2 * l))
            for n in (3, 4):
                for c in range(n):
                    t.banks.take(by_piece=(c == n - 1))
                t.piece += 1
            all_taken(t)
            dve.tensor_copy(lk[:, :, :, 0:P], lkv[:, :, :, 0:P])
            t.link(dve.tensor_copy(lk[:, :, :, P:MLA_QK],
                                   z[:, :, Z_KR:Z_KR + 64].unsqueeze(2).to_broadcast([P, TT, MLA_H, 64])))
            cos = const[:, C_COS:C_COS + 64].rearrange("p (a c) -> p a c", a=TT)
            sin = const[:, C_SIN:C_SIN + 64].rearrange("p (a c) -> p a c", a=TT)
            for v, g in ((lq, R_MQ), (lk, R_MK)):
                rms_vector(t, v, TT * MLA_H, MLA_QK)
                w = rows[:, g + MLA_QK * l:g + MLA_QK * (l + 1)]
                t.link(dve.tensor_tensor(v, v, w.unsqueeze(1).unsqueeze(1).to_broadcast([P, TT, MLA_H, MLA_QK]), ALU.mult))
                rotate(t, v[:, :, :, P:P + 32], v[:, :, :, P + 32:P + 64], cos, sin, MLA_H, z_rt)
            flip_vector(t, lqT, 4)
            flip_vector(t, lqrT, 4, None, 64)
            flip_vector(t, lkT, 4)
            flip_vector(t, lkrT, 4, None, 64)
            attend_vector(t, MLA_H, float(MLA_QK) ** -0.5, None)
            branch_vector(t, 2)

        def triple_tensor(t, l):
            project_tensor(t, Z_W)
            na_tensor(t, l)
            gla_tensor(t, l)
            mla_tensor(t, l)
            flip_tensor(t, lambda k, a: mix[:, a, k * P:(k + 1) * P], KD)
            all_taken(t)
            down_tensor(t, hT, KD)

        def triple_scalar(t, l):
            project_scalar(t, [z[:, :, i * COLS:i * COLS + w] for i, w in enumerate(Z_W)])
            for b in range(4):
                t.e.wait_ge(taken[b], t.banks.uses[b])
            t.e.activation(z[:, :, Z_GT:Z_IN], z[:, :, Z_GT:Z_IN], ACT.Sigmoid)
            t.link(t.e.activation(z[:, :, Z_GR:Z_GR + 512], z[:, :, Z_GR:Z_GR + 512], ACT.Silu))
            t.e.sem_inc(to_dve, 1)
            na_scalar(t, l)
            gla_scalar(t, l)
            mla_scalar(t, l)
            flip_scalar(t, hT, KD)
            t.piece += 4

        def triple_vector(t, l):
            project_vector(t, len(Z_W))
            all_taken(t)
            t.e.wait_ge(to_dve, t.see(to_dve))
            na_vector(t, l)
            gla_vector(t, l)
            mla_vector(t, l)
            flip_vector(t, hT, KD)
            t.piece += 4
            add_to_x(t, 1.0)

        FFNS = [(A["ffn_w_gate"][l, i], A["ffn_w_up"][l, i], A["ffn_w_down"][l, i], G_FFN + 8 * (2 * l + i))
                for l in range(DEPTH) for i in range(2)]
        for l in range(DEPTH):
            FFNS.append((A["ffn1_w1_2"][l], A["ffn1_w3_2"][l], A["ffn1_w2_2"][l], G_FFN1 + 8 * l))
            FFNS.append((A["ffn2_w1_2"][l], A["ffn2_w3_2"][l], A["ffn2_w2_2"][l], G_FFN2 + 8 * l))
        MIXERS = [(G_MIX, hybrid_sync, hybrid_tensor, hybrid_scalar, hybrid_vector, ()),
                  (G_MIX + 8, sparse_sync, sparse_tensor, sparse_scalar, sparse_vector, ())]
        MIXERS += [(G_MIX2 + 8 * l, triple_sync, triple_tensor, triple_scalar, triple_vector, (l,))
                   for l in range(DEPTH)]

        def flip_gains_scalar(t):
            b = filled(t)
            t.e.activation(gain[:, :], bank[:, b, 0:N_GA + N_GB], ACT.Copy).then_inc(taken[b], 1)
            t.e.wait_ge(taken[b], t.banks.uses[b])

        block = ctx.enter_context(nc.Block())

        @block.sync
        def _(sp):
            t = Thread(sp, steps["sp"])
            for n in range(4):
                ffn_sync(t, *FFNS[2 * n][:3])
                MIXERS[n][1](t, *MIXERS[n][5])
                ffn_sync(t, *FFNS[2 * n + 1][:3])
            sp.wait_ge(x_final, 1)
            sp.dma_start(out[0].rearrange("(a p) d -> p a d", p=P), x[:, :, :]).then_inc(out_done, 16)
            sp.wait_ge(out_done, 16)

        smalls = []

        def small(dst, src):
            smalls.append((dst, src))

        small(x[:, :, :], A["x"][0].rearrange("(a p) d -> p a d", p=P))
        small(const[:, :], A["constants"])
        at = 0
        for name in ("ffn_norm", "mix_norm", "ffn1_norm_2", "mix_norm_2", "ffn2_norm_2"):
            v = A[name].rearrange("l i (k p) -> (l i k) p", p=P) if len(A[name].shape) == 3 else \
                A[name].rearrange("l (k p) -> (l k) p", p=P)
            small(gain_rows[at:at + v.shape[0], 0, :], v)
            at += v.shape[0]
        at = 0
        for v in (A["hy_conv_w"][0].rearrange("t (k p) -> (t k) p", p=P),
                  A["hy_conv_b"].rearrange("l (k p) -> (l k) p", p=P),
                  A["hy_ssd_norm"].rearrange("l (k p) -> (l k) p", p=P),
                  A["hy_mlstm_norm"].rearrange("l (k p) -> (l k) p", p=P),
                  A["gla_out_norm_2"],
                  A["mla_cq_norm_2"].rearrange("l (k p) -> (l k) p", p=P),
                  A["mla_ckv_norm_2"].rearrange("l (k p) -> (l k) p", p=P)):
            small(gain_rows[at:at + v.shape[0], 1, :], v)
            at += v.shape[0]
        small(pos_i[:, :], A["positions"][0].rearrange("(a p) -> p a", p=P))
        small(rows[:, R_DSKIP:R_DSKIP + 16], A["hy_d_skip"][0].partition_broadcast(P))
        small(rows[:, R_SAQ:R_SAQ + 64], A["sa_q_norm"][0].partition_broadcast(P))
        small(rows[:, R_SAK:R_SAK + 64], A["sa_k_norm"][0].partition_broadcast(P))
        for l in range(DEPTH):
            small(rows[:, R_NAQ + 64 * l:R_NAQ + 64 * (l + 1)], A["na_q_norm_2"][l].partition_broadcast(P))
            small(rows[:, R_NAK + 64 * l:R_NAK + 64 * (l + 1)], A["na_k_norm_2"][l].partition_broadcast(P))
            small(rows[:, R_MQ + 192 * l:R_MQ + 192 * (l + 1)], A["mla_q_norm_2"][l].partition_broadcast(P))
            small(rows[:, R_MK + 192 * l:R_MK + 192 * (l + 1)], A["mla_k_norm_2"][l].partition_broadcast(P))
            for d, n in enumerate(("gf", "gb")):
                small(rows[:, R_GB + (2 * l + d) * 256:R_GB + (2 * l + d + 1) * 256],
                      A[f"gla_{n}_bias_2"][l].partition_broadcast(P))
                small(gate_up[:, l, d, :], A[f"gla_{n}_up_2"][l])
        small(heads_in[:, 0:1], A["hy_dt_bias"][0].unsqueeze(1))
        small(heads_in[:, 1:2], A["hy_a_log"][0].unsqueeze(1))
        small(heads_in[0:ML_H, 2:3], A["hy_igate_bias"][0].unsqueeze(1))
        small(fg_bias[:, :], A["hy_fgate_bias"][0].unsqueeze(1))
        wg3 = A["hy_w_in"][0].rearrange("(k p) c -> p k c", p=P)
        small(w_gates[:, :, 0:16], wg3[:, :, HY_DT:HY_DT + 16])
        small(w_gates[:, :, 16:24], wg3[:, :, HY_IG:HY_IG + 8])
        ALL_SMALL = 16 * len(smalls)

        @block.scalar
        def _(act):
            t = Thread(act, steps["act"])
            with nc.allow_non_contiguous_dma(reason="one position and one bias per partition"):
                for dst, src in smalls:
                    act.dma_start(dst, src).then_inc(small_in, 16)
            act.wait_ge(small_in, ALL_SMALL)
            act.wait_ge(to_act, t.see(to_act))
            act.activation(rope1[:, 1, :, :].rearrange("p a c -> p (a c)"), rope_t[:, 0, :], ACT.Sin)
            act.activation(rope1[:, 0, :, :].rearrange("p a c -> p (a c)"), rope_t[:, 1, :], ACT.Sin).then_inc(to_dve, 1)
            flip_gains_scalar(t)
            for n in range(4):
                pre_scalar(t, FFNS[2 * n][3])
                ffn_scalar(t, 2 * n)
                pre_scalar(t, MIXERS[n][0])
                MIXERS[n][3](t, *MIXERS[n][5])
                pre_scalar(t, FFNS[2 * n + 1][3])
                ffn_scalar(t, 2 * n + 1)

        @block.gpsimd
        def _(pool):
            t = Thread(pool, steps["pool"])
            pool.wait_ge(small_in, ALL_SMALL)
            win = const[:, C_WIN:C_WIN + GRID_W]
            for l in range(DEPTH):
                pool.wait_ge(bias_room, l + 1)
                rpb = A["na_rpb_2"]
                for a in range(TT):
                    for half in range(2):
                        for r in range(ROWS):
                            row = r - (2 * a + half) + WIN_R - 1
                            src = bass.AP(tensor=rpb.tensor,
                                          offset=(l * NA_H * RPB_R + row) * RPB_C + WIN_C - GRID_W,
                                          ap=[[1, GRID_W], [RPB_R * RPB_C, NA_H], [1, GRID_W]])
                            dst = na_bias[half * 64:(half + 1) * 64, :, a, r * GRID_W:(r + 1) * GRID_W]
                            pool.dma_start(dst, src).then_inc(bias_in, 16)
                pool.wait_ge(bias_in, 16 * 4 * ROWS * (l + 1))
                for h in range(NA_H):
                    v = na_bias[:, h, :, :].rearrange("p a (r c) -> p (a r) c", c=GRID_W)
                    t.link(pool.tensor_tensor(v, v, win.unsqueeze(1).to_broadcast([P, TT * ROWS, GRID_W]), ALU.add))
                pool.sem_inc(bias_ready, 1)

        @block.vector
        def _(dve):
            t = Thread(dve, steps["dve"])
            dve.memset(zeros[:, :], 0.0)
            t.done(dve.memset(ones[:, :], 1.0), setup_v)
            dve.wait_ge(small_in, ALL_SMALL)
            two_pi = 2 * np.pi
            t.link(dve.tensor_copy(pos_f[:, :], pos_i[:, :]))
            inv = const[:, C_INV:C_INV + 32]
            ang, n = rope_t[:, 0, :], rope_t[:, 2, :]
            for a in range(TT):
                t.link(dve.tensor_scalar(rope_t[:, 0, a * 32:(a + 1) * 32], inv, pos_f[:, a:a + 1], None, ALU.mult))
            magic = 1.5 * 2.0 ** 23
            t.link(dve.tensor_scalar(n, ang, 1.0 / two_pi, magic, ALU.mult, ALU.add))
            t.link(dve.tensor_scalar(n, n, magic, None, ALU.subtract))
            c1 = 6.28125
            c2 = float(np.float32(np.floor((two_pi - c1) * 2 ** 24) / 2 ** 24))
            c3 = two_pi - c1 - c2
            for c in (c1, c2, c3):
                t.link(dve.scalar_tensor_tensor(ang, n, -c, ang, ALU.mult, ALU.add))
            t.link(dve.tensor_scalar(rope_t[:, 1, :], ang, np.pi / 2, -two_pi, ALU.is_gt, ALU.mult))
            t.link(dve.scalar_tensor_tensor(rope_t[:, 1, :], ang, np.pi / 2, rope_t[:, 1, :], ALU.add, ALU.add))
            pi_in = 3.1415925
            t.link(dve.tensor_scalar(rope_t[:, 0:2, :], rope_t[:, 0:2, :], pi_in, -pi_in, ALU.min, ALU.max))
            dve.sem_inc(to_act, 1)
            dve.wait_ge(to_dve, t.see(to_dve))
            t.banks.take()
            all_taken(t)
            for n in range(4):
                pre_vector(t, FFNS[2 * n][3])
                ffn_vector(t, 2 * n)
                pre_vector(t, MIXERS[n][0])
                MIXERS[n][4](t, *MIXERS[n][5])
                if n in (1, 2):
                    dve.sem_inc(bias_room, 1)
                pre_vector(t, FFNS[2 * n + 1][3])
                ffn_vector(t, 2 * n + 1)
            dve.sem_inc(x_final, 1)

        @block.tensor
        def _(pe):
            t = Thread(pe, steps["pe"])
            t.acc_uses = 0
            pe.sem_inc(piece_done, RING)
            pe.wait_ge(setup_v, 1)
            pe.wait_ge(small_in, ALL_SMALL)
            b = claim(t)
            pe.transpose(bank[:, b, 0:N_GA], gain_rows[0:N_GA, 0, :], const[0:N_GA, C_ID:C_ID + N_GA])
            pe.transpose(bank[:, b, N_GA:N_GA + N_GB], gain_rows[0:N_GB, 1, :], const[0:N_GB, C_ID:C_ID + N_GB])\
                .then_inc(full[b], 1)
            for n in range(4):
                pre_tensor(t, FFNS[2 * n][3])
                ffn_tensor(t, 2 * n)
                pre_tensor(t, MIXERS[n][0])
                MIXERS[n][2](t, *MIXERS[n][5])
                pre_tensor(t, FFNS[2 * n + 1][3])
                ffn_tensor(t, 2 * n + 1)


_INS = ["x", "positions", "ffn_norm", "ffn_w_gate", "ffn_w_up", "ffn_w_down", "mix_norm", "hy_w_in", "hy_conv_w",
        "hy_conv_b", "hy_dt_bias", "hy_a_log", "hy_d_skip", "hy_ssd_norm", "hy_igate_bias", "hy_fgate_bias",
        "hy_mlstm_norm", "hy_w_out", "sa_w_in", "sa_q_norm", "sa_k_norm", "sa_w_out", "ffn1_norm_2", "ffn1_w1_2",
        "ffn1_w3_2", "ffn1_w2_2", "mix_norm_2", "w_in_2", "na_q_norm_2", "na_k_norm_2", "na_rpb_2", "gla_gf_up_2",
        "gla_gf_bias_2", "gla_gb_up_2", "gla_gb_bias_2", "gla_out_norm_2", "mla_cq_norm_2", "mla_ckv_norm_2",
        "mla_w_uq_2", "mla_w_ukv_2", "mla_q_norm_2", "mla_k_norm_2", "w_br_na_2", "w_br_gla_2", "w_br_mla_2",
        "w_out_2", "ffn2_norm_2", "ffn2_w1_2", "ffn2_w3_2", "ffn2_w2_2"]


def kernel(**inputs):
    import concourse.bacc as bacc
    from concourse.bass_utils import run_bass_kernel_spmd

    nc = bacc.Bacc("TRN2", target_bir_lowering=False, num_devices=1)
    arrays, aps = {}, {}
    for name in _INS:
        a = np.ascontiguousarray(inputs[name])
        arrays[f"in_{name}"] = a
        aps[name] = nc.dram_tensor(f"in_{name}", a.shape, mybir.dt.from_np(a.dtype), kind="ExternalInput").ap()
    arrays["in_constants"] = constants()
    aps["constants"] = nc.dram_tensor("in_constants", (P, N_CONST), F32, kind="ExternalInput").ap()
    out = nc.dram_tensor("out_x", (1, S, D), F32, kind="ExternalOutput").ap()
    two_blocks(nc, aps, out)
    r = run_bass_kernel_spmd(nc, [arrays], core_ids=[0])
    return r.results[0]["out_x"]
```

```python
from contextlib import ExitStack

import concourse.bass as bass
import numpy as np
from concourse import mybir

F32 = mybir.dt.float32
F32R = mybir.dt.float32r
BF16 = mybir.dt.bfloat16
I32 = mybir.dt.int32
ALU = mybir.AluOpType
ACT = mybir.ActivationFunctionType
AX = mybir.AxisListType

P = 128
S = 256
TT = S // P
D = 1024
KD = D // P
FF = 2816
DEPTH = 2
EPS = 1e-6
NEG = -1e30
TAKEN_KEY = -3e38

RAW = 3
PARTS = 2
SLOT = 2048
LOOP = 6
COLS = 256
CHUNKS = FF // COLS

SSD_W = 1024
SSD_H = 16
SSD_G = 2
SSD_N = 128
CONV_DIM = SSD_W + 2 * SSD_G * SSD_N
CONV_T = CONV_DIM // P
CONV_K = 4
ML_H = 4
ML_V = 256
ML_VA = ML_V + 1
HY_Z, HY_XBC, HY_DT = 0, SSD_W, SSD_W + CONV_DIM
HY_Q = HY_DT + SSD_H
HY_K = HY_Q + 512
HY_V = HY_K + 512
HY_O = HY_V + 1024
HY_IG = HY_O + 1024
HY_FG = HY_IG + ML_H

SA_H, SA_IH, SA_D = 16, 8, 64
SA_IN = SA_H * SA_D + 2 * SA_D + SA_IH * SA_D + SA_D + SA_IH
SA_K, SA_V, SA_QI = 1024, 1088, 1152
SA_KI, SA_WI = SA_QI + SA_IH * SA_D, SA_QI + SA_IH * SA_D + SA_D
SA_W = [COLS] * 6 + [SA_IN - 6 * COLS]
TOPK = min(256, S // 4)

GRID_W, WIN_R, WIN_C = 64, 8, 16
ROWS = S // GRID_W
NA_H = 8
RPB_R, RPB_C = 2 * WIN_R - 1, 2 * WIN_C - 1
GLA_H, GLA_DK, GLA_DV, GLA_C = 4, 64, 128, 64
MLA_H, MLA_NOPE, MLA_R, MLA_DV = 4, 128, 64, 128
MLA_QK = MLA_NOPE + MLA_R
Z_NQ, Z_NK, Z_NV = 0, 512, 1024
Z_GQ, Z_GK, Z_GV, Z_GR, Z_GL = 1536, 1792, 2048, 2560, 3072
Z_CQ, Z_CKV, Z_KR, Z_GT = 3104, 3360, 3616, 3680
Z_IN = Z_GT
Z_W = [COLS] * (Z_IN // COLS) + [Z_IN % COLS]

G_FFN, G_MIX, G_FFN1, G_MIX2, G_FFN2 = 0, 32, 48, 64, 80
G_CW, G_CB, G_SSD, G_ML, G_GLA, G_CQ, G_CKV = 96, 144, 156, 164, 172, 174, 178
N_GA, N_GB = 96, 86

R_DSKIP, R_SAQ, R_SAK, R_NAQ, R_NAK = 0, 16, 80, 144, 272
R_GB, R_MQ, R_MK = 400, 1424, 1808
N_ROW = 2192

C_ID, C_CAUS_T, C_CAUS, C_WIN = 0, 128, 256, 768
C_LE, C_GT, C_GE, C_LT = 832, 960, 1088, 1216
C_INV, C_COS, C_SIN, C_REV = 1344, 1376, 1440, 1504
N_CONST = 1632


FFN_PIECES = [SLOT] * (3 * CHUNKS)
MIXER_PIECES = [[SLOT] * (6 + 4 + 12 + 8), [KD * w for w in SA_W] + [SLOT] * 4]
MIXER_PIECES += [[KD * w for w in Z_W] + [SLOT] * (4 + 2 + 4 + 2) + [2 * MLA_H * MLA_QK, SLOT] + [SLOT] * (4 + 2 + 4)] * 2
PIECES = [n for m in MIXER_PIECES for n in FFN_PIECES + m + FFN_PIECES]


def constants():
    c = np.zeros((P, N_CONST), np.float32)
    i, j = np.arange(P)[:, None], np.arange(P)[None, :]
    c[:, C_ID:C_ID + P] = i == j
    c[:, C_CAUS_T:C_CAUS_T + P] = np.where(i <= j, 0, NEG)
    key = np.arange(S)[None, :]
    for t in range(TT):
        c[:, C_CAUS + t * S:C_CAUS + (t + 1) * S] = np.where(key <= i + t * P, 0, NEG)
    c[:, C_REV:C_REV + P] = (i // GRID_W == j // GRID_W) & (i % GRID_W + j % GRID_W == GRID_W - 1)
    cq, ck = GRID_W - 1 - np.arange(P)[:, None] % GRID_W, np.arange(GRID_W)[None, :]
    c0 = np.clip(cq - WIN_C // 2, 0, GRID_W - WIN_C)
    c[:, C_WIN:C_WIN + GRID_W] = np.where((ck >= c0) & (ck < c0 + WIN_C), 0, NEG)
    same = i // GLA_C == j // GLA_C
    for at, m in ((C_LE, i <= j), (C_GT, i > j), (C_GE, i >= j), (C_LT, i < j)):
        c[:, at:at + P] = same & m
    half = MLA_R // 2
    inv = (np.float32(10000.0) ** (-np.arange(half, dtype=np.float32) / np.float32(half))).astype(np.float32)
    c[:, C_INV:C_INV + half] = inv
    ang = np.arange(S, dtype=np.float32)[:, None] * inv[None, :]
    for t in range(TT):
        c[:, C_COS + t * half:C_COS + (t + 1) * half] = np.cos(ang[t * P:(t + 1) * P])
        c[:, C_SIN + t * half:C_SIN + (t + 1) * half] = np.sin(ang[t * P:(t + 1) * P])
    return c


class Tally:

    def __init__(self):
        self.at = {}

    def __call__(self, sem, n=1):
        self.at[sem.name] = self.at.get(sem.name, 0) + n
        return self.at[sem.name]


class Banks:

    def __init__(self):
        self.next, self.uses, self.filled = 0, [0] * 4, [0] * 4

    def take(self, by_piece=False):
        b = self.next
        self.next = (b + 1) % 4
        self.uses[b] += 1
        self.filled[b] += not by_piece
        return b


class Thread:

    def __init__(self, e, step):
        self.e, self.step = e, step
        self.see, self.banks, self.piece = Tally(), Banks(), 0

    def link(self, ins):
        ins.then_inc(self.step, 1)
        self.e.wait_ge(self.step, self.see(self.step))

    def done(self, ins, sem):
        ins.then_inc(sem, 1)
        self.e.wait_ge(sem, self.see(sem))


def two_blocks(nc, A, out):
    with ExitStack() as ctx:
        def sb(name, shape, dt=F32, where=ctx):
            return where.enter_context(nc.sbuf_tensor(name, shape, dt))

        def sem(name):
            return ctx.enter_context(nc.semaphore(name))

        x = sb("x", [P, TT, D])
        hT = sb("hT", [P, 2, KD, S], F32R)
        raw = sb("raw", [P, RAW, SLOT])
        parts = sb("parts", [P, PARTS, 2, SLOT], F32R)
        silu_gate = sb("silu_gate", [P, 2, 512])
        with ExitStack() as m:
            gated = sb("gated", [P, 2, 2, 512], F32R, where=m)
        with ExitStack() as m:
            cb = sb("cb", [P, SSD_G, TT, P], where=m)
            b_tok = sb("b_tok", [P, SSD_G, P], where=m)
            cst = sb("cst", [P, ML_H, ML_VA], where=m)
        with ExitStack() as m:
            gain_rows = sb("gain_rows", [P, 2, P], where=m)
            rope_t = sb("rope_t", [P, 3, TT * 32], where=m)
            w_gates = sb("w_gates", [P, KD, 24], where=m)
        ctx.enter_context(nc.sbuf_tensor("gated_room", [P, 2048], F32))
        const = sb("const", [P, N_CONST])
        gain = sb("gain", [P, N_GA + N_GB])
        rows = sb("rows", [P, N_ROW])
        heads_in = sb("heads_in", [SSD_H, 4])
        w_gates_s = sb("w_gates_s", [P, 2, KD, 24], F32R)
        gate_up = sb("gate_up", [16, DEPTH, 2, 256])
        zeros = sb("zeros", [P, P], BF16)
        ones = sb("ones", [SSD_H, P])
        pos_i = sb("pos_i", [P, TT], I32)
        pos_f = sb("pos_f", [P, TT])
        rope1 = sb("rope1", [P, 2, TT, 32])
        squares = sb("squares", [P, 2048])
        stat = sb("stat", [P, 3, 32])
        normed = squares[:, :].rearrange("p (a d) -> p a d", a=TT)
        gdec = sb("gdec", [P, 2, 2, 4])
        heads4 = sb("heads4", [ML_H, 1])
        fg_bias = sb("fg_bias", [ML_H, 1])

        with ExitStack() as m:
            xbc = sb("xbc", [P, CONV_T, CONV_K - 1 + S], where=m)
            conv = sb("conv", [P, CONV_T, S], where=m)
            mq = sb("mq", [P, ML_H, S], where=m)
            mk = sb("mk", [P, ML_H, S], where=m)
            mv = sb("mv", [P, TT, ML_H, ML_VA], where=m)
            og = sb("og", [P, TT, 1024], where=m)
            hrow = sb("hrow", [SSD_H, 10, S], where=m)
            gtok = sb("gtok", [P, TT, 24], where=m)
            cols = sb("cols", [P, TT, 64], where=m)
            ecols = sb("ecols", [P, SSD_H], where=m)
            xs = sb("xs", [P, TT, SSD_W], where=m)
            xd = sb("xd", [P, TT, SSD_W], where=m)
            late = sb("late", [P, TT * ML_H * ML_VA], where=m)
            hden = sb("hden", [P, 2, TT * ML_H], where=m)
            zg = late[:, 0:TT * SSD_W].rearrange("p (a c) -> p a c", a=TT)
            hm = late[:, :].rearrange("p (c h v) -> p c h v", c=TT, h=ML_H)
            xde = squares[:, 0:1024]
            state = squares[:, 1024:2048].rearrange("p (g n) -> p g n", g=SSD_G)
            seg = silu_gate
            kw = conv[:, 4:6, :].rearrange("p k (h n) -> p (k h) n", n=P)
            qw = conv[:, 6:8, :].rearrange("p k (h n) -> p (k h) n", n=P)
        with ExitStack() as m:
            wT = sb("wT", [P, SSD_H, S], where=m)
        with ExitStack() as m:
            yT = sb("yT", [P, 2, 16, S], F32R, where=m)
        with ExitStack() as m:
            soft_s = sb("soft_s", [P, 2, TT, S], where=m)
            soft_p = sb("soft_p", [P, 2, TT, S], where=m)
            soft_pT = sb("soft_pT", [P, 2, 512], where=m)
            soft_m = sb("soft_m", [P, 2, 2, TT], where=m)
            soft_r = sb("soft_r", [P, 2, TT], where=m)
            with ExitStack() as g:
                sa = sb("sa", [P, TT, SA_IN], where=g)
                sa_kd = sb("sa_kd", [P, TT, 2, P], where=g)
                sa_qT = sb("sa_qT", [P, 8, S], where=g)
                sa_kT = sb("sa_kT", [P, 1, S], where=g)
                sa_qiT = sb("sa_qiT", [P, 4, S], where=g)
                sa_kiT = sb("sa_kiT", [P, 1, S], where=g)
                sa_sc = sb("sa_sc", [P, TT, S], where=g)
                sa_tmp = sb("sa_tmp", [P, TT, S], where=g)
                sa_m8 = sb("sa_m8", [P, 8], where=g)
                sa_bias = sb("sa_bias", [P, TT, S], where=g)
                sa_rt = sb("sa_rt", [P, 4, TT, SA_H * 32], where=g)
            z = sb("z", [P, TT, Z_IN], where=m)
            mix = sb("mix", [P, TT, D], where=m)
            gt = sb("gt", [P, TT, D], where=m)
            brT = gated[:, :, :, :].rearrange("p q a (k s) -> p q (a k) s", s=S)
            with ExitStack() as g:
                na_bias = sb("na_bias", [P, NA_H, TT, S], where=g)
                na_qT = sb("na_qT", [P, 4, S], where=g)
                na_kT = silu_gate[:, :, :].rearrange("p a (k s) -> p (a k) s", s=S)
            with ExitStack() as g:
                ep = sb("ep", [P, 2, 2, S], where=g)
                em = sb("em", [P, 2, 2, S], where=g)
                gqT = sb("gqT", [P, 2, S], where=g)
                gkT = sb("gkT", [P, 2, S], where=g)
                gst = sb("gst", [P, 2, 2, 3, P], where=g)
                go = sb("go", [P, TT, GLA_H, P], where=g)
                gg = z[:, :, 0:512].rearrange("p a (d n) -> p d a n", d=2)
                ge = z[:, :, 512:1024].rearrange("p a (d n) -> p d a n", d=2)
                ke = z[:, :, 1024:1536].rearrange("p a (d n) -> p d a n", d=2)
                am = squares[:, 0:512].rearrange("p (d a n) -> p d a n", d=2, a=TT)
                glT = squares[0:16, 512:1024].rearrange("p (d s) -> p d s", d=2)
                a_in = squares[:, 1024:2048].rearrange("p (h a n) -> p h a n", h=GLA_H, a=TT)
            with ExitStack() as g:
                cT = sb("cT", [P, 2, 2, 2, S], F32R, where=g)
                lqT = sb("lqT", [P, MLA_H, S], where=g)
                lkT = sb("lkT", [P, MLA_H, S], where=g)
                lqrT = sb("lqrT", [64, MLA_H, S], where=g)
                lkrT = sb("lkrT", [64, MLA_H, S], where=g)
                lq = z[:, :, 0:768].rearrange("p a (h d) -> p a h d", h=MLA_H)
                lk = z[:, :, 768:1536].rearrange("p a (h d) -> p a h d", h=MLA_H)
                lkv = z[:, :, 1536:2560].rearrange("p a (h d) -> p a h d", h=MLA_H)
            z_rt = squares[:, :].rearrange("p (n a c) -> p n a c", n=4, a=TT)

        acc = ctx.enter_context(nc.psum_tensor("acc", [P, 4, 512], F32))
        bank = ctx.enter_context(nc.psum_tensor("bank", [P, 4, 512], F32))

        raw_in = [sem(f"raw_in{i}") for i in range(RAW)]
        hi_ready, lo_ready = sem("hi_ready"), sem("lo_ready")
        flip_hi = sem("flip_hi")
        full = [sem(f"bank_full{i}") for i in range(4)]
        taken = [sem(f"bank_taken{i}") for i in range(4)]
        piece_done = sem("piece_done")
        small_in = sem("small_in")
        bias_in = sem("na_bias_in")
        bias_ready = sem("na_bias_ready")
        bias_room = sem("na_bias_room")
        out_done = sem("out_done")
        setup_v, setup_g, setup_a = sem("setup_vector"), sem("setup_gpsimd"), sem("setup_scalar")
        silu_ready, gate_made, gated_ready = sem("silu_ready"), sem("gate_made"), sem("gated_ready")
        acc_full, acc_taken = sem("acc_full"), sem("acc_taken")
        norm_src, squares_ready, var_ready, root_ready = (
            sem("norm_src"), sem("squares_ready"), sem("var_ready"), sem("root_ready"))
        flip_src = sem("flip_src")
        to_act, to_dve, dve_operand, act_operand = (
            sem("vector_to_scalar"), sem("scalar_to_vector"), sem("vector_operand"), sem("scalar_operand"))
        score_ready, prob_ready, softmax_ready = sem("score_ready"), sem("prob_ready"), sem("softmax_ready")
        x_final = sem("x_final")
        steps = {n: sem(f"{n}_step") for n in ("pe", "act", "dve", "pool", "sp")}

        ident = const[:, C_ID:C_ID + P]
        reverse = const[:, C_REV:C_REV + P]

        def selector(n, h):
            return const[0:n, C_ID + h:C_ID + h + 1].to_broadcast([n, P])

        def bank_of(b):
            return bank[:, b, :]

        def halves(b, w=COLS):
            return bank[:, b, :].rearrange("p (a c) -> p a c", a=2)[:, :, 0:w]

        def acc2():
            return acc[:, :, :].rearrange("p (a b) c -> p a (b c)", a=TT)

        def all_taken(t):
            for b in range(4):
                if t.banks.uses[b]:
                    t.e.wait_ge(taken[b], t.banks.uses[b])

        def claim(t, by_piece=False):
            b = t.banks.take(by_piece)
            if t.banks.uses[b] > 1:
                t.e.wait_ge(taken[b], t.banks.uses[b] - 1)
            return b

        def filled(t):
            b = t.banks.take()
            t.e.wait_ge(full[b], t.banks.filled[b])
            return b

        def load(t, src, i=None):
            n = t.piece
            t.piece += 1
            t.e.wait_ge(lo_ready, later(n + 1, i, LOOP))
            k = src.shape[1]
            dst = raw[:, n % RAW, 0:k * src.shape[2]].rearrange("p (k c) -> p k c", k=k)
            t.e.dma_start(dst, src).then_inc(raw_in[n % RAW], 16)

        def later(count, i, step):
            return count if i is None else i * step + count

        def cols_of(w, c, n=COLS):
            return w.rearrange("(k p) c -> p k c", p=P)[:, :, bass.ds(c, n)]

        def rows_of(w, r, n=D):
            return w.rearrange("(k p) c -> p k c", p=P)[:, bass.ds(r, 2), 0:n]

        def load_cols(t, w, c, n=COLS):
            load(t, cols_of(w, c, n))

        def load_rows(t, w, r, n=D):
            load(t, rows_of(w, r, n))

        def split_hi(t, n, i=None):
            if n < len(PIECES):
                size = PIECES[n]
                t.e.wait_ge(raw_in[n % RAW], later(16 * (n // RAW + 1), i, 16 * LOOP // RAW))
                t.e.wait_ge(piece_done, later(n + 1, i, LOOP))
                t.e.activation(parts[:, n % PARTS, 0, 0:size], raw[:, n % RAW, 0:size], ACT.Copy).then_inc(hi_ready, 1)

        def split_lo(t, n, i=None):
            if n < len(PIECES):
                size = PIECES[n]
                t.e.wait_ge(hi_ready, later(n + 1, i, LOOP))
                t.e.tensor_tensor(parts[:, n % PARTS, 1, 0:size], raw[:, n % RAW, 0:size],
                                  parts[:, n % PARTS, 0, 0:size].bitcast(F32), ALU.subtract).then_inc(lo_ready, 1)

        def next_hi(t):
            t.piece += 1
            split_hi(t, t.piece - 1 + PARTS)

        def next_lo(t):
            t.piece += 1
            split_lo(t, t.piece - 1 + PARTS)

        def through(t):
            return PARTS + t.piece

        def arrived(t, i=None, n=None):
            if n is None:
                n = t.piece
                t.piece += 1
            t.e.wait_ge(lo_ready, later(RAW + n + 1, i, LOOP))
            return n % PARTS

        def slot_cols(s, part, w=COLS):
            return parts[:, s, part, 0:KD * w].rearrange("p (k c) -> p k c", k=KD)

        def slot_rows(s, part, n=D):
            return parts[:, s, part, 0:2 * n].rearrange("p (k c) -> p k c", k=2)

        PASSES = ((0, 0), (0, 1), (1, 0))

        def ffn_sync(t, wg, wu, wd):
            load_cols(t, wg, 0)
            load_cols(t, wu, 0)
            n0 = t.piece
            with t.e.Fori(0, (CHUNKS - 1) // 2) as i:
                for j in range(2):
                    load(t, cols_of(wg, i * 512 + COLS * (1 + j)), i)
                    load(t, cols_of(wu, i * 512 + COLS * (1 + j)), i)
                    load(t, rows_of(wd, i * 4 + 2 * j), i)
            t.piece = n0 + 3 * (CHUNKS - 1)
            load_rows(t, wd, 2 * (CHUNKS - 1))

        def up_bank(t, c, which):
            return (t.banks.next + 2 * (c % 2) + which) % 4

        def ffn_up(t, c, s, which, hT_k=None):
            pe = t.e
            for f in range(2):
                for k in range(KD):
                    if hT_k and f == 0 and k % 2 == 0:
                        hT_k(k // 2)
                    for w, h in PASSES:
                        mm = pe.matmul(bank[:, up_bank(t, c, which), f * S:(f + 1) * S],
                                       slot_cols(s, w)[:, k, f * P:(f + 1) * P], hT[:, h, k, :],
                                       start=(k == 0 and w + h == 0), stop=(k == KD - 1 and w == 1))
            mm.then_inc(piece_done, 1)

        def down_product(pe, stationary, s, k, a, first, last):
            for g, w in PASSES:
                for n in range(2):
                    mm = pe.matmul(acc[:, 2 * a + n, :], stationary(g), slot_rows(s, w)[:, k, n * 512:(n + 1) * 512],
                                   start=(first and g + w == 0), stop=(last and g == 1), skip_group_check=True)
            return mm

        def ffn_down(pe, c, s, last=False):
            order = [(a, f) for a in range(TT) for f in range(2)]
            for a, f in order:
                mm = down_product(pe, lambda g: gated[:, g, c % 2, f * S + a * P:f * S + (a + 1) * P], s, f, a,
                                  False, last and f == 1)
                if last and (a, f) == (0, 1):
                    mm.then_inc(acc_full, 1)
            mm.then_inc(piece_done, 1)

        def ffn_tensor(t, k):
            pe = t.e
            acc_is_free(t)
            for b in range(4):
                pe.matmul(acc[:, b, :], zeros[:, :], zeros[:, :].unsqueeze(1).to_broadcast([P, 4, P]), start=True,
                          stop=False, skip_group_check=True)
            ffn_up(t, 0, arrived(t), 0, hT_waits(t))
            ffn_up(t, 0, arrived(t), 1)
            n0 = t.piece
            with pe.Fori(0, (CHUNKS - 1) // 2) as i:
                for j in range(2):
                    for which in range(2):
                        ffn_up(t, 1 + j, arrived(t, i, n0 + 3 * j + which), which)
                    s = arrived(t, i, n0 + 3 * j + 2)
                    pe.wait_ge(gated_ready, i * 2 + (CHUNKS * k + 1 + j))
                    ffn_down(pe, j, s)
            t.piece += 3 * (CHUNKS - 1)
            s = arrived(t)
            pe.wait_ge(gated_ready, CHUNKS * (k + 1))
            ffn_down(pe, CHUNKS - 1, s, last=True)

        def ffn_scalar(t, k):
            act = t.e
            n0 = t.piece

            def chunk(c, n, i=None):
                split_hi(t, n + 2, i)
                act.wait_ge(piece_done, later(PARTS + n + 1, i, LOOP))
                act.activation(silu_gate[:, c % 2, :], bank_of(up_bank(t, c, 0)), ACT.Silu).then_inc(silu_ready, 1)
                split_hi(t, n + 3, i)
                if c:
                    split_hi(t, n + 4, i)

            chunk(0, n0)
            with act.Fori(0, (CHUNKS - 3) // 2) as i:
                for j in range(2):
                    chunk(1 + j, n0 + 2 + 3 * j, i)
            for c in (CHUNKS - 2, CHUNKS - 1):
                chunk(c, n0 + 2 + 3 * (c - 1))
            t.piece += 3 * CHUNKS - 1
            next_hi(t)

        def ffn_vector(t, k):
            dve = t.e
            n0 = t.piece

            def chunk(c, n, i=None):
                split_lo(t, n + 2, i)
                dve.wait_ge(piece_done, later(PARTS + n + 2, i, LOOP))
                dve.wait_ge(silu_ready, later(CHUNKS * k + c + 1, i, 2))
                v = silu_gate[:, c % 2, :]
                dve.tensor_tensor(v, bank_of(up_bank(t, c, 1)), v, ALU.mult).then_inc(gate_made, 1)
                dve.wait_ge(gate_made, later(2 * (CHUNKS * k + c) + 1, i, 4))
                dve.tensor_copy(gated[:, 0, c % 2, :], v).then_inc(gate_made, 1)
                dve.wait_ge(gate_made, later(2 * (CHUNKS * k + c) + 2, i, 4))
                dve.tensor_tensor(gated[:, 1, c % 2, :], v, gated[:, 0, c % 2, :].bitcast(F32), ALU.subtract)\
                    .then_inc(gated_ready, 1)
                split_lo(t, n + 3, i)
                if c:
                    split_lo(t, n + 4, i)

            chunk(0, n0)
            with dve.Fori(0, (CHUNKS - 3) // 2) as i:
                for j in range(2):
                    chunk(1 + j, n0 + 2 + 3 * j, i)
            for c in (CHUNKS - 2, CHUNKS - 1):
                chunk(c, n0 + 2 + 3 * (c - 1))
            t.piece += 3 * CHUNKS - 1
            add_to_x(t, 0.5)

        def acc_is_free(t):
            if t.acc_uses:
                t.e.wait_ge(acc_taken, t.acc_uses)
            t.acc_uses += 1

        def add_to_x(t, scale):
            dve = t.e
            dve.wait_ge(acc_full, t.see(acc_full))
            dve.scalar_tensor_tensor(x[:, 0, :], acc2()[:, 0, :], scale, x[:, 0, :], ALU.mult, ALU.add)\
                .then_inc(norm_src, 1)
            dve.wait_ge(piece_done, PARTS + t.piece + 1)
            dve.scalar_tensor_tensor(x[:, 1, :], acc2()[:, 1, :], scale, x[:, 1, :], ALU.mult, ALU.add)\
                .then_inc(norm_src, 1)
            dve.wait_ge(norm_src, t.see(norm_src, 2))
            dve.sem_inc(acc_taken, 1)
            t.see(acc_taken)
            next_lo(t)

        def rms_scalar(t, src, n, d):
            act = t.e
            act.wait_ge(norm_src, t.see(norm_src))
            sq = squares[:, 0:n * d]
            if len(src.shape) == 3:
                sq = sq.rearrange("p (n d) -> p n d", n=n)
            else:
                sq = sq.rearrange("p (a n d) -> p a n d", a=TT, d=d)
            act.activation(sq, src, ACT.Square).then_inc(squares_ready, 1)
            root_scalar(t, n)

        def root_vector(t, n, d):
            dve = t.e
            v, y, w = stat[:, 0, 0:n], stat[:, 1, 0:n], stat[:, 2, 0:n]
            t.done(dve.tensor_scalar(v, v, 1.0 / d, EPS, ALU.mult, ALU.add), var_ready)
            dve.wait_ge(root_ready, t.see(root_ready))
            t.link(dve.tensor_tensor(w, y, y, ALU.mult))
            t.link(dve.tensor_tensor(w, w, v, ALU.mult))
            t.link(dve.tensor_scalar(w, w, -0.5, 1.5, ALU.mult, ALU.add))
            t.link(dve.tensor_tensor(y, y, w, ALU.mult))
            return y

        def root_scalar(t, n):
            act = t.e
            act.wait_ge(var_ready, t.see(var_ready))
            t.link(act.activation(stat[:, 1, 0:n], stat[:, 0, 0:n], ACT.Ln))
            act.activation(stat[:, 1, 0:n], stat[:, 1, 0:n], ACT.Exp, scale=-0.5).then_inc(root_ready, 1)

        def rms_vector(t, src, n, d, dst=None):
            dve = t.e
            dst = src if dst is None else dst
            dve.sem_inc(norm_src, 1)
            t.see(norm_src)
            dve.wait_ge(squares_ready, t.see(squares_ready))
            t.link(dve.tensor_reduce(stat[:, 0, 0:n], squares[:, 0:n * d].rearrange("p (n d) -> p n d", n=n), AX.X,
                                     ALU.add))
            y = root_vector(t, n, d)
            if len(src.shape) == 3:
                yb = y.unsqueeze(2).to_broadcast([P, n, d])
            else:
                yb = y.rearrange("p (a n) -> p a n", a=TT).unsqueeze(3).to_broadcast([P, TT, n // TT, d])
            t.link(dve.tensor_tensor(dst, src, yb, ALU.mult))

        def flip_tensor(t, src, n, rows_out=P, order=None):
            pe = t.e
            pe.wait_ge(flip_src, t.see(flip_src))
            for k0 in range(0, n, 2):
                b = claim(t)
                for k in range(k0, min(k0 + 2, n)):
                    for a in range(TT):
                        o = (k - k0) * S + a * P
                        mm = pe.transpose(bank[0:rows_out, b, o:o + P], src(k, a), ident if order is None else order)
                mm.then_inc(full[b], 1)

        def flip_out(t, dst, n, scale, rows_out, mine):
            for k0 in range(0, n, 2):
                if (k0 // 2) % 2 != mine:
                    t.banks.take()
                    continue
                b = filled(t)
                ks = range(k0, min(k0 + 2, n))
                if not callable(scale):
                    parts = [(dst[0:rows_out, k0:k0 + len(ks), :],
                              bank[0:rows_out, b, 0:len(ks) * S].rearrange("p (k s) -> p k s", s=S), scale)]
                else:
                    parts = [(dst[0:rows_out, k, :], bank[0:rows_out, b, (k - k0) * S:(k - k0 + 1) * S], scale(k))
                             for k in ks]
                for o, i, g in parts:
                    if mine == 0:
                        ins = t.e.activation(o, i, ACT.Copy, scale=1.0 if g is None else g)
                    else:
                        ins = t.e.tensor_scalar(o, i, 1.0 if g is None else g, None, ALU.mult)
                ins.then_inc(taken[b], 1)

        def flip_scalar(t, dst, n, scale=None, rows_out=P):
            flip_out(t, dst, n, scale, rows_out, 0)

        def flip_vector(t, dst, n, scale=None, rows_out=P):
            t.e.sem_inc(flip_src, 1)
            flip_out(t, dst, n, scale, rows_out, 1)

        def gain_col(at):
            return lambda k: gain[:, at + k:at + k + 1]

        def split_flip_scalar(t, dst, n, scale=None):
            for k0 in range(0, n, 2):
                b = filled(t)
                if scale is None:
                    ins = t.e.activation(dst[:, 0, k0:k0 + 2, :], halves(b), ACT.Copy)
                else:
                    for k in (k0, k0 + 1):
                        ins = t.e.activation(dst[:, 0, k, :], halves(b)[:, k - k0, :], ACT.Copy, scale=scale(k))
                ins.then_inc(flip_hi, 1)

        def split_flip_vector(t, dst, n, scale=None, signal=True):
            if signal:
                t.e.sem_inc(flip_src, 1)
            for k0 in range(0, n, 2):
                b = filled(t)
                t.e.wait_ge(flip_hi, t.see(flip_hi))
                if scale is None:
                    ins = t.e.tensor_tensor(dst[:, 1, k0:k0 + 2, :], halves(b), dst[:, 0, k0:k0 + 2, :].bitcast(F32),
                                            ALU.subtract)
                else:
                    for k in (k0, k0 + 1):
                        ins = t.e.scalar_tensor_tensor(dst[:, 1, k, :], halves(b)[:, k - k0, :], scale(k),
                                                       dst[:, 0, k, :].bitcast(F32), ALU.mult, ALU.subtract)
                ins.then_inc(taken[b], 1)

        def pre_tensor(t, at):
            flip_tensor(t, lambda k, a: normed[:, a, k * P:(k + 1) * P], KD)
            t.hT_banks = [((t.banks.next + j) % 4, t.banks.uses[(t.banks.next + j) % 4]) for j in range(4)]

        def hT_waits(t):
            return lambda j: t.e.wait_ge(taken[t.hT_banks[j][0]], t.hT_banks[j][1])

        def pre_scalar(t, at):
            act = t.e
            for a in range(TT):
                act.wait_ge(norm_src, t.see(norm_src))
                ins = act.activation(squares[:, a * D:(a + 1) * D], x[:, a, :], ACT.Square,
                                     accum_out=stat[:, 0, a:a + 1])
            ins.then_inc(squares_ready, 1)
            root_scalar(t, TT)
            split_flip_scalar(t, hT, KD, gain_col(at))

        def pre_vector(t, at):
            dve = t.e
            dve.wait_ge(squares_ready, t.see(squares_ready))
            y = root_vector(t, TT, D)
            for a in range(TT):
                ins = dve.tensor_scalar(normed[:, a, :], x[:, a, :], y[:, a:a + 1], None, ALU.mult)
            ins.then_inc(flip_src, 1)
            split_flip_vector(t, hT, KD, gain_col(at), signal=False)

        def project_tensor(t, widths, feature_major=False, hT_k=None):
            pe = t.e
            for w in widths:
                s = arrived(t)
                b = claim(t, by_piece=True)
                for a in range(2):
                    for k in range(KD):
                        if hT_k and a == 0 and k % 2 == 0:
                            hT_k(k // 2)
                        for p, q in PASSES:
                            if feature_major:
                                mm = pe.matmul(bank[:, b, a * S:(a + 1) * S], slot_cols(s, p)[:, k, a * P:(a + 1) * P],
                                               hT[:, q, k, :], start=(k == 0 and p + q == 0),
                                               stop=(k == KD - 1 and p == 1))
                            else:
                                mm = pe.matmul(bank[:, b, a * COLS:a * COLS + w], hT[:, p, k, a * P:(a + 1) * P],
                                               slot_cols(s, q, w)[:, k, :], start=(k == 0 and p + q == 0),
                                               stop=(k == KD - 1 and p == 1))
                mm.then_inc(piece_done, 1)
                hT_k = None

        def project_scalar(t, dsts, scale=1.0, func=ACT.Copy):
            for dst in dsts:
                b = t.banks.take(by_piece=True)
                next_hi(t)
                t.e.wait_ge(piece_done, through(t))
                t.e.activation(dst, halves(b, dst.shape[-1]), func, scale=scale).then_inc(taken[b], 1)

        def project_vector(t, n):
            for _ in range(n):
                t.banks.take(by_piece=True)
                next_lo(t)

        def down_tensor(t, actT, n):
            pe = t.e
            acc_is_free(t)
            for k0 in range(0, n, 2):
                s = arrived(t)
                end = k0 == n - 2
                for a in range(TT):
                    for k in (k0, k0 + 1):
                        mm = down_product(pe, lambda g: actT[:, g, k, a * P:(a + 1) * P], s, k - k0, a, k == 0,
                                          k == n - 1)
                    if end and a == 0:
                        mm.then_inc(acc_full, 1)
                mm.then_inc(piece_done, 1)

        def down_scalar(t, n):
            for _ in range(n // 2):
                next_hi(t)

        def down_vector(t, n):
            for _ in range(n // 2 - 1):
                next_lo(t)

        def rotate(t, lo, hi, cos, sin, heads, tmp):
            dve = t.e
            c = cos.unsqueeze(2).to_broadcast([P, TT, heads, 32])
            s = sin.unsqueeze(2).to_broadcast([P, TT, heads, 32])
            v = [tmp[:, n, :, 0:heads * 32].rearrange("p a (h c) -> p a h c", c=32) for n in range(4)]
            dve.tensor_tensor(v[0], lo, c, ALU.mult)
            dve.tensor_tensor(v[1], hi, s, ALU.mult)
            dve.tensor_tensor(v[2], lo, s, ALU.mult)
            t.link(dve.tensor_tensor(v[3], hi, c, ALU.mult))
            dve.tensor_tensor(lo, v[0], v[1], ALU.subtract)
            t.link(dve.tensor_tensor(hi, v[2], v[3], ALU.add))

        def attend_tensor(t, heads, parts, value, dv, base, order=None, fill=None):
            pe = t.e
            all_taken(t)
            for i in range(heads + 2):
                if i < heads:
                    b = claim(t)
                    for a in range(TT):
                        ps = parts(i, a)
                        for n, (q, k) in enumerate(ps):
                            mm = pe.matmul(bank[:, b, a * S:(a + 1) * S], q, k, start=(n == 0), stop=(n == len(ps) - 1))
                    mm.then_inc(full[b], 1)
                if fill:
                    fill(i)
                if 1 <= i <= heads:
                    pe.wait_ge(softmax_ready, t.see(softmax_ready))
                    b = claim(t)
                    for st in range(TT):
                        for a in range(TT):
                            o = st * S + a * P
                            mm = pe.transpose(bank[:, b, o:o + P], soft_p[:, (i - 1) % 2, a, st * P:(st + 1) * P],
                                              ident if order is None else order)
                    mm.then_inc(full[b], 1)
                if i >= 2:
                    h = i - 2
                    pe.wait_ge(act_operand, t.see(act_operand))
                    b = claim(t)
                    r = base(h)
                    for st in range(TT):
                        mm = pe.matmul(bank[r:r + dv, b, 0:S], value(h, st), soft_pT[:, h % 2, st * S:(st + 1) * S],
                                       start=(st == 0), stop=(st == TT - 1))
                    mm.then_inc(full[b], 1)

        def attend_scalar(t, heads, dst, fill=None):
            act = t.e
            for i in range(heads + 2):
                if i < heads:
                    t.banks.take()
                    act.wait_ge(score_ready, t.see(score_ready))
                    for a in range(TT):
                        ins = act.activation(soft_p[:, i % 2, a, :], soft_s[:, i % 2, a, :], ACT.Exp,
                                             bias=soft_m[:, i % 2, 0, a:a + 1], accum_out=soft_m[:, i % 2, 1, a:a + 1])
                    ins.then_inc(prob_ready, 1)
                if fill:
                    fill(i)
                if 1 <= i <= heads:
                    b = filled(t)
                    act.activation(soft_pT[:, (i - 1) % 2, :], bank_of(b), ACT.Copy).then_inc(taken[b], 1)
                    act.wait_ge(taken[b], t.banks.uses[b])
                    act.sem_inc(act_operand, 1)
                if i >= 2:
                    b = filled(t)
                    o, r, dv = dst(i - 2)
                    act.activation(o(0), bank[r:r + dv, b, 0:S], ACT.Copy).then_inc(flip_hi, 1)

        def attend_vector(t, heads, scale, bias, dst, fill=None):
            dve = t.e
            for i in range(heads + 2):
                if i < heads:
                    b = filled(t)
                    s = soft_s[:, i % 2, :, :]
                    if bias is None:
                        ins = dve.tensor_scalar(s, halves(b), scale, None, ALU.mult)
                    else:
                        ins = dve.scalar_tensor_tensor(s, halves(b), scale, bias(i), ALU.mult, ALU.add)
                    ins.then_inc(taken[b], 1)
                    dve.wait_ge(taken[b], t.banks.uses[b])
                    dve.tensor_reduce(soft_m[:, i % 2, 0, :], s, AX.X, ALU.max, negate=True).then_inc(score_ready, 1)
                if fill:
                    fill(i)
                if 1 <= i <= heads:
                    t.banks.take()
                    h = i - 1
                    dve.wait_ge(prob_ready, t.see(prob_ready))
                    t.link(dve.reciprocal(soft_r[:, h % 2, :], soft_m[:, h % 2, 1, :]))
                    for a in range(TT):
                        ins = dve.tensor_scalar(soft_p[:, h % 2, a, :], soft_p[:, h % 2, a, :],
                                                soft_r[:, h % 2, a:a + 1], None, ALU.mult)
                    ins.then_inc(softmax_ready, 1)
                if i >= 2:
                    b = filled(t)
                    dve.wait_ge(flip_hi, t.see(flip_hi))
                    o, r, dv = dst(i - 2)
                    dve.tensor_tensor(o(1), bank[r:r + dv, b, 0:S], o(0).bitcast(F32), ALU.subtract)\
                        .then_inc(taken[b], 1)

        R_DT, R_FG, R_IG, R_T, R_L, R_A, R_ACS, R_DEND, R_B, R_M = range(10)
        HY_FEATURE = ((HY_XBC, 6), (HY_Q, 2), (HY_K, 2))
        HY_TOKEN = ((HY_Z, 4), (HY_V, 4), (HY_O, 4))

        def hybrid_sync(t):
            w = A["hy_w_in"][0]
            for at, n in HY_FEATURE + HY_TOKEN:
                for i in range(n):
                    load_cols(t, w, at + i * COLS)
            for r in range(0, 16, 2):
                load_rows(t, A["hy_w_out"][0], r)

        def hybrid_tensor(t):
            pe = t.e
            b = claim(t)
            hT_k = hT_waits(t)
            for a in range(TT):
                for k in range(KD):
                    if a == 0 and k % 2 == 0:
                        hT_k(k // 2)
                    for p, q in PASSES:
                        mm = pe.matmul(bank[:, b, a * 32:a * 32 + 24], hT[:, p, k, a * P:(a + 1) * P],
                                       w_gates_s[:, q, k, :], start=(k == 0 and p + q == 0), stop=(k == KD - 1 and p == 1))
            mm.then_inc(full[b], 1)
            project_tensor(t, [COLS] * 6, feature_major=True)
            all_taken(t)
            b = claim(t)
            for col, n, o in ((0, SSD_H, 0), (16, ML_H, S)):
                for a in range(TT):
                    mm = pe.transpose(bank[0:n, b, o + a * P:o + (a + 1) * P], gtok[:, a, col:col + n], ident)
            mm.then_inc(full[b], 1)
            b = claim(t)
            for a in range(TT):
                mm = pe.transpose(bank[0:ML_H, b, a * P:(a + 1) * P], gtok[:, a, 20:24], ident)
            mm.then_inc(full[b], 1)
            project_tensor(t, [COLS] * 4, feature_major=True)
            project_tensor(t, [COLS] * 12)
            pe.wait_ge(dve_operand, t.see(dve_operand))
            b = claim(t)
            for c in range(TT):
                for row, n, o in ((R_DT, 16, 0), (R_ACS, 16, 16), (R_DEND, 16, 32), (R_B, 4, 48), (R_T, 4, 52),
                                  (R_A, 4, 56)):
                    mm = pe.transpose(bank[:, b, c * 64 + o:c * 64 + o + n], hrow[0:n, row, c * P:(c + 1) * P],
                                      const[0:n, C_ID:C_ID + n])
            mm.then_inc(full[b], 1)
            pe.wait_ge(act_operand, t.see(act_operand))
            b = claim(t)
            for g in range(SSD_G):
                for c in range(TT):
                    o = (g * TT + c) * P
                    mm = pe.matmul(bank[:, b, o:o + P], conv[:, 8 + g, c * P:(c + 1) * P],
                                   conv[:, 10 + g, c * P:(c + 1) * P], start=True, stop=True)
            mm.then_inc(full[b], 1)
            for c in range(TT):
                for h in range(2):
                    b = claim(t)
                    for k in range(4):
                        mm = pe.transpose(bank[:, b, k * P:(k + 1) * P], conv[:, 4 * h + k, c * P:(c + 1) * P], ident)
                    mm.then_inc(full[b], 1)
            b = claim(t)
            for g in range(SSD_G):
                mm = pe.transpose(bank[:, b, g * P:(g + 1) * P], conv[:, 8 + g, 0:P], ident)
            mm.then_inc(full[b], 1)
            for h in range(0, SSD_H, 2):
                b = claim(t)
                for j in range(2):
                    mm = pe.matmul(bank[:, b, j * S:(j + 1) * S], selector(SSD_H, h + j),
                                   hrow[:, R_ACS, :], start=True, stop=True)
                mm.then_inc(full[b], 1)
            pe.wait_ge(dve_operand, t.see(dve_operand))
            all_taken(t)
            for g in range(SSD_G):
                b = claim(t)
                pe.matmul(bank_of(b), b_tok[:, g, :], xde[:, g * 512:(g + 1) * 512], start=True, stop=True)\
                    .then_inc(full[b], 1)
            pe.wait_ge(dve_operand, t.see(dve_operand))
            acc_is_free(t)
            for c in range(TT):
                for h in range(SSD_H):
                    mm = pe.matmul(acc[:, 2 * c + h // 8, (h % 8) * 64:(h % 8 + 1) * 64], wT[:, h, c * P:(c + 1) * P],
                                   xd[:, c, h * 64:(h + 1) * 64], start=True, stop=True)
            mm.then_inc(acc_full, 1)
            all_taken(t)
            for g in range(SSD_G):
                b = claim(t)
                pe.matmul(bank_of(b), conv[:, 10 + g, P:S], state[:, g, :], start=True, stop=True).then_inc(full[b], 1)

            b = claim(t)
            for h in range(ML_H):
                mm = pe.transpose(bank[:, b, h * P:(h + 1) * P], mk[:, h, 0:P], ident)
            mm.then_inc(full[b], 1)
            all_taken(t)
            for h in range(ML_H):
                b = claim(t)
                pe.matmul(bank[:, b, 0:ML_VA], kw[:, h, :], mv[:, 0, h, :], start=True, stop=True).then_inc(full[b], 1)
            for h in range(0, ML_H, 2):
                b = claim(t)
                for j in range(2):
                    mm = pe.matmul(bank[:, b, j * S:(j + 1) * S], selector(ML_H, h + j),
                                   hrow[0:ML_H, R_M, :], start=True, stop=True)
                mm.then_inc(full[b], 1)
                b = claim(t)
                for j in range(2):
                    for c in range(TT):
                        mm = pe.matmul(bank[:, b, j * S + c * P:j * S + (c + 1) * P], mk[:, h + j, c * P:(c + 1) * P],
                                       mq[:, h + j, c * P:(c + 1) * P], start=True, stop=True)
                mm.then_inc(full[b], 1)
            b = claim(t)
            for h in range(ML_H):
                mm = pe.matmul(bank[:, b, h * P:(h + 1) * P], selector(ML_H, h),
                               hrow[0:ML_H, R_L, P:S], start=True, stop=True)
            mm.then_inc(full[b], 1)
            all_taken(t)
            for c in range(TT):
                for h in range(ML_H):
                    b = claim(t)
                    mm = pe.matmul(bank[:, b, 0:ML_VA], wT[:, h, c * P:(c + 1) * P], mv[:, c, h, :],
                                   start=True, stop=(c == 0))
                    if c:
                        mm = pe.matmul(bank[:, b, 0:ML_VA], qw[:, h, :], cst[:, h, :], start=False, stop=True)
                    mm.then_inc(full[b], 1)
            flip_tensor(t, lambda k, a: xs[:, a, k * P:(k + 1) * P], 8)
            flip_tensor(t, lambda k, a: xd[:, a, k * P:(k + 1) * P], 8)
            all_taken(t)
            down_tensor(t, yT, 16)

        def hybrid_scalar(t):
            act = t.e
            b = filled(t)
            act.activation(gtok[:, :, :], bank[:, b, 0:64].rearrange("p (a n) -> p a n", a=TT)[:, :, 0:24], ACT.Copy)\
                .then_inc(taken[b], 1)
            act.activation(heads_in[:, 3:4], heads_in[:, 1:2], ACT.Exp).then_inc(to_dve, 1)
            project_scalar(t, [xbc[:, 2 * i:2 * i + 2, CONV_K - 1:] for i in range(6)])
            t.banks.take(), t.banks.take()
            project_scalar(t, [mq[:, 2 * i:2 * i + 2, :] for i in range(2)], scale=float(P) ** -0.5)
            project_scalar(t, [mk[:, 2 * i:2 * i + 2, :] for i in range(2)])
            act.wait_ge(to_act, t.see(to_act))
            t.link(act.activation(hrow[:, R_T:R_T + 2, :], hrow[:, R_T:R_T + 2, :], ACT.Exp))
            act.activation(hrow[:, R_T:R_T + 2, :], hrow[:, R_T:R_T + 2, :], ACT.Ln, bias=1.0).then_inc(to_dve, 1)
            project_scalar(t, [zg[:, :, i * COLS:(i + 1) * COLS] for i in range(4)])
            project_scalar(t, [mv[:, :, i, 0:ML_V] for i in range(4)])
            project_scalar(t, [og[:, :, i * COLS:(i + 1) * COLS] for i in range(4)])
            act.wait_ge(to_act, t.see(to_act))
            act.activation(hrow[:, R_DEND, :], hrow[:, R_DEND, :], ACT.Exp)
            act.activation(hrow[0:ML_H, R_T, :], hrow[0:ML_H, R_T, :], ACT.Exp)
            act.activation(hrow[0:ML_H, R_A, :], hrow[0:ML_H, R_A, :], ACT.Exp)
            act.activation(hrow[0:ML_H, R_L, :], hrow[0:ML_H, R_L, :], ACT.Exp).then_inc(to_dve, 1)
            act.wait_ge(to_act, t.see(to_act))
            t.link(act.activation(conv[:, :, :], conv[:, :, :], ACT.Silu))
            act.sem_inc(act_operand, 1)
            act.activation(zg[:, :, :], zg[:, :, :], ACT.Silu)
            act.activation(og[:, :, :], og[:, :, :], ACT.Sigmoid).then_inc(to_dve, 1)
            b = filled(t)
            act.activation(cols[:, :, :], bank[:, b, 0:TT * 64].rearrange("p (c n) -> p c n", c=TT), ACT.Copy)\
                .then_inc(taken[b], 1)
            act.wait_ge(taken[b], t.banks.uses[b])
            act.activation(ecols[:, :], cols[:, 1, 16:32], ACT.Exp).then_inc(to_dve, 1)
            b = filled(t)
            act.activation(cb[:, :, :, :], bank_of(b).rearrange("p (g c n) -> p g c n", g=2, c=2), ACT.Copy)\
                .then_inc(taken[b], 1)
            for c in range(TT):
                for h in range(2):
                    b = filled(t)
                    act.activation(xs[:, c, h * 512:(h + 1) * 512], bank_of(b), ACT.Copy).then_inc(taken[b], 1)
            b = filled(t)
            act.activation(b_tok[:, :, :], bank[:, b, 0:S].rearrange("p (g n) -> p g n", g=2),
                           ACT.Copy).then_inc(taken[b], 1)
            for h in range(0, SSD_H, 2):
                t.banks.take()
                act.wait_ge(to_act, t.see(to_act))
                act.activation(seg[:, (h // 2) % 2, :], seg[:, (h // 2) % 2, :], ACT.Exp).then_inc(to_dve, 1)
            for g in range(SSD_G):
                b = filled(t)
                act.activation(state[:, g, :], bank_of(b), ACT.Copy).then_inc(taken[b], 1)
            t.banks.take(), t.banks.take()
            rms_scalar(t, xs[:, :, :].rearrange("p a (g d) -> p (a g) d", g=2), 4, 512)
            t.banks.take()
            for h in range(ML_H):
                b = filled(t)
                act.activation(cst[:, h, :], bank[:, b, 0:ML_VA], ACT.Copy).then_inc(taken[b], 1)
            for h in range(0, ML_H, 2):
                t.banks.take(), t.banks.take()
                act.wait_ge(to_act, t.see(to_act))
                act.activation(seg[:, (h // 2) % 2, :], seg[:, (h // 2) % 2, :], ACT.Exp).then_inc(to_dve, 1)
            t.banks.take()
            for c in range(TT):
                for h in range(ML_H):
                    b = filled(t)
                    act.activation(hm[:, c, h, :], bank[:, b, 0:ML_VA], ACT.Copy).then_inc(taken[b], 1)
            rms_scalar(t, xd[:, :, :].rearrange("p a (g d) -> p (a g) d", g=ML_H), 8, 256)
            split_flip_scalar(t, yT[:, :, 0:8, :], 8, gain_col(G_SSD))
            split_flip_scalar(t, yT[:, :, 8:16, :], 8, gain_col(G_ML))
            down_scalar(t, 16)

        def hybrid_vector(t):
            dve = t.e
            r = lambda n, k=SSD_H: hrow[0:k, n, :]
            t.link(dve.memset(hrow[:, :, :], 0.0))
            dve.memset(mv[:, :, :, ML_V:ML_VA], 1.0)
            t.link(dve.memset(xbc[:, :, 0:CONV_K - 1], 0.0))
            t.banks.take()
            project_vector(t, 6)
            b = filled(t)
            dve.tensor_scalar(r(R_DT), bank[0:SSD_H, b, 0:S], heads_in[:, 0:1], None, ALU.add)
            dve.tensor_scalar(r(R_IG, ML_H), bank[0:ML_H, b, S:2 * S], heads_in[0:ML_H, 2:3], None, ALU.add)\
                .then_inc(taken[b], 1)
            dve.wait_ge(taken[b], t.banks.uses[b])
            b = filled(t)
            dve.tensor_scalar(r(R_FG, ML_H), bank[0:ML_H, b, 0:S], fg_bias[:, 0:1], None, ALU.add).then_inc(taken[b], 1)
            dve.wait_ge(taken[b], t.banks.uses[b])
            both, e = hrow[:, R_DT:R_DT + 2, :], hrow[:, R_T:R_T + 2, :]
            dve.wait_ge(to_dve, t.see(to_dve))
            dve.scalar_tensor_tensor(e, both, -1.0, both, ALU.mult, ALU.min).then_inc(to_act, 1)
            dve_waits_for_taps = [(b, t.banks.uses[b]) for b in range(4)]
            for b, n in dve_waits_for_taps:
                dve.wait_ge(taken[b], n)
            for k in range(CONV_T):
                project_vector(t, 1)
                o = conv[:, k, :]
                tap = lambda n: gain[:, G_CW + n * CONV_T + k:G_CW + n * CONV_T + k + 1]
                t.link(dve.tensor_scalar(o, xbc[:, k, 0:S], tap(0), gain[:, G_CB + k:G_CB + k + 1], ALU.mult, ALU.add))
                for n in range(1, CONV_K):
                    t.link(dve.scalar_tensor_tensor(o, xbc[:, k, n:n + S], tap(n), o, ALU.mult, ALU.add))
            project_vector(t, 4)
            dve.wait_ge(to_dve, t.see(to_dve))
            t.link(dve.scalar_tensor_tensor(r(R_DT), r(R_DT), 0.0, r(R_T), ALU.max, ALU.add))
            t.link(dve.scalar_tensor_tensor(r(R_FG), r(R_FG), 0.0, r(R_L), ALU.min, ALU.subtract))
            t.link(dve.tensor_scalar(r(R_A), r(R_DT), heads_in[:, 3:4], -1.0, ALU.mult, ALU.mult))
            for c in range(TT):
                cc = slice(c * P, (c + 1) * P)
                t.link(dve.tensor_tensor_scan(hrow[:, R_ACS, cc], ones[:, :], hrow[:, R_A, cc], 0.0, ALU.mult, ALU.add))
                t.link(dve.tensor_scalar(hrow[:, R_DEND, cc], hrow[:, R_ACS, cc], hrow[:, R_ACS, c * P + P - 1:c * P + P],
                                         -1.0, ALU.subtract, ALU.mult))
            q = ML_H
            for c in range(TT):
                cc = slice(c * P, (c + 1) * P)
                last = c * P + P - 1
                m_in = 0.0 if c == 0 else heads4[:, 0:1]
                t.link(dve.tensor_tensor_scan(hrow[0:q, R_L, cc], ones[0:q, :], hrow[0:q, R_FG, cc], 0.0,
                                              ALU.mult, ALU.add))
                t.link(dve.tensor_tensor(hrow[0:q, R_B, cc], hrow[0:q, R_IG, cc], hrow[0:q, R_L, cc], ALU.subtract))
                t.link(dve.tensor_tensor_scan(hrow[0:q, R_M, cc], hrow[0:q, R_B, cc], hrow[0:q, R_B, cc], m_in,
                                              ALU.max, ALU.max))
                t.link(dve.scalar_tensor_tensor(hrow[0:q, R_T, cc], hrow[0:q, R_L, cc], -1.0, hrow[0:q, R_M, cc],
                                                ALU.mult, ALU.subtract))
                t.link(dve.tensor_scalar(hrow[0:q, R_A, cc], hrow[0:q, R_B, cc], hrow[0:q, R_M, last:last + 1], None,
                                         ALU.subtract))
                if c == 0:
                    t.link(dve.tensor_tensor(heads4[:, 0:1], hrow[0:q, R_L, last:last + 1],
                                             hrow[0:q, R_M, last:last + 1], ALU.add))
                t.link(dve.tensor_scalar(hrow[0:q, R_M, cc], hrow[0:q, R_M, cc], -1.0, None, ALU.mult))
                if c == 0:
                    t.link(dve.memset(hrow[0:q, R_L, cc], 0.0))
                else:
                    t.link(dve.tensor_scalar(hrow[0:q, R_L, cc], hrow[0:q, R_M, cc], m_in, None, ALU.add))
            dve.sem_inc(to_act, 1)
            dve.wait_ge(to_dve, t.see(to_dve))
            dve.sem_inc(dve_operand, 1)
            all_taken(t)
            dve.sem_inc(to_act, 1)
            b_cols = t.banks.take()
            dve.wait_ge(to_dve, t.see(to_dve, 2))
            t.banks.take()
            for _ in range(5):
                t.banks.take()
            all_taken(t)
            v4 = lambda ap: ap.rearrange("p c (h d) -> p c h d", h=SSD_H)
            t.link(dve.tensor_tensor(v4(xd[:, :, :]), v4(xs[:, :, :]),
                                     cols[:, :, 0:16].unsqueeze(3).to_broadcast([P, TT, SSD_H, 64]), ALU.mult))
            caus = const[:, C_CAUS_T:C_CAUS_T + P]

            def weigh(h):
                dve.wait_ge(to_dve, t.see(to_dve))
                g = h // 8
                t.link(dve.tensor_tensor(wT[:, h:h + 2, :].rearrange("p j (c n) -> p j c n", c=TT),
                                         seg[:, (h // 2) % 2, :].rearrange("p (j c n) -> p j c n", j=2, c=TT),
                                         cb[:, g, :, :].unsqueeze(1).to_broadcast([P, 2, TT, P]), ALU.mult))

            for h in range(0, SSD_H, 2):
                b = filled(t)
                s4 = seg[:, (h // 2) % 2, :].rearrange("p (j c n) -> p j c n", j=2, c=TT)
                a4 = cols[:, :, 16 + h:18 + h].rearrange("p c j -> p j c").unsqueeze(3).to_broadcast([P, 2, TT, P])
                dve.tensor_tensor(s4, bank_of(b).rearrange("p (j c n) -> p j c n", j=2, c=TT), a4, ALU.subtract)\
                    .then_inc(taken[b], 1)
                dve.wait_ge(taken[b], t.banks.uses[b])
                s3 = seg[:, (h // 2) % 2, :].rearrange("p (k n) -> p k n", n=P)
                dve.tensor_tensor(s3, s3, caus.unsqueeze(1).to_broadcast([P, 4, P]), ALU.add).then_inc(to_act, 1)
                if h == 0:
                    t.link(dve.tensor_tensor(xde[:, :].rearrange("p (h d) -> p h d", h=SSD_H),
                                             xd[:, 0, :].rearrange("p (h d) -> p h d", h=SSD_H),
                                             cols[:, 0, 32:48].unsqueeze(2).to_broadcast([P, SSD_H, 64]), ALU.mult))
                    dve.sem_inc(dve_operand, 1)
                else:
                    weigh(h - 2)
            weigh(SSD_H - 2)
            dve.sem_inc(dve_operand, 1)
            t.link(dve.tensor_tensor(v4(xs[:, :, :]), v4(xs[:, :, :]),
                                     rows[:, R_DSKIP:R_DSKIP + 16].unsqueeze(1).unsqueeze(3)
                                     .to_broadcast([P, TT, SSD_H, 64]), ALU.mult))
            dve.wait_ge(acc_full, t.see(acc_full))
            t.done(dve.tensor_tensor(xs[:, :, :], xs[:, :, :], acc2(), ALU.add), acc_taken)
            t.banks.take(), t.banks.take()
            for g in range(SSD_G):
                b = filled(t)
                dve.tensor_tensor(seg[:, g, :].rearrange("p (h d) -> p h d", h=8),
                                  bank_of(b).rearrange("p (h d) -> p h d", h=8),
                                  ecols[:, 8 * g:8 * g + 8].unsqueeze(2).to_broadcast([P, 8, 64]), ALU.mult)\
                    .then_inc(taken[b], 1)
                dve.wait_ge(taken[b], t.banks.uses[b])
                t.link(dve.tensor_tensor(xs[:, 1, g * 512:(g + 1) * 512], xs[:, 1, g * 512:(g + 1) * 512],
                                         seg[:, g, :], ALU.add))
            t.link(dve.tensor_tensor(xs[:, :, :], xs[:, :, :], zg[:, :, :], ALU.mult))
            rms_vector(t, xs[:, :, :].rearrange("p a (g d) -> p (a g) d", g=2), 4, 512)
            b = filled(t)
            dve.tensor_tensor(kw[:, :, :], bank_of(b).rearrange("p (h n) -> p h n", h=ML_H),
                              cols[:, 0, 56:60].unsqueeze(2).to_broadcast([P, ML_H, P]), ALU.mult).then_inc(taken[b], 1)
            for h in range(ML_H):
                t.banks.take()
            for h in range(0, ML_H, 2):
                b = filled(t)
                s4 = seg[:, (h // 2) % 2, :].rearrange("p (j c n) -> p j c n", j=2, c=TT)
                a4 = cols[:, :, 48 + h:50 + h].rearrange("p c j -> p j c").unsqueeze(3).to_broadcast([P, 2, TT, P])
                dve.tensor_tensor(s4, bank_of(b).rearrange("p (j c n) -> p j c n", j=2, c=TT), a4, ALU.add)\
                    .then_inc(taken[b], 1)
                dve.wait_ge(taken[b], t.banks.uses[b])
                s3 = seg[:, (h // 2) % 2, :].rearrange("p (k n) -> p k n", n=P)
                dve.tensor_tensor(s3, s3, caus.unsqueeze(1).to_broadcast([P, 4, P]), ALU.add).then_inc(to_act, 1)
                b = filled(t)
                dve.wait_ge(to_dve, t.see(to_dve))
                dve.tensor_tensor(wT[:, h:h + 2, :].rearrange("p j n -> p (j n)"), bank_of(b),
                                  seg[:, (h // 2) % 2, :], ALU.mult).then_inc(taken[b], 1)
            b = filled(t)
            dve.tensor_tensor(qw[:, :, :], bank_of(b).rearrange("p (h n) -> p h n", h=ML_H), mq[:, :, P:S], ALU.mult)\
                .then_inc(taken[b], 1)
            for _ in range(8):
                t.banks.take()
            all_taken(t)
            den = hm[:, :, :, ML_V:ML_VA].rearrange("p c h o -> p c (h o)")
            d0 = hden[:, 0, :].rearrange("p (c h) -> p c h", c=TT)
            t.link(dve.scalar_tensor_tensor(d0, den, -1.0, den, ALU.mult, ALU.max))
            t.link(dve.tensor_tensor(d0, d0, cols[:, :, 52:56], ALU.max))
            t.link(dve.reciprocal(hden[:, 1, :], hden[:, 0, :]))
            h4 = xd[:, :, :].rearrange("p c (h d) -> p c h d", h=ML_H)
            t.link(dve.tensor_tensor(h4, hm[:, :, :, 0:ML_V], hden[:, 1, :].rearrange("p (c h) -> p c h", c=TT)
                                     .unsqueeze(3).to_broadcast([P, TT, ML_H, ML_V]), ALU.mult))
            rms_vector(t, xd[:, :, :].rearrange("p a (g d) -> p (a g) d", g=ML_H), 8, 256)
            t.link(dve.tensor_tensor(xd[:, :, :], xd[:, :, :], og[:, :, :], ALU.mult))
            split_flip_vector(t, yT[:, :, 0:8, :], 8, gain_col(G_SSD))
            split_flip_vector(t, yT[:, :, 8:16, :], 8, gain_col(G_ML))
            down_vector(t, 16)
            add_to_x(t, 1.0)

        def sparse_sync(t):
            for i, w in enumerate(SA_W):
                load_cols(t, A["sa_w_in"][0], i * COLS, w)
            for r in range(0, 8, 2):
                load_rows(t, A["sa_w_out"][0], r)

        def sparse_tensor(t):
            pe = t.e
            project_tensor(t, SA_W, hT_k=hT_waits(t))
            all_taken(t)
            flip_tensor(t, lambda k, a: sa[:, a, SA_QI + k * P:SA_QI + (k + 1) * P], 4)
            flip_tensor(t, lambda k, a: sa_kd[:, a, 1, :], 1)
            all_taken(t)
            for h in range(SA_IH):
                b = claim(t)
                r = 64 * (h % 2)
                for a in range(TT):
                    mm = pe.matmul(bank[:, b, a * S:(a + 1) * S], sa_qiT[r:r + 64, h // 2, a * P:(a + 1) * P],
                                   sa_kiT[r:r + 64, 0, :], start=True, stop=True)
                mm.then_inc(full[b], 1)
            flip_tensor(t, lambda k, a: sa[:, a, k * P:(k + 1) * P], 8)
            flip_tensor(t, lambda k, a: sa_kd[:, a, 0, :], 1)
            lo = lambda h: 64 * (h % 2)
            attend_tensor(t, SA_H, lambda h, a: [(sa_qT[lo(h):lo(h) + 64, h // 2, a * P:(a + 1) * P],
                                                  sa_kT[lo(h):lo(h) + 64, 0, :])],
                          lambda h, st: sa[:, st, SA_V:SA_V + SA_D], 64, lo)
            all_taken(t)
            down_tensor(t, hT, 8)

        def pair_of(dst):
            def at(h):
                r = 64 * (h % 2)
                return lambda part: dst[r:r + 64, part, h // 2, :], r, 64
            return at

        def head_views(ap, at, heads, d=64):
            v = ap[:, :, at:at + heads * d].rearrange("p a (h d) -> p a h d", d=d)
            return v

        def sparse_scalar(t):
            project_scalar(t, [sa[:, :, i * COLS:i * COLS + w] for i, w in enumerate(SA_W)])
            flip_scalar(t, sa_qiT, 4)
            flip_scalar(t, sa_kiT, 1)
            for h in range(SA_IH):
                t.banks.take()
            rms_scalar(t, head_views(sa, 0, SA_H), TT * SA_H, 64)
            rms_scalar(t, sa[:, :, SA_K:SA_K + 64], TT, 64)
            flip_scalar(t, sa_qT, 8)
            flip_scalar(t, sa_kT, 1)
            attend_scalar(t, SA_H, pair_of(hT))
            down_scalar(t, 8)

        def sparse_vector(t):
            dve = t.e
            cos, sin = rope1[:, 0, :, :], rope1[:, 1, :, :]
            project_vector(t, 7)
            all_taken(t)
            for at, n in ((SA_QI, SA_IH), (SA_KI, 1)):
                v = head_views(sa, at, n)
                rotate(t, v[:, :, :, 0:32], v[:, :, :, 32:64], cos, sin, n, sa_rt)
            t.link(dve.tensor_scalar(sa[:, :, SA_WI:SA_WI + SA_IH], sa[:, :, SA_WI:SA_WI + SA_IH],
                                     float(SA_IH) ** -0.5 * float(SA_D) ** -0.5, None, ALU.mult))
            dve.tensor_copy(sa_kd[:, :, 1, 0:64], sa[:, :, SA_KI:SA_KI + 64])
            t.link(dve.tensor_copy(sa_kd[:, :, 1, 64:128], sa[:, :, SA_KI:SA_KI + 64]))
            flip_vector(t, sa_qiT, 4)
            flip_vector(t, sa_kiT, 1)
            for h in range(SA_IH):
                b = filled(t)
                dst = sa_sc if h == 0 else sa_tmp
                wi = sa[:, :, SA_WI + h:SA_WI + h + 1].to_broadcast([P, TT, S])
                dve.scalar_tensor_tensor(dst[:, :, :], halves(b), 0.0, wi, ALU.max, ALU.mult).then_inc(taken[b], 1)
                dve.wait_ge(taken[b], t.banks.uses[b])
                if h:
                    t.link(dve.tensor_tensor(sa_sc[:, :, :], sa_sc[:, :, :], sa_tmp[:, :, :], ALU.add))
            caus = const[:, C_CAUS:C_CAUS + TT * S].rearrange("p (a s) -> p a s", a=TT)
            t.link(dve.tensor_tensor(sa_sc[:, :, :], sa_sc[:, :, :], caus, ALU.add))
            for a in range(TT):
                for _ in range(TOPK // 8):
                    t.link(dve.max(sa_m8[:, :], sa_sc[:, a, :]))
                    t.link(dve.match_replace(sa_sc[:, a, :], sa_m8[:, :], sa_sc[:, a, :], TAKEN_KEY))
            t.link(dve.tensor_scalar(sa_bias[:, :, :], sa_sc[:, :, :], 0.5 * TAKEN_KEY, NEG, ALU.is_gt, ALU.mult))
            t.link(dve.tensor_tensor(sa_bias[:, :, :], sa_bias[:, :, :], caus, ALU.add))
            for at, n, g in ((0, SA_H, R_SAQ), (SA_K, 1, R_SAK)):
                v = head_views(sa, at, n)
                if n > 1:
                    rms_vector(t, v, TT * n, 64)
                else:
                    rms_vector(t, sa[:, :, at:at + 64], TT, 64)
                t.link(dve.tensor_tensor(v, v, rows[:, g:g + 64].unsqueeze(1).unsqueeze(1).to_broadcast([P, TT, n, 64]),
                                         ALU.mult))
                rotate(t, v[:, :, :, 0:32], v[:, :, :, 32:64], cos, sin, n, sa_rt)
            dve.tensor_copy(sa_kd[:, :, 0, 0:64], sa[:, :, SA_K:SA_K + 64])
            t.link(dve.tensor_copy(sa_kd[:, :, 0, 64:128], sa[:, :, SA_K:SA_K + 64]))
            flip_vector(t, sa_qT, 8)
            flip_vector(t, sa_kT, 1)
            attend_vector(t, SA_H, float(SA_D) ** -0.5, lambda h: sa_bias[:, :, :], pair_of(hT))
            down_vector(t, 8)
            add_to_x(t, 1.0)

        def triple_sync(t, l):
            def load_gates(n):
                for i in range(4):
                    load_cols(t, A["w_in_2"][l], Z_GT + n * D + i * COLS)

            for i, w in enumerate(Z_W):
                load_cols(t, A["w_in_2"][l], i * COLS, w)
            load_gates(0)
            for r in (0, 2):
                load_rows(t, A["w_br_na_2"][l], r)
            load_gates(1)
            for r in (0, 2):
                load_rows(t, A["w_br_gla_2"][l], r)
            load_rows(t, A["mla_w_uq_2"][l], 0, MLA_H * MLA_QK)
            load_rows(t, A["mla_w_ukv_2"][l], 0)
            load_gates(2)
            for r in (0, 2):
                load_rows(t, A["w_br_mla_2"][l], r)
            for r in range(0, 8, 2):
                load_rows(t, A["w_out_2"][l], r)

        GATE_STEPS = {NA_H: (1, 3, 5, 7), MLA_H: (1, 2, 3, 4)}

        def gate_tensor(t, steps):
            return lambda i: project_tensor(t, [COLS]) if i in steps else None

        def gate_scalar(t, steps):
            return lambda i: gate_quarter(t, steps.index(i)) if i in steps else None

        def gate_quarter(t, n):
            project_scalar(t, [gt[:, :, n * COLS:(n + 1) * COLS]], scale=-1.0, func=ACT.Exp)

        def gate_vector(t, steps):
            return lambda i: project_vector(t, 1) if i in steps else None

        def na_tensor(t, l):
            flip_tensor(t, lambda k, a: z[:, a, Z_NQ + k * P:Z_NQ + (k + 1) * P], 4, order=reverse)
            flip_tensor(t, lambda k, a: z[:, a, Z_NK + k * P:Z_NK + (k + 1) * P], 4)
            lo = lambda h: 64 * (h % 2)
            attend_tensor(t, NA_H, lambda h, a: [(na_qT[lo(h):lo(h) + 64, h // 2, a * P:(a + 1) * P],
                                                  na_kT[lo(h):lo(h) + 64, h // 2, :])],
                          lambda h, st: z[:, st, Z_NV + h * 64:Z_NV + (h + 1) * 64], 64, lo, order=reverse,
                          fill=gate_tensor(t, GATE_STEPS[NA_H]))
            all_taken(t)
            down_tensor(t, brT, 4)

        def na_scalar(t, l):
            for at in (Z_NQ, Z_NK):
                rms_scalar(t, head_views(z, at, NA_H), TT * NA_H, 64)
            flip_scalar(t, na_qT, 4)
            flip_scalar(t, na_kT, 4)
            attend_scalar(t, NA_H, pair_of(brT), gate_scalar(t, GATE_STEPS[NA_H]))
            down_scalar(t, 4)

        def na_vector(t, l):
            dve = t.e
            for at, g in ((Z_NQ, R_NAQ), (Z_NK, R_NAK)):
                v = head_views(z, at, NA_H)
                rms_vector(t, v, TT * NA_H, 64)
                t.link(dve.tensor_tensor(v, v, rows[:, g + 64 * l:g + 64 * (l + 1)].unsqueeze(1).unsqueeze(1)
                                         .to_broadcast([P, TT, NA_H, 64]), ALU.mult))
            flip_vector(t, na_qT, 4)
            flip_vector(t, na_kT, 4)
            dve.wait_ge(bias_ready, l + 1)
            attend_vector(t, NA_H, 0.125, lambda h: na_bias[:, h, :, :], pair_of(brT), gate_vector(t, GATE_STEPS[NA_H]))
            branch_vector(t, 0)

        def branch_vector(t, n):
            dve = t.e
            t.link(dve.tensor_scalar(gt[:, :, :], gt[:, :, :], 1.0, None, ALU.add))
            t.link(dve.reciprocal(gt[:, :, :], gt[:, :, :]))
            down_vector(t, 4)
            dve.wait_ge(acc_full, t.see(acc_full))
            dst = gt if n else mix
            t.link(dve.tensor_tensor(dst[:, 0, :], acc2()[:, 0, :], gt[:, 0, :], ALU.mult))
            next_lo(t)
            dve.wait_ge(piece_done, through(t))
            t.done(dve.tensor_tensor(dst[:, 1, :], acc2()[:, 1, :], gt[:, 1, :], ALU.mult), acc_taken)
            if n:
                t.link(dve.tensor_tensor(mix[:, :, :], mix[:, :, :], gt[:, :, :], ALU.add))

        def gla_tensor(t, l):
            pe = t.e
            b = claim(t)
            for d in range(2):
                for a in range(TT):
                    mm = pe.transpose(bank[0:16, b, d * S + a * P:d * S + (a + 1) * P],
                                      z[:, a, Z_GL + 16 * d:Z_GL + 16 * d + 16], ident)
            mm.then_inc(full[b], 1)
            flip_tensor(t, lambda k, a: z[:, a, Z_GQ + k * P:Z_GQ + (k + 1) * P], 2)
            flip_tensor(t, lambda k, a: z[:, a, Z_GK + k * P:Z_GK + (k + 1) * P], 2)
            all_taken(t)
            for d in range(2):
                b = claim(t)
                for a in range(TT):
                    mm = pe.matmul(bank[:, b, a * 256:(a + 1) * 256], glT[:, d, a * P:(a + 1) * P],
                                   gate_up[:, l, d, :], start=True, stop=True)
                mm.then_inc(full[b], 1)
            project_tensor(t, [COLS] * 2)
            pe.wait_ge(dve_operand, t.see(dve_operand))
            for d, incl, rest in ((0, C_LE, C_GT), (1, C_GE, C_LT)):
                b = claim(t)
                for j in range(2):
                    for a in range(TT):
                        mm = pe.matmul(bank[:, b, j * S + a * P:j * S + (a + 1) * P], gg[:, d, a, j * P:(j + 1) * P],
                                       const[:, incl:incl + P], start=True, stop=True)
                mm.then_inc(full[b], 1)
                b = claim(t)
                for a in range(TT):
                    mm = pe.matmul(bank[:, b, a * 256:(a + 1) * 256], const[:, rest:rest + P], gg[:, d, a, :],
                                   start=True, stop=True)
                mm.then_inc(full[b], 1)
            project_tensor(t, [COLS] * 2)
            pe.wait_ge(dve_operand, t.see(dve_operand))
            for h in range(GLA_H):
                b = claim(t)
                r, j = 64 * (h % 2), h // 2
                for d in range(2):
                    for a in range(TT):
                        o = (d * TT + a) * P
                        mm = pe.matmul(bank[:, b, o:o + P], em[r:r + 64, d, j, a * P:(a + 1) * P],
                                       ep[r:r + 64, d, j, a * P:(a + 1) * P], start=True, stop=True)
                mm.then_inc(full[b], 1)
            for d in range(2):
                for half in range(2):
                    b = claim(t)
                    r = 64 * half
                    for n in range(3):
                        c = n if d == 0 else 3 - n
                        if c % 2 != half:
                            continue
                        for h in range(GLA_H):
                            o = (h // 2 * 2 + n // 2) * P
                            mm = pe.matmul(bank[64 * (h % 2):64 * (h % 2) + 64, b, o:o + P],
                                           ke[r:r + 64, d, c // 2, h * 64:(h + 1) * 64],
                                           z[r:r + 64, c // 2, Z_GV + h * P:Z_GV + (h + 1) * P], start=True, stop=True)
                    mm.then_inc(full[b], 1)
            pe.wait_ge(dve_operand, t.see(dve_operand))
            for parity in range(2):
                b = claim(t)
                r = 64 * parity
                for j in range(2):
                    h = 2 * j + parity
                    for a in range(TT):
                        o = (j * TT + a) * P
                        pe.matmul(bank[:, b, o:o + P], a_in[:, h, a, :], z[:, a, Z_GV + h * P:Z_GV + (h + 1) * P],
                                  start=True, stop=False, skip_group_check=True)
                        for c in (2 * a, 2 * a + 1):
                            for d in range(2):
                                n = c - 1 if d == 0 else 2 - c
                                if n < 0:
                                    continue
                                mm = pe.matmul(bank[64 * (c % 2):64 * (c % 2) + 64, b, o:o + P],
                                               ep[r:r + 64, d, j, c * 64:(c + 1) * 64], gst[r:r + 64, d, j, n, :],
                                               start=False, stop=False, skip_group_check=True)
                mm.then_inc(full[b], 1)
            flip_tensor(t, lambda k, a: go[:, a, k, :], 4)
            all_taken(t)
            down_tensor(t, brT, 4)

        def gla_scalar(t, l):
            act = t.e
            b = filled(t)
            act.activation(glT[:, :, :], bank[0:16, b, :].rearrange("p (d s) -> p d s", d=2), ACT.Copy)\
                .then_inc(taken[b], 1)
            flip_scalar(t, gqT, 2, float(GLA_DK) ** -0.5)
            flip_scalar(t, gkT, 2)
            t.banks.take(), t.banks.take()
            act.wait_ge(to_act, t.see(to_act))
            t.link(act.activation(ge[:, :, :, :], ge[:, :, :, :], ACT.Exp))
            act.activation(ge[:, :, :, :], ge[:, :, :, :], ACT.Ln, bias=1.0).then_inc(to_dve, 1)
            gate_quarter(t, 0)
            gate_quarter(t, 1)
            tau = 1.0 / 16.0
            for d in range(2):
                b = filled(t)
                act.activation(ep[:, d, :, :], bank_of(b).rearrange("p (j s) -> p j s", j=2), ACT.Exp, scale=tau)
                act.activation(em[:, d, :, :], bank_of(b).rearrange("p (j s) -> p j s", j=2), ACT.Exp, scale=-tau)\
                    .then_inc(taken[b], 1)
                b = filled(t)
                act.activation(ke[:, d, :, :], bank_of(b).rearrange("p (a n) -> p a n", a=TT), ACT.Exp, scale=tau)\
                    .then_inc(taken[b], 1)
            gate_quarter(t, 2)
            gate_quarter(t, 3)
            for _ in range(8):
                t.banks.take()
            for parity in range(2):
                b = filled(t)
                act.activation(go[:, :, parity::2, :].rearrange("p a j v -> p j a v"),
                               bank_of(b).rearrange("p (j a v) -> p j a v", j=2, a=TT), ACT.Copy).then_inc(taken[b], 1)
            rms_scalar(t, go[:, :, :, :].rearrange("p a h v -> p (a h) v"), TT * GLA_H, P)
            split_flip_scalar(t, brT, 4, lambda k: gain[:, G_GLA + l:G_GLA + l + 1])
            down_scalar(t, 4)

        def gla_vector(t, l):
            dve = t.e
            t.banks.take()
            flip_vector(t, gqT, 2, float(GLA_DK) ** -0.5)
            flip_vector(t, gkT, 2)
            for d in range(2):
                b = filled(t)
                bias = rows[:, R_GB + (2 * l + d) * 256:R_GB + (2 * l + d + 1) * 256]
                dve.tensor_tensor(gg[:, d, :, :], bank_of(b).rearrange("p (a n) -> p a n", a=TT),
                                  bias.unsqueeze(1).to_broadcast([P, TT, 256]), ALU.add).then_inc(taken[b], 1)
                dve.wait_ge(taken[b], t.banks.uses[b])
            g3, e3 = z[:, :, 0:512], z[:, :, 512:1024]
            dve.scalar_tensor_tensor(e3, g3, -1.0, g3, ALU.mult, ALU.min)\
                .then_inc(to_act, 1)
            dve.wait_ge(to_dve, t.see(to_dve))
            t.done(dve.scalar_tensor_tensor(g3, g3, 0.0, e3, ALU.min, ALU.subtract), dve_operand)
            project_vector(t, 2)
            for _ in range(4):
                t.banks.take()
            all_taken(t)
            project_vector(t, 2)
            t.link(dve.tensor_copy(gdec[:, 0, :, :], ep[:, 0, :, :].rearrange("p j (c n) -> p j c n", n=64)[:, :, :, 63]))
            t.link(dve.tensor_copy(gdec[:, 1, :, :], ep[:, 1, :, :].rearrange("p j (c n) -> p j c n", n=64)[:, :, :, 0]))
            for d in range(2):
                dve.tensor_tensor(ep[:, d, :, :], ep[:, d, :, :], gqT[:, :, :], ALU.mult)
                dve.tensor_tensor(em[:, d, :, :], em[:, d, :, :], gkT[:, :, :], ALU.mult)
                ins = dve.tensor_tensor(ke[:, d, :, :], ke[:, d, :, :], z[:, :, Z_GK:Z_GK + 256], ALU.mult)
            t.done(ins, dve_operand)
            masks = const[:, C_LE:C_LE + 2 * P].rearrange("p (d n) -> p d n", d=2)
            for h in range(GLA_H):
                b = filled(t)
                dve.tensor_tensor(am[:, :, :, :], bank_of(b).rearrange("p (d a n) -> p d a n", d=2, a=TT),
                                  masks.unsqueeze(2).to_broadcast([P, 2, TT, P]), ALU.mult).then_inc(taken[b], 1)
                dve.wait_ge(taken[b], t.banks.uses[b])
                t.link(dve.tensor_tensor(a_in[:, h, :, :], am[:, 0, :, :], am[:, 1, :, :], ALU.add))
            for d in range(2):
                of_half = [filled(t), filled(t)]
                for n in range(3):
                    c = n if d == 0 else 3 - n
                    for j in range(2):
                        o = (2 * j + n // 2) * P
                        added = bank[:, of_half[c % 2], o:o + P]
                        if n == 0:
                            ins = dve.tensor_copy(gst[:, d, j, 0, :], added)
                        else:
                            ins = dve.scalar_tensor_tensor(gst[:, d, j, n, :], gst[:, d, j, n - 1, :],
                                                           gdec[:, d, j, c:c + 1], added, ALU.mult, ALU.add)
                    if n < 2:
                        t.link(ins)
                ins.then_inc(taken[of_half[c % 2]], 1)
                dve.wait_ge(taken[of_half[c % 2]], t.banks.uses[of_half[c % 2]])
                dve.sem_inc(taken[of_half[1 - c % 2]], 1)
            dve.sem_inc(dve_operand, 1)
            t.banks.take(), t.banks.take()
            all_taken(t)
            rms_vector(t, go[:, :, :, :].rearrange("p a h v -> p (a h) v"), TT * GLA_H, P)
            t.link(dve.tensor_tensor(go[:, :, :, :].rearrange("p a h v -> p a (h v)"),
                                     go[:, :, :, :].rearrange("p a h v -> p a (h v)"),
                                     z[:, :, Z_GR:Z_GR + 512], ALU.mult))
            split_flip_vector(t, brT, 4, lambda k: gain[:, G_GLA + l:G_GLA + l + 1])
            branch_vector(t, 1)

        def mla_tensor(t, l):
            pe = t.e
            flip_tensor(t, lambda k, a: z[:, a, Z_CQ + k * P:Z_CQ + (k + 1) * P], 2)
            flip_tensor(t, lambda k, a: z[:, a, Z_CKV + k * P:Z_CKV + (k + 1) * P], 2)
            all_taken(t)
            for i, n in enumerate((3, 4)):
                s = arrived(t)
                for c in range(n):
                    b = claim(t, by_piece=(c == n - 1))
                    for a in range(TT):
                        for k in range(2):
                            for p, q in PASSES:
                                mm = pe.matmul(bank[:, b, a * 256:(a + 1) * 256], cT[:, i, p, k, a * P:(a + 1) * P],
                                               slot_rows(s, q, n * 256)[:, k, c * 256:(c + 1) * 256],
                                               start=(k == 0 and p + q == 0), stop=(k == 1 and p == 1))
                    mm.then_inc(piece_done if c == n - 1 else full[b], 1)
            flip_tensor(t, lambda h, a: lq[:, a, h, 0:P], 4)
            flip_tensor(t, lambda h, a: lq[:, a, h, P:MLA_QK], 4, 64)
            flip_tensor(t, lambda h, a: lk[:, a, h, 0:P], 4)
            flip_tensor(t, lambda h, a: lk[:, a, h, P:MLA_QK], 4, 64)
            attend_tensor(t, MLA_H, lambda h, a: [(lqT[:, h, a * P:(a + 1) * P], lkT[:, h, :]),
                                                  (lqrT[:, h, a * P:(a + 1) * P], lkrT[:, h, :])],
                          lambda h, st: lkv[:, st, h, P:2 * P], P, lambda h: 0,
                          fill=gate_tensor(t, GATE_STEPS[MLA_H]))
            all_taken(t)
            down_tensor(t, brT, 4)

        def mla_scalar(t, l):
            act = t.e
            for at in (Z_CQ, Z_CKV):
                rms_scalar(t, z[:, :, at:at + 256], TT, 256)
            split_flip_scalar(t, cT[:, 0], 2, gain_col(G_CQ + 2 * l))
            split_flip_scalar(t, cT[:, 1], 2, gain_col(G_CKV + 2 * l))
            qf = lq[:, :, :, :].rearrange("p a h d -> p a (h d)")
            kf = lkv[:, :, :, :].rearrange("p a h d -> p a (h d)")
            for n, dst in ((3, qf), (4, kf)):
                for c in range(n):
                    if c == n - 1:
                        b = t.banks.take(by_piece=True)
                        next_hi(t)
                        act.wait_ge(piece_done, through(t))
                    else:
                        b = filled(t)
                    act.activation(dst[:, :, c * 256:(c + 1) * 256], halves(b), ACT.Copy).then_inc(taken[b], 1)
            rms_scalar(t, lq, TT * MLA_H, MLA_QK)
            rms_scalar(t, lk, TT * MLA_H, MLA_QK)
            flip_scalar(t, lqT, 4)
            flip_scalar(t, lqrT, 4, None, 64)
            flip_scalar(t, lkT, 4)
            flip_scalar(t, lkrT, 4, None, 64)
            attend_scalar(t, MLA_H, lambda h: (lambda part: brT[:, part, h, :], 0, P), gate_scalar(t, GATE_STEPS[MLA_H]))
            down_scalar(t, 4)

        def mla_vector(t, l):
            dve = t.e
            for at in (Z_CQ, Z_CKV):
                rms_vector(t, z[:, :, at:at + 256], TT, 256)
            split_flip_vector(t, cT[:, 0], 2, gain_col(G_CQ + 2 * l))
            split_flip_vector(t, cT[:, 1], 2, gain_col(G_CKV + 2 * l))
            for n in (3, 4):
                for c in range(n):
                    t.banks.take(by_piece=(c == n - 1))
                next_lo(t)
            all_taken(t)
            dve.tensor_copy(lk[:, :, :, 0:P], lkv[:, :, :, 0:P])
            t.link(dve.tensor_copy(lk[:, :, :, P:MLA_QK],
                                   z[:, :, Z_KR:Z_KR + 64].unsqueeze(2).to_broadcast([P, TT, MLA_H, 64])))
            cos = const[:, C_COS:C_COS + 64].rearrange("p (a c) -> p a c", a=TT)
            sin = const[:, C_SIN:C_SIN + 64].rearrange("p (a c) -> p a c", a=TT)
            for v, g in ((lq, R_MQ), (lk, R_MK)):
                rms_vector(t, v, TT * MLA_H, MLA_QK)
                w = rows[:, g + MLA_QK * l:g + MLA_QK * (l + 1)]
                t.link(dve.tensor_tensor(v, v, w.unsqueeze(1).unsqueeze(1).to_broadcast([P, TT, MLA_H, MLA_QK]), ALU.mult))
                rotate(t, v[:, :, :, P:P + 32], v[:, :, :, P + 32:P + 64], cos, sin, MLA_H, z_rt)
            flip_vector(t, lqT, 4)
            flip_vector(t, lqrT, 4, None, 64)
            flip_vector(t, lkT, 4)
            flip_vector(t, lkrT, 4, None, 64)
            attend_vector(t, MLA_H, float(MLA_QK) ** -0.5, None, lambda h: (lambda part: brT[:, part, h, :], 0, P),
                          gate_vector(t, GATE_STEPS[MLA_H]))
            branch_vector(t, 2)

        def triple_tensor(t, l):
            project_tensor(t, Z_W, hT_k=hT_waits(t))
            all_taken(t)
            na_tensor(t, l)
            gla_tensor(t, l)
            mla_tensor(t, l)
            flip_tensor(t, lambda k, a: mix[:, a, k * P:(k + 1) * P], KD)
            all_taken(t)
            down_tensor(t, hT, KD)

        def triple_scalar(t, l):
            project_scalar(t, [z[:, :, i * COLS:i * COLS + w] for i, w in enumerate(Z_W)])
            for b in range(4):
                t.e.wait_ge(taken[b], t.banks.uses[b])
            t.link(t.e.activation(z[:, :, Z_GR:Z_GR + 512], z[:, :, Z_GR:Z_GR + 512], ACT.Silu))
            t.e.sem_inc(to_dve, 1)
            na_scalar(t, l)
            gla_scalar(t, l)
            mla_scalar(t, l)
            split_flip_scalar(t, hT, KD)
            down_scalar(t, KD)

        def triple_vector(t, l):
            project_vector(t, len(Z_W))
            all_taken(t)
            t.e.wait_ge(to_dve, t.see(to_dve))
            na_vector(t, l)
            gla_vector(t, l)
            mla_vector(t, l)
            split_flip_vector(t, hT, KD)
            down_vector(t, KD)
            add_to_x(t, 1.0)

        FFNS = [(A["ffn_w_gate"][l, i], A["ffn_w_up"][l, i], A["ffn_w_down"][l, i], G_FFN + 8 * (2 * l + i))
                for l in range(DEPTH) for i in range(2)]
        for l in range(DEPTH):
            FFNS.append((A["ffn1_w1_2"][l], A["ffn1_w3_2"][l], A["ffn1_w2_2"][l], G_FFN1 + 8 * l))
            FFNS.append((A["ffn2_w1_2"][l], A["ffn2_w3_2"][l], A["ffn2_w2_2"][l], G_FFN2 + 8 * l))
        MIXERS = [(G_MIX, hybrid_sync, hybrid_tensor, hybrid_scalar, hybrid_vector, ()),
                  (G_MIX + 8, sparse_sync, sparse_tensor, sparse_scalar, sparse_vector, ())]
        MIXERS += [(G_MIX2 + 8 * l, triple_sync, triple_tensor, triple_scalar, triple_vector, (l,))
                   for l in range(DEPTH)]

        def flip_gains_scalar(t):
            b = filled(t)
            t.e.activation(gain[:, :], bank[:, b, 0:N_GA + N_GB], ACT.Copy).then_inc(taken[b], 1)
            t.e.wait_ge(taken[b], t.banks.uses[b])

        block = ctx.enter_context(nc.Block())

        @block.sync
        def _(sp):
            t = Thread(sp, steps["sp"])
            for n in range(4):
                ffn_sync(t, *FFNS[2 * n][:3])
                MIXERS[n][1](t, *MIXERS[n][5])
                ffn_sync(t, *FFNS[2 * n + 1][:3])
            sp.wait_ge(x_final, 1)
            sp.dma_start(out[0].rearrange("(a p) d -> p a d", p=P), x[:, :, :]).then_inc(out_done, 16)
            sp.wait_ge(out_done, 16)

        smalls = []

        def small(dst, src):
            smalls.append((dst, src))

        small(x[:, :, :], A["x"][0].rearrange("(a p) d -> p a d", p=P))
        small(const[:, :], A["constants"])
        at = 0
        for name in ("ffn_norm", "mix_norm", "ffn1_norm_2", "mix_norm_2", "ffn2_norm_2"):
            v = A[name].rearrange("l i (k p) -> (l i k) p", p=P) if len(A[name].shape) == 3 else \
                A[name].rearrange("l (k p) -> (l k) p", p=P)
            small(gain_rows[at:at + v.shape[0], 0, :], v)
            at += v.shape[0]
        at = 0
        for v in (A["hy_conv_w"][0].rearrange("t (k p) -> (t k) p", p=P),
                  A["hy_conv_b"].rearrange("l (k p) -> (l k) p", p=P),
                  A["hy_ssd_norm"].rearrange("l (k p) -> (l k) p", p=P),
                  A["hy_mlstm_norm"].rearrange("l (k p) -> (l k) p", p=P),
                  A["gla_out_norm_2"],
                  A["mla_cq_norm_2"].rearrange("l (k p) -> (l k) p", p=P),
                  A["mla_ckv_norm_2"].rearrange("l (k p) -> (l k) p", p=P)):
            small(gain_rows[at:at + v.shape[0], 1, :], v)
            at += v.shape[0]
        small(pos_i[:, :], A["positions"][0].rearrange("(a p) -> p a", p=P))
        small(rows[:, R_DSKIP:R_DSKIP + 16], A["hy_d_skip"][0].partition_broadcast(P))
        small(rows[:, R_SAQ:R_SAQ + 64], A["sa_q_norm"][0].partition_broadcast(P))
        small(rows[:, R_SAK:R_SAK + 64], A["sa_k_norm"][0].partition_broadcast(P))
        for l in range(DEPTH):
            small(rows[:, R_NAQ + 64 * l:R_NAQ + 64 * (l + 1)], A["na_q_norm_2"][l].partition_broadcast(P))
            small(rows[:, R_NAK + 64 * l:R_NAK + 64 * (l + 1)], A["na_k_norm_2"][l].partition_broadcast(P))
            small(rows[:, R_MQ + 192 * l:R_MQ + 192 * (l + 1)], A["mla_q_norm_2"][l].partition_broadcast(P))
            small(rows[:, R_MK + 192 * l:R_MK + 192 * (l + 1)], A["mla_k_norm_2"][l].partition_broadcast(P))
            for d, n in enumerate(("gf", "gb")):
                small(rows[:, R_GB + (2 * l + d) * 256:R_GB + (2 * l + d + 1) * 256],
                      A[f"gla_{n}_bias_2"][l].partition_broadcast(P))
                small(gate_up[:, l, d, :], A[f"gla_{n}_up_2"][l])
        small(heads_in[:, 0:1], A["hy_dt_bias"][0].unsqueeze(1))
        small(heads_in[:, 1:2], A["hy_a_log"][0].unsqueeze(1))
        small(heads_in[0:ML_H, 2:3], A["hy_igate_bias"][0].unsqueeze(1))
        small(fg_bias[:, :], A["hy_fgate_bias"][0].unsqueeze(1))
        wg3 = A["hy_w_in"][0].rearrange("(k p) c -> p k c", p=P)
        small(w_gates[:, :, 0:16], wg3[:, :, HY_DT:HY_DT + 16])
        small(w_gates[:, :, 16:24], wg3[:, :, HY_IG:HY_IG + 8])
        ALL_SMALL = 16 * len(smalls)

        @block.scalar
        def _(act):
            t = Thread(act, steps["act"])
            with nc.allow_non_contiguous_dma(reason="one position and one bias per partition"):
                for dst, src in smalls:
                    act.dma_start(dst, src).then_inc(small_in, 16)
            act.wait_ge(small_in, ALL_SMALL)
            for n in range(PARTS):
                split_hi(t, n)
            act.activation(w_gates_s[:, 0, :, :], w_gates[:, :, :], ACT.Copy).then_inc(setup_a, 1)
            act.wait_ge(to_act, t.see(to_act))
            act.activation(rope1[:, 1, :, :].rearrange("p a c -> p (a c)"), rope_t[:, 0, :], ACT.Sin)
            act.activation(rope1[:, 0, :, :].rearrange("p a c -> p (a c)"), rope_t[:, 1, :], ACT.Sin).then_inc(to_dve, 1)
            flip_gains_scalar(t)
            for n in range(4):
                pre_scalar(t, FFNS[2 * n][3])
                ffn_scalar(t, 2 * n)
                pre_scalar(t, MIXERS[n][0])
                MIXERS[n][3](t, *MIXERS[n][5])
                pre_scalar(t, FFNS[2 * n + 1][3])
                ffn_scalar(t, 2 * n + 1)

        @block.gpsimd
        def _(pool):
            t = Thread(pool, steps["pool"])
            pool.wait_ge(small_in, ALL_SMALL)
            win = const[:, C_WIN:C_WIN + GRID_W]
            for l in range(DEPTH):
                pool.wait_ge(bias_room, l + 1)
                rpb = A["na_rpb_2"]
                for a in range(TT):
                    for half in range(2):
                        for r in range(ROWS):
                            row = r - (2 * a + half) + WIN_R - 1
                            src = bass.AP(tensor=rpb.tensor,
                                          offset=(l * NA_H * RPB_R + row) * RPB_C + WIN_C - GRID_W,
                                          ap=[[1, GRID_W], [RPB_R * RPB_C, NA_H], [1, GRID_W]])
                            dst = na_bias[half * 64:(half + 1) * 64, :, a, r * GRID_W:(r + 1) * GRID_W]
                            pool.dma_start(dst, src).then_inc(bias_in, 16)
                pool.wait_ge(bias_in, 16 * 4 * ROWS * (l + 1))
                for h in range(NA_H):
                    v = na_bias[:, h, :, :].rearrange("p a (r c) -> p (a r) c", c=GRID_W)
                    t.link(pool.tensor_tensor(v, v, win.unsqueeze(1).to_broadcast([P, TT * ROWS, GRID_W]), ALU.add))
                pool.sem_inc(bias_ready, 1)

        @block.vector
        def _(dve):
            t = Thread(dve, steps["dve"])
            dve.sem_inc(lo_ready, RAW)
            dve.memset(zeros[:, :], 0.0)
            t.done(dve.memset(ones[:, :], 1.0), setup_v)
            dve.wait_ge(small_in, ALL_SMALL)
            dve.sem_inc(norm_src, 2)
            t.see(norm_src, 2)
            for n in range(PARTS):
                split_lo(t, n)
            dve.wait_ge(setup_a, 1)
            dve.tensor_tensor(w_gates_s[:, 1, :, :], w_gates[:, :, :], w_gates_s[:, 0, :, :].bitcast(F32), ALU.subtract)
            two_pi = 2 * np.pi
            t.link(dve.tensor_copy(pos_f[:, :], pos_i[:, :]))
            inv = const[:, C_INV:C_INV + 32]
            ang, n = rope_t[:, 0, :], rope_t[:, 2, :]
            for a in range(TT):
                t.link(dve.tensor_scalar(rope_t[:, 0, a * 32:(a + 1) * 32], inv, pos_f[:, a:a + 1], None, ALU.mult))
            magic = 1.5 * 2.0 ** 23
            t.link(dve.tensor_scalar(n, ang, 1.0 / two_pi, magic, ALU.mult, ALU.add))
            t.link(dve.tensor_scalar(n, n, magic, None, ALU.subtract))
            c1 = 6.28125
            c2 = float(np.float32(np.floor((two_pi - c1) * 2 ** 24) / 2 ** 24))
            c3 = two_pi - c1 - c2
            for c in (c1, c2, c3):
                t.link(dve.scalar_tensor_tensor(ang, n, -c, ang, ALU.mult, ALU.add))
            t.link(dve.tensor_scalar(rope_t[:, 1, :], ang, np.pi / 2, -two_pi, ALU.is_gt, ALU.mult))
            t.link(dve.scalar_tensor_tensor(rope_t[:, 1, :], ang, np.pi / 2, rope_t[:, 1, :], ALU.add, ALU.add))
            pi_in = 3.1415925
            t.link(dve.tensor_scalar(rope_t[:, 0:2, :], rope_t[:, 0:2, :], pi_in, -pi_in, ALU.min, ALU.max))
            dve.sem_inc(to_act, 1)
            dve.wait_ge(to_dve, t.see(to_dve))
            t.banks.take()
            all_taken(t)
            for n in range(4):
                pre_vector(t, FFNS[2 * n][3])
                ffn_vector(t, 2 * n)
                pre_vector(t, MIXERS[n][0])
                MIXERS[n][4](t, *MIXERS[n][5])
                if n in (1, 2):
                    dve.sem_inc(bias_room, 1)
                pre_vector(t, FFNS[2 * n + 1][3])
                ffn_vector(t, 2 * n + 1)
            dve.sem_inc(x_final, 1)

        @block.tensor
        def _(pe):
            t = Thread(pe, steps["pe"])
            t.acc_uses = 0
            pe.sem_inc(piece_done, PARTS)
            pe.wait_ge(setup_v, 1)
            pe.wait_ge(small_in, ALL_SMALL)
            b = claim(t)
            pe.transpose(bank[:, b, 0:N_GA], gain_rows[0:N_GA, 0, :], const[0:N_GA, C_ID:C_ID + N_GA])
            pe.transpose(bank[:, b, N_GA:N_GA + N_GB], gain_rows[0:N_GB, 1, :], const[0:N_GB, C_ID:C_ID + N_GB])\
                .then_inc(full[b], 1)
            for n in range(4):
                pre_tensor(t, FFNS[2 * n][3])
                ffn_tensor(t, 2 * n)
                pre_tensor(t, MIXERS[n][0])
                MIXERS[n][2](t, *MIXERS[n][5])
                pre_tensor(t, FFNS[2 * n + 1][3])
                ffn_tensor(t, 2 * n + 1)


_INS = ["x", "positions", "ffn_norm", "ffn_w_gate", "ffn_w_up", "ffn_w_down", "mix_norm", "hy_w_in", "hy_conv_w",
        "hy_conv_b", "hy_dt_bias", "hy_a_log", "hy_d_skip", "hy_ssd_norm", "hy_igate_bias", "hy_fgate_bias",
        "hy_mlstm_norm", "hy_w_out", "sa_w_in", "sa_q_norm", "sa_k_norm", "sa_w_out", "ffn1_norm_2", "ffn1_w1_2",
        "ffn1_w3_2", "ffn1_w2_2", "mix_norm_2", "w_in_2", "na_q_norm_2", "na_k_norm_2", "na_rpb_2", "gla_gf_up_2",
        "gla_gf_bias_2", "gla_gb_up_2", "gla_gb_bias_2", "gla_out_norm_2", "mla_cq_norm_2", "mla_ckv_norm_2",
        "mla_w_uq_2", "mla_w_ukv_2", "mla_q_norm_2", "mla_k_norm_2", "w_br_na_2", "w_br_gla_2", "w_br_mla_2",
        "w_out_2", "ffn2_norm_2", "ffn2_w1_2", "ffn2_w3_2", "ffn2_w2_2"]


def kernel(**inputs):
    import concourse.bacc as bacc
    from concourse.bass_utils import run_bass_kernel_spmd

    nc = bacc.Bacc("TRN2", target_bir_lowering=False, num_devices=1)
    arrays, aps = {}, {}
    for name in _INS:
        a = np.ascontiguousarray(inputs[name])
        arrays[f"in_{name}"] = a
        aps[name] = nc.dram_tensor(f"in_{name}", a.shape, mybir.dt.from_np(a.dtype), kind="ExternalInput").ap()
    arrays["in_constants"] = constants()
    aps["constants"] = nc.dram_tensor("in_constants", (P, N_CONST), F32, kind="ExternalInput").ap()
    out = nc.dram_tensor("out_x", (1, S, D), F32, kind="ExternalOutput").ap()
    two_blocks(nc, aps, out)
    r = run_bass_kernel_spmd(nc, [arrays], core_ids=[0])
    return r.results[0]["out_x"]
```

```python
from contextlib import ExitStack

import concourse.bass as bass
import numpy as np
from concourse import mybir

F32 = mybir.dt.float32
F32R = mybir.dt.float32r
BF16 = mybir.dt.bfloat16
I32 = mybir.dt.int32
ALU = mybir.AluOpType
ACT = mybir.ActivationFunctionType
AX = mybir.AxisListType

P = 128
S = 256
TT = S // P
D = 1024
KD = D // P
FF = 2816
DEPTH = 2
EPS = 1e-6
NEG = -1e30
TAKEN_KEY = -3e38

RAW = 3
PARTS = 2
SLOT = 2048
LOOP = 6
COLS = 256
CHUNKS = FF // COLS

SSD_W = 1024
SSD_H = 16
SSD_G = 2
SSD_N = 128
CONV_DIM = SSD_W + 2 * SSD_G * SSD_N
CONV_T = CONV_DIM // P
CONV_K = 4
ML_H = 4
ML_V = 256
ML_VA = ML_V + 1
HY_Z, HY_XBC, HY_DT = 0, SSD_W, SSD_W + CONV_DIM
HY_Q = HY_DT + SSD_H
HY_K = HY_Q + 512
HY_V = HY_K + 512
HY_O = HY_V + 1024
HY_IG = HY_O + 1024
HY_FG = HY_IG + ML_H

SA_H, SA_IH, SA_D = 16, 8, 64
SA_IN = SA_H * SA_D + 2 * SA_D + SA_IH * SA_D + SA_D + SA_IH
SA_K, SA_V, SA_QI = 1024, 1088, 1152
SA_KI, SA_WI = SA_QI + SA_IH * SA_D, SA_QI + SA_IH * SA_D + SA_D
SA_W = [COLS] * 6 + [SA_IN - 6 * COLS]
TOPK = min(256, S // 4)

GRID_W, WIN_R, WIN_C = 64, 8, 16
ROWS = S // GRID_W
NA_H = 8
RPB_R, RPB_C = 2 * WIN_R - 1, 2 * WIN_C - 1
GLA_H, GLA_DK, GLA_DV, GLA_C = 4, 64, 128, 64
MLA_H, MLA_NOPE, MLA_R, MLA_DV = 4, 128, 64, 128
MLA_QK = MLA_NOPE + MLA_R
Z_NQ, Z_NK, Z_NV = 0, 512, 1024
Z_GQ, Z_GK, Z_GV, Z_GR, Z_GL = 1536, 1792, 2048, 2560, 3072
Z_CQ, Z_CKV, Z_KR, Z_GT = 3104, 3360, 3616, 3680
Z_IN = Z_GT
Z_TILES = (12, 13, 14, 10, 11, 0, 1, 2, 3, 4, 5, 6, 7, 8, 9)
Z_W = [min(COLS, Z_IN - i * COLS) for i in Z_TILES]

G_FFN, G_MIX, G_FFN1, G_MIX2, G_FFN2 = 0, 32, 48, 64, 80
G_CW, G_CB, G_SSD, G_ML, G_GLA, G_CQ, G_CKV = 96, 144, 156, 164, 172, 174, 178
N_GA, N_GB = 96, 86

R_DSKIP, R_SAQ, R_SAK, R_NAQ, R_NAK = 0, 16, 80, 144, 272
R_GB, R_MQ, R_MK = 400, 1424, 1808
N_ROW = 2192

C_ID, C_CAUS_T, C_CAUS, C_WIN = 0, 128, 256, 768
C_LE, C_GT, C_GE, C_LT = 832, 960, 1088, 1216
C_INV, C_COS, C_SIN, C_REV = 1344, 1376, 1440, 1504
N_CONST = 1632


FFN_PIECES = [SLOT] * (3 * CHUNKS)
MIXER_PIECES = [[SLOT] * (6 + 4 + 12 + 8), [KD * w for w in SA_W] + [SLOT] * 4]
MIXER_PIECES += [[KD * w for w in Z_W] + [SLOT] * (4 + 2 + 4 + 2) + [2 * MLA_H * MLA_QK, SLOT] + [SLOT] * (4 + 2 + 4)] * 2
PIECES = [n for m in MIXER_PIECES for n in FFN_PIECES + m + FFN_PIECES]


def constants():
    c = np.zeros((P, N_CONST), np.float32)
    i, j = np.arange(P)[:, None], np.arange(P)[None, :]
    c[:, C_ID:C_ID + P] = i == j
    c[:, C_CAUS_T:C_CAUS_T + P] = np.where(i <= j, 0, NEG)
    key = np.arange(S)[None, :]
    for t in range(TT):
        c[:, C_CAUS + t * S:C_CAUS + (t + 1) * S] = np.where(key <= i + t * P, 0, NEG)
    c[:, C_REV:C_REV + P] = (i // GRID_W == j // GRID_W) & (i % GRID_W + j % GRID_W == GRID_W - 1)
    cq, ck = GRID_W - 1 - np.arange(P)[:, None] % GRID_W, np.arange(GRID_W)[None, :]
    c0 = np.clip(cq - WIN_C // 2, 0, GRID_W - WIN_C)
    c[:, C_WIN:C_WIN + GRID_W] = np.where((ck >= c0) & (ck < c0 + WIN_C), 0, NEG)
    same = i // GLA_C == j // GLA_C
    for at, m in ((C_LE, i <= j), (C_GT, i > j), (C_GE, i >= j), (C_LT, i < j)):
        c[:, at:at + P] = same & m
    half = MLA_R // 2
    inv = (np.float32(10000.0) ** (-np.arange(half, dtype=np.float32) / np.float32(half))).astype(np.float32)
    c[:, C_INV:C_INV + half] = inv
    ang = np.arange(S, dtype=np.float32)[:, None] * inv[None, :]
    for t in range(TT):
        c[:, C_COS + t * half:C_COS + (t + 1) * half] = np.cos(ang[t * P:(t + 1) * P])
        c[:, C_SIN + t * half:C_SIN + (t + 1) * half] = np.sin(ang[t * P:(t + 1) * P])
    return c


class Tally:

    def __init__(self):
        self.at = {}

    def __call__(self, sem, n=1):
        self.at[sem.name] = self.at.get(sem.name, 0) + n
        return self.at[sem.name]


class Banks:

    def __init__(self):
        self.next, self.uses, self.filled = 0, [0] * 4, [0] * 4

    def take(self, by_piece=False):
        b = self.next
        self.next = (b + 1) % 4
        self.uses[b] += 1
        self.filled[b] += not by_piece
        return b


class Thread:

    def __init__(self, e, step):
        self.e, self.step = e, step
        self.see, self.banks, self.piece = Tally(), Banks(), 0

    def link(self, ins):
        ins.then_inc(self.step, 1)
        self.e.wait_ge(self.step, self.see(self.step))

    def done(self, ins, sem):
        ins.then_inc(sem, 1)
        self.e.wait_ge(sem, self.see(sem))


def two_blocks(nc, A, out):
    with ExitStack() as ctx:
        def sb(name, shape, dt=F32, where=ctx):
            return where.enter_context(nc.sbuf_tensor(name, shape, dt))

        def sem(name):
            return ctx.enter_context(nc.semaphore(name))

        x = sb("x", [P, TT, D])
        hT = sb("hT", [P, 2, KD, S], F32R)
        raw = sb("raw", [P, RAW, SLOT])
        parts = sb("parts", [P, PARTS, 2, SLOT], F32R)
        silu_gate = sb("silu_gate", [P, 2, 512])
        with ExitStack() as m:
            gated = sb("gated", [P, 2, 2, 512], F32R, where=m)
        with ExitStack() as m:
            cb = sb("cb", [P, SSD_G, TT, P], where=m)
            b_tok = sb("b_tok", [P, SSD_G, P], where=m)
            cst = sb("cst", [P, ML_H, ML_VA], where=m)
        with ExitStack() as m:
            gain_rows = sb("gain_rows", [P, 2, P], where=m)
            rope_t = sb("rope_t", [P, 3, TT * 32], where=m)
            w_gates = sb("w_gates", [P, KD, 24], where=m)
        ctx.enter_context(nc.sbuf_tensor("gated_room", [P, 2048], F32))
        const = sb("const", [P, N_CONST])
        gain = sb("gain", [P, N_GA + N_GB])
        rows = sb("rows", [P, N_ROW])
        heads_in = sb("heads_in", [SSD_H, 4])
        w_gates_s = sb("w_gates_s", [P, 2, KD, 24], F32R)
        gate_up = sb("gate_up", [16, DEPTH, 2, 256])
        zeros = sb("zeros", [P, P], BF16)
        ones = sb("ones", [SSD_H, P])
        pos_i = sb("pos_i", [P, TT], I32)
        pos_f = sb("pos_f", [P, TT])
        rope1 = sb("rope1", [P, 2, TT, 32])
        squares = sb("squares", [P, 2048])
        stat = sb("stat", [P, 4, 32])
        root_diag = squares[:, D:D + TT * P].rearrange("p (a n) -> p a n", a=TT)
        gdec = sb("gdec", [P, 2, 2, 4])
        heads4 = sb("heads4", [ML_H, 1])
        fg_bias = sb("fg_bias", [ML_H, 1])

        with ExitStack() as m:
            xbc = sb("xbc", [P, CONV_T, CONV_K - 1 + S], where=m)
            conv = sb("conv", [P, CONV_T, S], where=m)
            mq = sb("mq", [P, ML_H, S], where=m)
            mk = sb("mk", [P, ML_H, S], where=m)
            mv = sb("mv", [P, TT, ML_H, ML_VA], where=m)
            og = sb("og", [P, TT, 1024], where=m)
            hrow = sb("hrow", [SSD_H, 10, S], where=m)
            gtok = sb("gtok", [P, TT, 24], where=m)
            cols = sb("cols", [P, TT, 64], where=m)
            ecols = sb("ecols", [P, SSD_H], where=m)
            xs = sb("xs", [P, TT, SSD_W], where=m)
            xd = sb("xd", [P, TT, SSD_W], where=m)
            late = sb("late", [P, TT * ML_H * ML_VA], where=m)
            hden = sb("hden", [P, 2, TT * ML_H], where=m)
            zg = late[:, 0:TT * SSD_W].rearrange("p (a c) -> p a c", a=TT)
            hm = late[:, :].rearrange("p (c h v) -> p c h v", c=TT, h=ML_H)
            xde = squares[:, 0:1024]
            state = squares[:, 1024:2048].rearrange("p (g n) -> p g n", g=SSD_G)
            seg = silu_gate
            kw = conv[:, 4:6, :].rearrange("p k (h n) -> p (k h) n", n=P)
            qw = conv[:, 6:8, :].rearrange("p k (h n) -> p (k h) n", n=P)
        with ExitStack() as m:
            wT = sb("wT", [P, SSD_H, S], where=m)
        with ExitStack() as m:
            yT = sb("yT", [P, 2, 16, S], F32R, where=m)
        with ExitStack() as m:
            soft = sb("soft", [P, 3, TT, S], where=m)
            soft_pT = sb("soft_pT", [P, 2, 512], where=m)
            soft_m = sb("soft_m", [P, 2, 2, TT], where=m)
            soft_r = sb("soft_r", [P, 2, TT], where=m)
            with ExitStack() as g:
                sa = sb("sa", [P, TT, SA_IN], where=g)
                sa_kd = sb("sa_kd", [P, TT, 2, P], where=g)
                sa_qT = sb("sa_qT", [P, 8, S], where=g)
                sa_kT = sb("sa_kT", [P, 1, S], where=g)
                sa_qiT = sb("sa_qiT", [P, 4, S], where=g)
                sa_kiT = sb("sa_kiT", [P, 1, S], where=g)
                sa_sc = sb("sa_sc", [P, TT, S], where=g)
                sa_m8 = sb("sa_m8", [P, TT, 8], where=g)
                sa_bias = sb("sa_bias", [P, TT, S], where=g)
                sa_rt = sb("sa_rt", [P, 4, TT, SA_H * 32], where=g)
            z = sb("z", [P, TT, Z_IN], where=m)
            mix = sb("mix", [P, TT, D], where=m)
            gt = sb("gt", [P, TT, D], where=m)
            brT = gated[:, :, :, :].rearrange("p q a (k s) -> p q (a k) s", s=S)
            with ExitStack() as g:
                na_bias = sb("na_bias", [P, NA_H, TT, S], where=g)
                na_qT = sb("na_qT", [P, 4, S], where=g)
                na_kT = silu_gate[:, :, :].rearrange("p a (k s) -> p (a k) s", s=S)
            with ExitStack() as g:
                ep = sb("ep", [P, 2, 2, S], where=g)
                em = sb("em", [P, 2, 2, S], where=g)
                gqT = sb("gqT", [P, 2, S], where=g)
                gkT = sb("gkT", [P, 2, S], where=g)
                gst = sb("gst", [P, 2, 2, 3, P], where=g)
                go = sb("go", [P, TT, GLA_H, P], where=g)
                gg = z[:, :, 0:512].rearrange("p a (d n) -> p d a n", d=2)
                ge = z[:, :, 512:1024].rearrange("p a (d n) -> p d a n", d=2)
                ke = z[:, :, 1024:1536].rearrange("p a (d n) -> p d a n", d=2)
                am = squares[:, 0:512].rearrange("p (d a n) -> p d a n", d=2, a=TT)
                glT = squares[0:16, 512:1024].rearrange("p (d s) -> p d s", d=2)
                a_in = squares[:, 1024:2048].rearrange("p (h a n) -> p h a n", h=GLA_H, a=TT)
            with ExitStack() as g:
                cT = sb("cT", [P, 2, 2, 2, S], F32R, where=g)
                lqT = sb("lqT", [P, MLA_H, S], where=g)
                lkT = sb("lkT", [P, MLA_H, S], where=g)
                lqrT = sb("lqrT", [64, MLA_H, S], where=g)
                lkrT = sb("lkrT", [64, MLA_H, S], where=g)
                lq = z[:, :, 0:768].rearrange("p a (h d) -> p a h d", h=MLA_H)
                lk = z[:, :, 768:1536].rearrange("p a (h d) -> p a h d", h=MLA_H)
                lkv = z[:, :, 1536:2560].rearrange("p a (h d) -> p a h d", h=MLA_H)
            z_rt = squares[:, :].rearrange("p (n a c) -> p n a c", n=4, a=TT)

        acc = ctx.enter_context(nc.psum_tensor("acc", [P, 4, 512], F32))
        bank = ctx.enter_context(nc.psum_tensor("bank", [P, 4, 512], F32))

        raw_in = [sem(f"raw_in{i}") for i in range(RAW)]
        hi_ready, lo_ready = sem("hi_ready"), sem("lo_ready")
        flip_hi = sem("flip_hi")
        full = [sem(f"bank_full{i}") for i in range(4)]
        taken = [sem(f"bank_taken{i}") for i in range(4)]
        piece_done = sem("piece_done")
        first_in, small_in = sem("first_in"), sem("small_in")
        queries_normed, queries_rotated = sem("queries_normed"), sem("queries_rotated")
        bias_in = sem("na_bias_in")
        bias_ready = sem("na_bias_ready")
        bias_room = sem("na_bias_room")
        out_done = sem("out_done")
        setup_v, setup_a = sem("setup_vector"), sem("setup_scalar")
        silu_ready, gate_made, gated_ready = sem("silu_ready"), sem("gate_made"), sem("gated_ready")
        acc_full, acc_taken = sem("acc_full"), sem("acc_taken")
        norm_src, squares_ready = sem("norm_src"), sem("squares_ready")
        flip_src = sem("flip_src")
        to_act, to_dve, dve_operand, act_operand = (
            sem("vector_to_scalar"), sem("scalar_to_vector"), sem("vector_operand"), sem("scalar_operand"))
        score_ready, prob_ready, softmax_ready = sem("score_ready"), sem("prob_ready"), sem("softmax_ready")
        x_final = sem("x_final")
        steps = {n: sem(f"{n}_step") for n in ("pe", "act", "dve", "pool", "sp")}

        ident = const[:, C_ID:C_ID + P]
        reverse = const[:, C_REV:C_REV + P]

        def selector(n, h):
            return const[0:n, C_ID + h:C_ID + h + 1].to_broadcast([n, P])

        def bank_of(b):
            return bank[:, b, :]

        def halves(b, w=COLS):
            return bank[:, b, :].rearrange("p (a c) -> p a c", a=2)[:, :, 0:w]

        def acc2():
            return acc[:, :, :].rearrange("p (a b) c -> p a (b c)", a=TT)

        def all_taken(t):
            for b in range(4):
                if t.banks.uses[b]:
                    t.e.wait_ge(taken[b], t.banks.uses[b])

        def claim(t, by_piece=False):
            b = t.banks.take(by_piece)
            if t.banks.uses[b] > 1:
                t.e.wait_ge(taken[b], t.banks.uses[b] - 1)
            return b

        def filled(t):
            b = t.banks.take()
            t.e.wait_ge(full[b], t.banks.filled[b])
            return b

        def load(t, src, i=None):
            n = t.piece
            t.piece += 1
            t.e.wait_ge(lo_ready, later(n + 1, i, LOOP))
            k = src.shape[1]
            dst = raw[:, n % RAW, 0:k * src.shape[2]].rearrange("p (k c) -> p k c", k=k)
            t.e.dma_start(dst, src).then_inc(raw_in[n % RAW], 16)

        def later(count, i, step):
            return count if i is None else i * step + count

        def cols_of(w, c, n=COLS):
            return w.rearrange("(k p) c -> p k c", p=P)[:, :, bass.ds(c, n)]

        def rows_of(w, r, n=D):
            return w.rearrange("(k p) c -> p k c", p=P)[:, bass.ds(r, 2), 0:n]

        def load_cols(t, w, c, n=COLS):
            load(t, cols_of(w, c, n))

        def load_rows(t, w, r, n=D):
            load(t, rows_of(w, r, n))

        def split_hi(t, n, i=None):
            if n < len(PIECES):
                size = PIECES[n]
                t.e.wait_ge(raw_in[n % RAW], later(16 * (n // RAW + 1), i, 16 * LOOP // RAW))
                t.e.wait_ge(piece_done, later(n + 1, i, LOOP))
                t.e.activation(parts[:, n % PARTS, 0, 0:size], raw[:, n % RAW, 0:size], ACT.Copy).then_inc(hi_ready, 1)

        def split_lo(t, n, i=None):
            if n < len(PIECES):
                size = PIECES[n]
                t.e.wait_ge(hi_ready, later(n + 1, i, LOOP))
                t.e.tensor_tensor(parts[:, n % PARTS, 1, 0:size], raw[:, n % RAW, 0:size],
                                  parts[:, n % PARTS, 0, 0:size].bitcast(F32), ALU.subtract).then_inc(lo_ready, 1)

        def next_hi(t):
            t.piece += 1
            split_hi(t, t.piece - 1 + PARTS)

        def next_lo(t):
            t.piece += 1
            split_lo(t, t.piece - 1 + PARTS)

        def through(t):
            return PARTS + t.piece

        def arrived(t, i=None, n=None):
            if n is None:
                n = t.piece
                t.piece += 1
            t.e.wait_ge(lo_ready, later(RAW + n + 1, i, LOOP))
            return n % PARTS

        def slot_cols(s, part, w=COLS):
            return parts[:, s, part, 0:KD * w].rearrange("p (k c) -> p k c", k=KD)

        def slot_rows(s, part, n=D):
            return parts[:, s, part, 0:2 * n].rearrange("p (k c) -> p k c", k=2)

        PASSES = ((0, 0), (0, 1), (1, 0))

        def ffn_sync(t, wg, wu, wd):
            load_cols(t, wg, 0)
            load_cols(t, wu, 0)
            n0 = t.piece
            with t.e.Fori(0, (CHUNKS - 1) // 2) as i:
                for j in range(2):
                    load(t, cols_of(wg, i * 512 + COLS * (1 + j)), i)
                    load(t, cols_of(wu, i * 512 + COLS * (1 + j)), i)
                    load(t, rows_of(wd, i * 4 + 2 * j), i)
            t.piece = n0 + 3 * (CHUNKS - 1)
            load_rows(t, wd, 2 * (CHUNKS - 1))

        def up_bank(t, c, which):
            return (t.banks.next + 2 * (c % 2) + which) % 4

        def ffn_up(t, c, s, which, hT_k=None):
            pe = t.e
            for f in range(2):
                for k in range(KD):
                    if hT_k and f == 0 and k % 2 == 0:
                        hT_k(k // 2)
                    for w, h in PASSES:
                        mm = pe.matmul(bank[:, up_bank(t, c, which), f * S:(f + 1) * S],
                                       slot_cols(s, w)[:, k, f * P:(f + 1) * P], hT[:, h, k, :],
                                       start=(k == 0 and w + h == 0), stop=(k == KD - 1 and w == 1))
            mm.then_inc(piece_done, 1)

        def down_product(pe, stationary, s, k, a, first, last):
            for g, w in PASSES:
                for n in range(2):
                    mm = pe.matmul(acc[:, 2 * a + n, :], stationary(g), slot_rows(s, w)[:, k, n * 512:(n + 1) * 512],
                                   start=(first and g + w == 0), stop=(last and g == 1), skip_group_check=True)
            return mm

        def ffn_down(pe, c, s, last=False):
            for a, f in [(a, f) for a in range(TT) for f in range(2)]:
                mm = down_product(pe, lambda g: gated[:, g, c % 2, f * S + a * P:f * S + (a + 1) * P], s, f, a,
                                  False, last and f == 1)
                if last and (a, f) == (0, 1):
                    mm.then_inc(acc_full, 1)
            mm.then_inc(piece_done, 1)

        def ffn_tensor(t, k):
            pe = t.e
            acc_is_free(t)
            for b in range(4):
                pe.matmul(acc[:, b, :], zeros[:, :], zeros[:, :].unsqueeze(1).to_broadcast([P, 4, P]), start=True,
                          stop=False, skip_group_check=True)
            ffn_up(t, 0, arrived(t), 0, hT_waits(t))
            ffn_up(t, 0, arrived(t), 1)
            n0 = t.piece
            with pe.Fori(0, (CHUNKS - 1) // 2) as i:
                for j in range(2):
                    for which in range(2):
                        ffn_up(t, 1 + j, arrived(t, i, n0 + 3 * j + which), which)
                    s = arrived(t, i, n0 + 3 * j + 2)
                    pe.wait_ge(gated_ready, i * 2 + (CHUNKS * k + 1 + j))
                    ffn_down(pe, j, s)
            t.piece += 3 * (CHUNKS - 1)
            s = arrived(t)
            pe.wait_ge(gated_ready, CHUNKS * (k + 1))
            ffn_down(pe, CHUNKS - 1, s, last=True)

        def ffn_scalar(t, k):
            act = t.e
            n0 = t.piece

            def chunk(c, n, i=None):
                split_hi(t, n + 2, i)
                act.wait_ge(piece_done, later(PARTS + n + 1, i, LOOP))
                act.activation(silu_gate[:, c % 2, :], bank_of(up_bank(t, c, 0)), ACT.Silu).then_inc(silu_ready, 1)
                split_hi(t, n + 3, i)
                if c:
                    split_hi(t, n + 4, i)

            chunk(0, n0)
            with act.Fori(0, (CHUNKS - 3) // 2) as i:
                for j in range(2):
                    chunk(1 + j, n0 + 2 + 3 * j, i)
            for c in (CHUNKS - 2, CHUNKS - 1):
                chunk(c, n0 + 2 + 3 * (c - 1))
            t.piece += 3 * CHUNKS - 1

        def ffn_vector(t, k):
            dve = t.e
            n0 = t.piece

            def chunk(c, n, i=None):
                split_lo(t, n + 2, i)
                dve.wait_ge(piece_done, later(PARTS + n + 2, i, LOOP))
                dve.wait_ge(silu_ready, later(CHUNKS * k + c + 1, i, 2))
                v = silu_gate[:, c % 2, :]
                dve.tensor_tensor(v, bank_of(up_bank(t, c, 1)), v, ALU.mult).then_inc(gate_made, 1)
                dve.wait_ge(gate_made, later(2 * (CHUNKS * k + c) + 1, i, 4))
                dve.tensor_copy(gated[:, 0, c % 2, :], v).then_inc(gate_made, 1)
                dve.wait_ge(gate_made, later(2 * (CHUNKS * k + c) + 2, i, 4))
                dve.tensor_tensor(gated[:, 1, c % 2, :], v, gated[:, 0, c % 2, :].bitcast(F32), ALU.subtract)\
                    .then_inc(gated_ready, 1)
                split_lo(t, n + 3, i)
                if c:
                    split_lo(t, n + 4, i)

            chunk(0, n0)
            with dve.Fori(0, (CHUNKS - 3) // 2) as i:
                for j in range(2):
                    chunk(1 + j, n0 + 2 + 3 * j, i)
            for c in (CHUNKS - 2, CHUNKS - 1):
                chunk(c, n0 + 2 + 3 * (c - 1))
            t.piece += 3 * CHUNKS - 1
            add_to_x(t, 0.5)

        def acc_is_free(t):
            if t.acc_uses:
                t.e.wait_ge(acc_taken, t.acc_uses)
            t.acc_uses += 1

        def add_to_x(t, scale):
            dve = t.e
            dve.wait_ge(acc_full, t.see(acc_full))
            dve.scalar_tensor_tensor(x[:, 0, :], acc2()[:, 0, :], scale, x[:, 0, :], ALU.mult, ALU.add)\
                .then_inc(norm_src, 1)
            dve.wait_ge(piece_done, PARTS + t.piece + 1)
            dve.scalar_tensor_tensor(x[:, 1, :], acc2()[:, 1, :], scale, x[:, 1, :], ALU.mult, ALU.add)\
                .then_inc(norm_src, 1)
            dve.wait_ge(norm_src, t.see(norm_src, 2))
            dve.sem_inc(acc_taken, 1)
            t.see(acc_taken)

        def rms_scalar(t, src, n, d):
            act = t.e
            act.wait_ge(norm_src, t.see(norm_src))
            sq = squares[:, 0:n * d]
            if len(src.shape) == 3:
                sq = sq.rearrange("p (n d) -> p n d", n=n)
            else:
                sq = sq.rearrange("p (a n d) -> p a n d", a=TT, d=d)
            act.activation(sq, src, ACT.Square).then_inc(squares_ready, 1)
            t.see(squares_ready)

        def root_vector(t, total, d, last_factor=False):
            dve = t.e
            o, n = total.offset % 32, total.shape[-1]
            v, y, w = (stat[:, j, o:o + n] for j in (1, 2, 3))
            t.link(dve.tensor_scalar(v, total, 1.0 / d, EPS, ALU.mult, ALU.add))
            t.link(dve.tensor_scalar(y.bitcast(I32), v.bitcast(I32), -0.5, float(0x5f3759df), ALU.mult, ALU.add))

            def weight():
                if n == 1:
                    t.link(dve.scalar_tensor_tensor(w, y, y, v, ALU.mult, ALU.mult))
                else:
                    t.link(dve.tensor_tensor(w, y, y, ALU.mult))
                    t.link(dve.tensor_tensor(w, w, v, ALU.mult))

            weight()
            t.link(dve.scalar_tensor_tensor(total, w, 0.375, w, ALU.mult, ALU.mult))
            t.link(dve.scalar_tensor_tensor(total, w, -1.25, total, ALU.mult, ALU.add))
            t.link(dve.scalar_tensor_tensor(y, total, 1.875, y, ALU.add, ALU.mult))
            weight()
            t.link(dve.tensor_scalar(w, w, -0.5, 1.5, ALU.mult, ALU.add))
            if last_factor:
                return y, w
            t.link(dve.tensor_tensor(y, y, w, ALU.mult))
            return y

        def mean_root_vector(t, n, d, behind_sum=None):
            dve = t.e
            dve.sem_inc(norm_src, 1)
            t.see(norm_src)
            dve.wait_ge(squares_ready, t.see(squares_ready))
            t.link(dve.tensor_reduce(stat[:, 0, 0:n], squares[:, 0:n * d].rearrange("p (n d) -> p n d", n=n), AX.X,
                                     ALU.add))
            y = root_vector(t, stat[:, 0, 0:n], d)
            if behind_sum:
                behind_sum()
            return y

        def rms_vector(t, src, n, d, behind_sum=None):
            dve = t.e
            y = mean_root_vector(t, n, d, behind_sum)
            if len(src.shape) == 3:
                yb = y.unsqueeze(2).to_broadcast([P, n, d])
            else:
                yb = y.rearrange("p (a n) -> p a n", a=TT).unsqueeze(3).to_broadcast([P, TT, n // TT, d])
            t.link(dve.tensor_tensor(src, src, yb, ALU.mult))

        def flip_tensor(t, src, n, rows_out=P, order=None):
            pe = t.e
            pe.wait_ge(flip_src, t.see(flip_src))
            for k0 in range(0, n, 2):
                b = claim(t)
                for k in range(k0, min(k0 + 2, n)):
                    for a in range(TT):
                        o = (k - k0) * S + a * P
                        mm = pe.transpose(bank[0:rows_out, b, o:o + P], src(k, a), ident if order is None else order)
                mm.then_inc(full[b], 1)

        def flip_out(t, dst, n, scale, rows_out, mine):
            for k0 in range(0, n, 2):
                if (k0 // 2) % 2 != mine:
                    t.banks.take()
                    continue
                b = filled(t)
                ks = range(k0, min(k0 + 2, n))
                if not callable(scale):
                    parts = [(dst[0:rows_out, k0:k0 + len(ks), :],
                              bank[0:rows_out, b, 0:len(ks) * S].rearrange("p (k s) -> p k s", s=S), scale)]
                else:
                    parts = [(dst[0:rows_out, k, :], bank[0:rows_out, b, (k - k0) * S:(k - k0 + 1) * S], scale(k))
                             for k in ks]
                for o, i, g in parts:
                    if mine == 0:
                        ins = t.e.activation(o, i, ACT.Copy, scale=1.0 if g is None else g)
                    else:
                        ins = t.e.tensor_scalar(o, i, 1.0 if g is None else g, None, ALU.mult)
                ins.then_inc(taken[b], 1)

        def flip_scalar(t, dst, n, scale=None, rows_out=P):
            flip_out(t, dst, n, scale, rows_out, 0)

        def flip_alone_scalar(t, dst, n):
            for k0 in range(0, n, 2):
                m = min(2, n - k0)
                b = filled(t)
                t.e.activation(dst[:, k0:k0 + m, :], bank[:, b, 0:m * S].rearrange("p (k s) -> p k s", s=S), ACT.Copy)\
                    .then_inc(taken[b], 1)

        def flip_alone_vector(t, n):
            t.e.sem_inc(flip_src, 1)
            for k0 in range(0, n, 2):
                t.banks.take()

        def flip_vector(t, dst, n, scale=None, rows_out=P):
            t.e.sem_inc(flip_src, 1)
            flip_out(t, dst, n, scale, rows_out, 1)

        def gain_col(at):
            return lambda k: gain[:, at + k:at + k + 1]

        def split_flip_scalar(t, dst, n, scale=None):
            for k0 in range(0, n, 2):
                b = filled(t)
                if scale is None:
                    ins = t.e.activation(dst[:, 0, k0:k0 + 2, :], halves(b), ACT.Copy)
                else:
                    for k in (k0, k0 + 1):
                        ins = t.e.activation(dst[:, 0, k, :], halves(b)[:, k - k0, :], ACT.Copy, scale=scale(k))
                ins.then_inc(flip_hi, 1)

        def split_flip_vector(t, dst, n, scale=None, signal=True):
            if signal:
                t.e.sem_inc(flip_src, 1)
            for k0 in range(0, n, 2):
                b = filled(t)
                t.e.wait_ge(flip_hi, t.see(flip_hi))
                if scale is None:
                    ins = t.e.tensor_tensor(dst[:, 1, k0:k0 + 2, :], halves(b), dst[:, 0, k0:k0 + 2, :].bitcast(F32),
                                            ALU.subtract)
                else:
                    for k in (k0, k0 + 1):
                        ins = t.e.scalar_tensor_tensor(dst[:, 1, k, :], halves(b)[:, k - k0, :], scale(k),
                                                       dst[:, 0, k, :].bitcast(F32), ALU.mult, ALU.subtract)
                ins.then_inc(taken[b], 1)

        PRE_BANKS = ((0, 4, 0), (0, 4, 4), (1, 2, 0), (1, 2, 2), (1, 2, 4), (1, 2, 6))

        def pre_tensor(t, at):
            pe = t.e
            for a, n, k0 in PRE_BANKS:
                if k0 == 0:
                    pe.wait_ge(flip_src, t.see(flip_src))
                b = claim(t)
                for j in range(n):
                    mm = pe.matmul(bank[:, b, j * P:(j + 1) * P], x[:, a, (k0 + j) * P:(k0 + j + 1) * P],
                                   root_diag[:, a, :], start=True, stop=True)
                mm.then_inc(full[b], 1)
            t.hT_banks = [((t.banks.next + j) % 4, t.banks.uses[(t.banks.next + j) % 4]) for j in range(4)]

        def hT_waits(t):
            return lambda j: t.e.wait_ge(taken[t.hT_banks[j][0]], t.hT_banks[j][1])

        def pre_scalar(t, at):
            act = t.e
            for a in range(TT):
                act.wait_ge(norm_src, t.see(norm_src))
                t.done(act.activation(squares[:, 0:D], x[:, a, :], ACT.Square, accum_out=stat[:, 0, a:a + 1]),
                       squares_ready)
            for a, n, k0 in PRE_BANKS:
                b = filled(t)
                for j in range(n):
                    ins = act.activation(hT[:, 0, k0 + j, a * P:(a + 1) * P], bank[:, b, j * P:(j + 1) * P], ACT.Copy,
                                         scale=gain[:, at + k0 + j:at + k0 + j + 1])
                ins.then_inc(flip_hi, 1)
            if t.piece:
                next_hi(t)

        def pre_vector(t, at):
            dve = t.e
            for a in range(TT):
                dve.wait_ge(squares_ready, t.see(squares_ready))
                y, w = root_vector(t, stat[:, 0, a:a + 1], D, last_factor=True)
                dve.tensor_scalar(root_diag[:, a, :], ident, y, w, ALU.mult, ALU.mult).then_inc(flip_src, 1)
            for a, n, k0 in PRE_BANKS:
                b = filled(t)
                dve.wait_ge(flip_hi, t.see(flip_hi))
                for j in range(n):
                    k = k0 + j
                    ins = dve.scalar_tensor_tensor(hT[:, 1, k, a * P:(a + 1) * P], bank[:, b, j * P:(j + 1) * P],
                                                   gain[:, at + k:at + k + 1],
                                                   hT[:, 0, k, a * P:(a + 1) * P].bitcast(F32), ALU.mult, ALU.subtract)
                ins.then_inc(taken[b], 1)
            if t.piece:
                next_lo(t)

        def project_tensor(t, widths, feature_major=False, hT_k=None):
            pe = t.e
            for w in widths:
                s = arrived(t)
                b = claim(t, by_piece=True)
                for a in range(2):
                    for k in range(KD):
                        if hT_k and a == 0 and k % 2 == 0:
                            hT_k(k // 2)
                        for p, q in PASSES:
                            if feature_major:
                                mm = pe.matmul(bank[:, b, a * S:(a + 1) * S], slot_cols(s, p)[:, k, a * P:(a + 1) * P],
                                               hT[:, q, k, :], start=(k == 0 and p + q == 0),
                                               stop=(k == KD - 1 and p == 1))
                            else:
                                mm = pe.matmul(bank[:, b, a * COLS:a * COLS + w], hT[:, p, k, a * P:(a + 1) * P],
                                               slot_cols(s, q, w)[:, k, :], start=(k == 0 and p + q == 0),
                                               stop=(k == KD - 1 and p == 1))
                mm.then_inc(piece_done, 1)
                hT_k = None

        def project_scalar(t, dsts, scale=1.0, func=ACT.Copy):
            for dst in dsts:
                b = t.banks.take(by_piece=True)
                next_hi(t)
                t.e.wait_ge(piece_done, through(t))
                t.e.activation(dst, halves(b, dst.shape[-1]), func, scale=scale).then_inc(taken[b], 1)

        def project_vector(t, n):
            for _ in range(n):
                t.banks.take(by_piece=True)
                next_lo(t)

        def down_tensor(t, actT, n):
            pe = t.e
            acc_is_free(t)
            for k0 in range(0, n, 2):
                s = arrived(t)
                end = k0 == n - 2
                for a in range(TT):
                    for k in (k0, k0 + 1):
                        mm = down_product(pe, lambda g: actT[:, g, k, a * P:(a + 1) * P], s, k - k0, a, k == 0,
                                          k == n - 1)
                    if end and a == 0:
                        mm.then_inc(acc_full, 1)
                mm.then_inc(piece_done, 1)

        def down_scalar(t, n, to_x=False):
            for _ in range(n // 2 - (1 if to_x else 0)):
                next_hi(t)

        def down_vector(t, n):
            for _ in range(n // 2 - 1):
                next_lo(t)

        def rotate(t, lo, hi, cos, sin, heads, tmp):
            dve = t.e
            c = cos.unsqueeze(2).to_broadcast([P, TT, heads, 32])
            s = sin.unsqueeze(2).to_broadcast([P, TT, heads, 32])
            v = [tmp[:, n, :, 0:heads * 32].rearrange("p a (h c) -> p a h c", c=32) for n in range(4)]
            dve.tensor_tensor(v[0], lo, c, ALU.mult)
            dve.tensor_tensor(v[1], hi, s, ALU.mult)
            dve.tensor_tensor(v[2], lo, s, ALU.mult)
            t.link(dve.tensor_tensor(v[3], hi, c, ALU.mult))
            dve.tensor_tensor(lo, v[0], v[1], ALU.subtract)
            t.link(dve.tensor_tensor(hi, v[2], v[3], ALU.add))

        def attend_tensor(t, heads, parts, value, dv, base, order=None, fill=None):
            pe = t.e
            all_taken(t)
            for i in range(heads + 3):
                if i < heads:
                    b = claim(t)
                    for a in range(TT):
                        ps = parts(i, a)
                        for n, (q, k) in enumerate(ps):
                            mm = pe.matmul(bank[:, b, a * S:(a + 1) * S], q, k, start=(n == 0), stop=(n == len(ps) - 1))
                    mm.then_inc(full[b], 1)
                if fill:
                    fill(i)
                if 2 <= i <= heads + 1:
                    pe.wait_ge(softmax_ready, t.see(softmax_ready))
                    b = claim(t)
                    for st in range(TT):
                        for a in range(TT):
                            o = st * S + a * P
                            mm = pe.transpose(bank[:, b, o:o + P], soft[:, (i - 2) % 3, a, st * P:(st + 1) * P],
                                              ident if order is None else order)
                    mm.then_inc(full[b], 1)
                if i >= 3:
                    h = i - 3
                    pe.wait_ge(act_operand, t.see(act_operand))
                    b = claim(t)
                    r = base(h)
                    for st in range(TT):
                        mm = pe.matmul(bank[r:r + dv, b, 0:S], value(h, st), soft_pT[:, h % 2, st * S:(st + 1) * S],
                                       start=(st == 0), stop=(st == TT - 1))
                    mm.then_inc(full[b], 1)

        def attend_scalar(t, heads, dst, fill=None):
            act = t.e
            for i in range(heads + 3):
                if i < heads:
                    t.banks.take()
                    act.wait_ge(score_ready, t.see(score_ready))
                    for a in range(TT):
                        ins = act.activation(soft[:, i % 3, a, :], soft[:, i % 3, a, :], ACT.Exp,
                                             bias=soft_m[:, i % 2, 0, a:a + 1], accum_out=soft_m[:, i % 2, 1, a:a + 1])
                    ins.then_inc(prob_ready, 1)
                if fill:
                    fill(i)
                if 2 <= i <= heads + 1:
                    b = filled(t)
                    act.activation(soft_pT[:, i % 2, :], bank_of(b), ACT.Copy).then_inc(taken[b], 1)
                    act.wait_ge(taken[b], t.banks.uses[b])
                    act.sem_inc(act_operand, 1)
                if i >= 3:
                    b = filled(t)
                    o, r, dv = dst(i - 3)
                    act.activation(o(0), bank[r:r + dv, b, 0:S], ACT.Copy).then_inc(flip_hi, 1)

        def attend_vector(t, heads, scale, bias, dst, fill=None):
            dve = t.e
            for i in range(heads + 3):
                if i < heads:
                    b = filled(t)
                    s = soft[:, i % 3, :, :]
                    if bias is None:
                        ins = dve.tensor_scalar(s, halves(b), scale, None, ALU.mult)
                    else:
                        ins = dve.scalar_tensor_tensor(s, halves(b), scale, bias(i), ALU.mult, ALU.add)
                    ins.then_inc(taken[b], 1)
                    dve.wait_ge(taken[b], t.banks.uses[b])
                    dve.tensor_reduce(soft_m[:, i % 2, 0, :], s, AX.X, ALU.max, negate=True).then_inc(score_ready, 1)
                if 1 <= i <= heads:
                    h = i - 1
                    dve.wait_ge(prob_ready, t.see(prob_ready))
                    t.link(dve.reciprocal(soft_r[:, h % 2, :], soft_m[:, h % 2, 1, :]))
                    for a in range(TT):
                        ins = dve.tensor_scalar(soft[:, h % 3, a, :], soft[:, h % 3, a, :],
                                                soft_r[:, h % 2, a:a + 1], None, ALU.mult)
                    ins.then_inc(softmax_ready, 1)
                if fill:
                    fill(i)
                if 2 <= i <= heads + 1:
                    t.banks.take()
                if i >= 3:
                    b = filled(t)
                    dve.wait_ge(flip_hi, t.see(flip_hi))
                    o, r, dv = dst(i - 3)
                    dve.tensor_tensor(o(1), bank[r:r + dv, b, 0:S], o(0).bitcast(F32), ALU.subtract)\
                        .then_inc(taken[b], 1)

        R_DT, R_FG, R_IG, R_T, R_L, R_A, R_ACS, R_DEND, R_B, R_M = range(10)
        HY_FEATURE = ((HY_XBC, 6), (HY_Q, 2), (HY_K, 2))
        HY_TOKEN = ((HY_Z, 4), (HY_V, 4), (HY_O, 4))

        def hybrid_sync(t):
            w = A["hy_w_in"][0]
            for at, n in HY_FEATURE + HY_TOKEN:
                for i in range(n):
                    load_cols(t, w, at + i * COLS)
            for r in range(0, 16, 2):
                load_rows(t, A["hy_w_out"][0], r)

        def hybrid_tensor(t):
            pe = t.e
            b = claim(t)
            hT_k = hT_waits(t)
            for a in range(TT):
                for k in range(KD):
                    if a == 0 and k % 2 == 0:
                        hT_k(k // 2)
                    for p, q in PASSES:
                        mm = pe.matmul(bank[:, b, a * 32:a * 32 + 24], hT[:, p, k, a * P:(a + 1) * P],
                                       w_gates_s[:, q, k, :], start=(k == 0 and p + q == 0), stop=(k == KD - 1 and p == 1))
            mm.then_inc(full[b], 1)
            project_tensor(t, [COLS] * 6, feature_major=True)
            all_taken(t)
            b = claim(t)
            for col, n, o in ((0, SSD_H, 0), (16, ML_H, S)):
                for a in range(TT):
                    mm = pe.transpose(bank[0:n, b, o + a * P:o + (a + 1) * P], gtok[:, a, col:col + n], ident)
            mm.then_inc(full[b], 1)
            b = claim(t)
            for a in range(TT):
                mm = pe.transpose(bank[0:ML_H, b, a * P:(a + 1) * P], gtok[:, a, 20:24], ident)
            mm.then_inc(full[b], 1)
            project_tensor(t, [COLS] * 4, feature_major=True)
            project_tensor(t, [COLS] * 12)
            pe.wait_ge(dve_operand, t.see(dve_operand))
            b = claim(t)
            for c in range(TT):
                for row, n, o in ((R_DT, 16, 0), (R_ACS, 16, 16), (R_DEND, 16, 32), (R_B, 4, 48), (R_T, 4, 52),
                                  (R_A, 4, 56)):
                    mm = pe.transpose(bank[:, b, c * 64 + o:c * 64 + o + n], hrow[0:n, row, c * P:(c + 1) * P],
                                      const[0:n, C_ID:C_ID + n])
            mm.then_inc(full[b], 1)
            pe.wait_ge(act_operand, t.see(act_operand))
            b = claim(t)
            for g in range(SSD_G):
                for c in range(TT):
                    o = (g * TT + c) * P
                    mm = pe.matmul(bank[:, b, o:o + P], conv[:, 8 + g, c * P:(c + 1) * P],
                                   conv[:, 10 + g, c * P:(c + 1) * P], start=True, stop=True)
            mm.then_inc(full[b], 1)
            for c in range(TT):
                for h in range(2):
                    b = claim(t)
                    for k in range(4):
                        mm = pe.transpose(bank[:, b, k * P:(k + 1) * P], conv[:, 4 * h + k, c * P:(c + 1) * P], ident)
                    mm.then_inc(full[b], 1)
            b = claim(t)
            for g in range(SSD_G):
                mm = pe.transpose(bank[:, b, g * P:(g + 1) * P], conv[:, 8 + g, 0:P], ident)
            mm.then_inc(full[b], 1)
            for h in range(0, SSD_H, 2):
                b = claim(t)
                for j in range(2):
                    mm = pe.matmul(bank[:, b, j * S:(j + 1) * S], selector(SSD_H, h + j),
                                   hrow[:, R_ACS, :], start=True, stop=True)
                mm.then_inc(full[b], 1)
            pe.wait_ge(dve_operand, t.see(dve_operand))
            all_taken(t)
            for g in range(SSD_G):
                b = claim(t)
                pe.matmul(bank_of(b), b_tok[:, g, :], xde[:, g * 512:(g + 1) * 512], start=True, stop=True)\
                    .then_inc(full[b], 1)
            pe.wait_ge(dve_operand, t.see(dve_operand))
            acc_is_free(t)
            for c in range(TT):
                for h in range(SSD_H):
                    mm = pe.matmul(acc[:, 2 * c + h // 8, (h % 8) * 64:(h % 8 + 1) * 64], wT[:, h, c * P:(c + 1) * P],
                                   xd[:, c, h * 64:(h + 1) * 64], start=True, stop=True)
            mm.then_inc(acc_full, 1)
            all_taken(t)
            for g in range(SSD_G):
                b = claim(t)
                pe.matmul(bank_of(b), conv[:, 10 + g, P:S], state[:, g, :], start=True, stop=True).then_inc(full[b], 1)

            b = claim(t)
            for h in range(ML_H):
                mm = pe.transpose(bank[:, b, h * P:(h + 1) * P], mk[:, h, 0:P], ident)
            mm.then_inc(full[b], 1)
            all_taken(t)
            for h in range(ML_H):
                b = claim(t)
                pe.matmul(bank[:, b, 0:ML_VA], kw[:, h, :], mv[:, 0, h, :], start=True, stop=True).then_inc(full[b], 1)
            for h in range(0, ML_H, 2):
                b = claim(t)
                for j in range(2):
                    mm = pe.matmul(bank[:, b, j * S:(j + 1) * S], selector(ML_H, h + j),
                                   hrow[0:ML_H, R_M, :], start=True, stop=True)
                mm.then_inc(full[b], 1)
                b = claim(t)
                for j in range(2):
                    for c in range(TT):
                        mm = pe.matmul(bank[:, b, j * S + c * P:j * S + (c + 1) * P], mk[:, h + j, c * P:(c + 1) * P],
                                       mq[:, h + j, c * P:(c + 1) * P], start=True, stop=True)
                mm.then_inc(full[b], 1)
            b = claim(t)
            for h in range(ML_H):
                mm = pe.matmul(bank[:, b, h * P:(h + 1) * P], selector(ML_H, h),
                               hrow[0:ML_H, R_L, P:S], start=True, stop=True)
            mm.then_inc(full[b], 1)
            all_taken(t)
            for c in range(TT):
                for h in range(ML_H):
                    b = claim(t)
                    mm = pe.matmul(bank[:, b, 0:ML_VA], wT[:, h, c * P:(c + 1) * P], mv[:, c, h, :],
                                   start=True, stop=(c == 0))
                    if c:
                        mm = pe.matmul(bank[:, b, 0:ML_VA], qw[:, h, :], cst[:, h, :], start=False, stop=True)
                    mm.then_inc(full[b], 1)
            flip_tensor(t, lambda k, a: xs[:, a, k * P:(k + 1) * P], 8)
            flip_tensor(t, lambda k, a: xd[:, a, k * P:(k + 1) * P], 8)
            all_taken(t)
            down_tensor(t, yT, 16)

        def hybrid_scalar(t):
            act = t.e
            b = filled(t)
            act.activation(gtok[:, :, :], bank[:, b, 0:64].rearrange("p (a n) -> p a n", a=TT)[:, :, 0:24], ACT.Copy)\
                .then_inc(taken[b], 1)
            act.activation(heads_in[:, 3:4], heads_in[:, 1:2], ACT.Exp).then_inc(to_dve, 1)
            project_scalar(t, [xbc[:, 2 * i:2 * i + 2, CONV_K - 1:] for i in range(6)])
            t.banks.take(), t.banks.take()
            project_scalar(t, [mq[:, 2 * i:2 * i + 2, :] for i in range(2)], scale=float(P) ** -0.5)
            project_scalar(t, [mk[:, 2 * i:2 * i + 2, :] for i in range(2)])
            act.wait_ge(to_act, t.see(to_act))
            t.link(act.activation(hrow[:, R_T:R_T + 2, :], hrow[:, R_T:R_T + 2, :], ACT.Exp))
            act.activation(hrow[:, R_T:R_T + 2, :], hrow[:, R_T:R_T + 2, :], ACT.Ln, bias=1.0).then_inc(to_dve, 1)
            project_scalar(t, [zg[:, :, i * COLS:(i + 1) * COLS] for i in range(4)])
            project_scalar(t, [mv[:, :, i, 0:ML_V] for i in range(4)])
            gates = [og[:, :, i * COLS:(i + 1) * COLS] for i in range(4)]
            project_scalar(t, gates[0:1])
            act.wait_ge(to_act, t.see(to_act))
            t.link(act.activation(conv[:, :, :], conv[:, :, :], ACT.Silu))
            act.sem_inc(act_operand, 1)
            project_scalar(t, gates[1:2])
            all_taken(t)
            act.activation(zg[:, :, :], zg[:, :, :], ACT.Silu)
            project_scalar(t, gates[2:4])
            act.wait_ge(to_act, t.see(to_act))
            act.activation(hrow[:, R_DEND, :], hrow[:, R_DEND, :], ACT.Exp)
            act.activation(hrow[0:ML_H, R_T, :], hrow[0:ML_H, R_T, :], ACT.Exp)
            act.activation(hrow[0:ML_H, R_A, :], hrow[0:ML_H, R_A, :], ACT.Exp)
            act.activation(hrow[0:ML_H, R_L, :], hrow[0:ML_H, R_L, :], ACT.Exp).then_inc(to_dve, 1)
            all_taken(t)
            act.activation(og[:, :, :], og[:, :, :], ACT.Sigmoid).then_inc(to_dve, 1)
            b = filled(t)
            act.activation(cols[:, :, :], bank[:, b, 0:TT * 64].rearrange("p (c n) -> p c n", c=TT), ACT.Copy)\
                .then_inc(taken[b], 1)
            act.wait_ge(taken[b], t.banks.uses[b])
            act.activation(ecols[:, :], cols[:, 1, 16:32], ACT.Exp).then_inc(to_dve, 1)
            b = filled(t)
            act.activation(cb[:, :, :, :], bank_of(b).rearrange("p (g c n) -> p g c n", g=2, c=2), ACT.Copy)\
                .then_inc(taken[b], 1)
            for c in range(TT):
                for h in range(2):
                    b = filled(t)
                    act.activation(xs[:, c, h * 512:(h + 1) * 512], bank_of(b), ACT.Copy).then_inc(taken[b], 1)
            b = filled(t)
            act.activation(b_tok[:, :, :], bank[:, b, 0:S].rearrange("p (g n) -> p g n", g=2),
                           ACT.Copy).then_inc(taken[b], 1)
            for h in range(0, SSD_H, 2):
                t.banks.take()
                act.wait_ge(to_act, t.see(to_act))
                act.activation(seg[:, (h // 2) % 2, :], seg[:, (h // 2) % 2, :], ACT.Exp).then_inc(to_dve, 1)
            for g in range(SSD_G):
                b = filled(t)
                act.activation(state[:, g, :], bank_of(b), ACT.Copy).then_inc(taken[b], 1)
            t.banks.take(), t.banks.take()
            t.banks.take()
            for h in range(ML_H):
                b = filled(t)
                act.activation(cst[:, h, :], bank[:, b, 0:ML_VA], ACT.Copy).then_inc(taken[b], 1)
            for h in range(0, ML_H, 2):
                t.banks.take(), t.banks.take()
                act.wait_ge(to_act, t.see(to_act))
                act.activation(seg[:, (h // 2) % 2, :], seg[:, (h // 2) % 2, :], ACT.Exp).then_inc(to_dve, 1)
            t.banks.take()
            rms_scalar(t, xs[:, :, :].rearrange("p a (g d) -> p (a g) d", g=2), 4, 512)
            for c in range(TT):
                for h in range(ML_H):
                    b = filled(t)
                    act.activation(hm[:, c, h, :], bank[:, b, 0:ML_VA], ACT.Copy).then_inc(taken[b], 1)
            rms_scalar(t, xd[:, :, :].rearrange("p a (g d) -> p (a g) d", g=ML_H), 8, 256)
            split_flip_scalar(t, yT[:, :, 0:8, :], 8, gain_col(G_SSD))
            split_flip_scalar(t, yT[:, :, 8:16, :], 8, gain_col(G_ML))
            down_scalar(t, 16, to_x=True)

        def hybrid_vector(t):
            dve = t.e
            r = lambda n, k=SSD_H: hrow[0:k, n, :]
            t.link(dve.memset(hrow[:, :, :], 0.0))
            dve.memset(mv[:, :, :, ML_V:ML_VA], 1.0)
            t.link(dve.memset(xbc[:, :, 0:CONV_K - 1], 0.0))
            t.banks.take()
            project_vector(t, 6)
            b = filled(t)
            dve.tensor_scalar(r(R_DT), bank[0:SSD_H, b, 0:S], heads_in[:, 0:1], None, ALU.add)
            dve.tensor_scalar(r(R_IG, ML_H), bank[0:ML_H, b, S:2 * S], heads_in[0:ML_H, 2:3], None, ALU.add)\
                .then_inc(taken[b], 1)
            dve.wait_ge(taken[b], t.banks.uses[b])
            b = filled(t)
            dve.tensor_scalar(r(R_FG, ML_H), bank[0:ML_H, b, 0:S], fg_bias[:, 0:1], None, ALU.add).then_inc(taken[b], 1)
            dve.wait_ge(taken[b], t.banks.uses[b])
            both, e = hrow[:, R_DT:R_DT + 2, :], hrow[:, R_T:R_T + 2, :]
            dve.wait_ge(to_dve, t.see(to_dve))
            dve.scalar_tensor_tensor(e, both, -1.0, both, ALU.mult, ALU.min).then_inc(to_act, 1)
            all_taken(t)
            for k in range(CONV_T):
                project_vector(t, 1)
                o = conv[:, k, :]
                tap = lambda n: gain[:, G_CW + n * CONV_T + k:G_CW + n * CONV_T + k + 1]
                t.link(dve.tensor_scalar(o, xbc[:, k, 0:S], tap(0), gain[:, G_CB + k:G_CB + k + 1], ALU.mult, ALU.add))
                for n in range(1, CONV_K):
                    t.link(dve.scalar_tensor_tensor(o, xbc[:, k, n:n + S], tap(n), o, ALU.mult, ALU.add))
            dve.sem_inc(to_act, 1)
            project_vector(t, 1)
            dve.wait_ge(to_dve, t.see(to_dve))
            t.link(dve.scalar_tensor_tensor(r(R_DT), r(R_DT), 0.0, r(R_T), ALU.max, ALU.add))
            t.link(dve.scalar_tensor_tensor(r(R_FG), r(R_FG), 0.0, r(R_L), ALU.min, ALU.subtract))
            t.link(dve.tensor_scalar(r(R_A), r(R_DT), heads_in[:, 3:4], -1.0, ALU.mult, ALU.mult))
            for c in range(TT):
                cc = slice(c * P, (c + 1) * P)
                t.link(dve.tensor_tensor_scan(hrow[:, R_ACS, cc], ones[:, :], hrow[:, R_A, cc], 0.0, ALU.mult, ALU.add))
                t.link(dve.tensor_scalar(hrow[:, R_DEND, cc], hrow[:, R_ACS, cc], hrow[:, R_ACS, c * P + P - 1:c * P + P],
                                         -1.0, ALU.subtract, ALU.mult))
            q = ML_H
            for c in range(TT):
                project_vector(t, 1)
                cc = slice(c * P, (c + 1) * P)
                last = c * P + P - 1
                m_in = 0.0 if c == 0 else heads4[:, 0:1]
                t.link(dve.tensor_tensor_scan(hrow[0:q, R_L, cc], ones[0:q, :], hrow[0:q, R_FG, cc], 0.0,
                                              ALU.mult, ALU.add))
                t.link(dve.tensor_tensor(hrow[0:q, R_B, cc], hrow[0:q, R_IG, cc], hrow[0:q, R_L, cc], ALU.subtract))
                t.link(dve.tensor_tensor_scan(hrow[0:q, R_M, cc], hrow[0:q, R_B, cc], hrow[0:q, R_B, cc], m_in,
                                              ALU.max, ALU.max))
                t.link(dve.scalar_tensor_tensor(hrow[0:q, R_T, cc], hrow[0:q, R_L, cc], -1.0, hrow[0:q, R_M, cc],
                                                ALU.mult, ALU.subtract))
                t.link(dve.tensor_scalar(hrow[0:q, R_A, cc], hrow[0:q, R_B, cc], hrow[0:q, R_M, last:last + 1], None,
                                         ALU.subtract))
                if c == 0:
                    t.link(dve.tensor_tensor(heads4[:, 0:1], hrow[0:q, R_L, last:last + 1],
                                             hrow[0:q, R_M, last:last + 1], ALU.add))
                t.link(dve.tensor_scalar(hrow[0:q, R_M, cc], hrow[0:q, R_M, cc], -1.0, None, ALU.mult))
                if c == 0:
                    t.link(dve.memset(hrow[0:q, R_L, cc], 0.0))
                else:
                    t.link(dve.tensor_scalar(hrow[0:q, R_L, cc], hrow[0:q, R_M, cc], m_in, None, ALU.add))
            dve.sem_inc(to_act, 1)
            project_vector(t, 1)
            dve.wait_ge(to_dve, t.see(to_dve))
            dve.sem_inc(dve_operand, 1)
            all_taken(t)
            t.banks.take()
            dve.wait_ge(to_dve, t.see(to_dve, 2))
            t.banks.take()
            for _ in range(5):
                t.banks.take()
            all_taken(t)
            v4 = lambda ap: ap.rearrange("p c (h d) -> p c h d", h=SSD_H)
            t.link(dve.tensor_tensor(v4(xd[:, :, :]), v4(xs[:, :, :]),
                                     cols[:, :, 0:16].unsqueeze(3).to_broadcast([P, TT, SSD_H, 64]), ALU.mult))
            caus = const[:, C_CAUS_T:C_CAUS_T + P]

            def weigh(h):
                dve.wait_ge(to_dve, t.see(to_dve))
                g = h // 8
                t.link(dve.tensor_tensor(wT[:, h:h + 2, :].rearrange("p j (c n) -> p j c n", c=TT),
                                         seg[:, (h // 2) % 2, :].rearrange("p (j c n) -> p j c n", j=2, c=TT),
                                         cb[:, g, :, :].unsqueeze(1).to_broadcast([P, 2, TT, P]), ALU.mult))

            for h in range(0, SSD_H, 2):
                b = filled(t)
                s4 = seg[:, (h // 2) % 2, :].rearrange("p (j c n) -> p j c n", j=2, c=TT)
                a4 = cols[:, :, 16 + h:18 + h].rearrange("p c j -> p j c").unsqueeze(3).to_broadcast([P, 2, TT, P])
                dve.tensor_tensor(s4, bank_of(b).rearrange("p (j c n) -> p j c n", j=2, c=TT), a4, ALU.subtract)\
                    .then_inc(taken[b], 1)
                dve.wait_ge(taken[b], t.banks.uses[b])
                s3 = seg[:, (h // 2) % 2, :].rearrange("p (k n) -> p k n", n=P)
                dve.tensor_tensor(s3, s3, caus.unsqueeze(1).to_broadcast([P, 4, P]), ALU.add).then_inc(to_act, 1)
                if h == 0:
                    t.link(dve.tensor_tensor(xde[:, :].rearrange("p (h d) -> p h d", h=SSD_H),
                                             xd[:, 0, :].rearrange("p (h d) -> p h d", h=SSD_H),
                                             cols[:, 0, 32:48].unsqueeze(2).to_broadcast([P, SSD_H, 64]), ALU.mult))
                    dve.sem_inc(dve_operand, 1)
                else:
                    weigh(h - 2)
            weigh(SSD_H - 2)
            dve.sem_inc(dve_operand, 1)
            t.link(dve.tensor_tensor(v4(xs[:, :, :]), v4(xs[:, :, :]),
                                     rows[:, R_DSKIP:R_DSKIP + 16].unsqueeze(1).unsqueeze(3)
                                     .to_broadcast([P, TT, SSD_H, 64]), ALU.mult))
            dve.wait_ge(acc_full, t.see(acc_full))
            t.done(dve.tensor_tensor(xs[:, :, :], xs[:, :, :], acc2(), ALU.add), acc_taken)
            t.banks.take(), t.banks.take()
            for g in range(SSD_G):
                b = filled(t)
                dve.tensor_tensor(seg[:, g, :].rearrange("p (h d) -> p h d", h=8),
                                  bank_of(b).rearrange("p (h d) -> p h d", h=8),
                                  ecols[:, 8 * g:8 * g + 8].unsqueeze(2).to_broadcast([P, 8, 64]), ALU.mult)\
                    .then_inc(taken[b], 1)
                dve.wait_ge(taken[b], t.banks.uses[b])
                t.link(dve.tensor_tensor(xs[:, 1, g * 512:(g + 1) * 512], xs[:, 1, g * 512:(g + 1) * 512],
                                         seg[:, g, :], ALU.add))
            t.link(dve.tensor_tensor(xs[:, :, :], xs[:, :, :], zg[:, :, :], ALU.mult))
            b = filled(t)
            dve.tensor_tensor(kw[:, :, :], bank_of(b).rearrange("p (h n) -> p h n", h=ML_H),
                              cols[:, 0, 56:60].unsqueeze(2).to_broadcast([P, ML_H, P]), ALU.mult).then_inc(taken[b], 1)
            for h in range(ML_H):
                t.banks.take()
            for h in range(0, ML_H, 2):
                b = filled(t)
                s4 = seg[:, (h // 2) % 2, :].rearrange("p (j c n) -> p j c n", j=2, c=TT)
                a4 = cols[:, :, 48 + h:50 + h].rearrange("p c j -> p j c").unsqueeze(3).to_broadcast([P, 2, TT, P])
                dve.tensor_tensor(s4, bank_of(b).rearrange("p (j c n) -> p j c n", j=2, c=TT), a4, ALU.add)\
                    .then_inc(taken[b], 1)
                dve.wait_ge(taken[b], t.banks.uses[b])
                s3 = seg[:, (h // 2) % 2, :].rearrange("p (k n) -> p k n", n=P)
                dve.tensor_tensor(s3, s3, caus.unsqueeze(1).to_broadcast([P, 4, P]), ALU.add).then_inc(to_act, 1)
                b = filled(t)
                dve.wait_ge(to_dve, t.see(to_dve))
                dve.tensor_tensor(wT[:, h:h + 2, :].rearrange("p j n -> p (j n)"), bank_of(b),
                                  seg[:, (h // 2) % 2, :], ALU.mult).then_inc(taken[b], 1)
            b = filled(t)
            dve.tensor_tensor(qw[:, :, :], bank_of(b).rearrange("p (h n) -> p h n", h=ML_H), mq[:, :, P:S], ALU.mult)\
                .then_inc(taken[b], 1)
            rms_vector(t, xs[:, :, :].rearrange("p a (g d) -> p (a g) d", g=2), 4, 512)
            for _ in range(8):
                t.banks.take()
            all_taken(t)
            den = hm[:, :, :, ML_V:ML_VA].rearrange("p c h o -> p c (h o)")
            d0 = hden[:, 0, :].rearrange("p (c h) -> p c h", c=TT)
            t.link(dve.scalar_tensor_tensor(d0, den, -1.0, den, ALU.mult, ALU.max))
            t.link(dve.tensor_tensor(d0, d0, cols[:, :, 52:56], ALU.max))
            t.link(dve.reciprocal(hden[:, 1, :], hden[:, 0, :]))
            h4 = xd[:, :, :].rearrange("p c (h d) -> p c h d", h=ML_H)
            t.link(dve.tensor_tensor(h4, hm[:, :, :, 0:ML_V], hden[:, 1, :].rearrange("p (c h) -> p c h", c=TT)
                                     .unsqueeze(3).to_broadcast([P, TT, ML_H, ML_V]), ALU.mult))
            y = mean_root_vector(t, 8, 256, lambda: split_flip_vector(t, yT[:, :, 0:8, :], 8, gain_col(G_SSD)))
            for n in range(8):
                c, h = n // ML_H, n % ML_H
                v = xd[:, c, h * ML_V:(h + 1) * ML_V]
                ins = dve.scalar_tensor_tensor(v, v, y[:, n:n + 1], og[:, c, h * ML_V:(h + 1) * ML_V], ALU.mult,
                                               ALU.mult)
            t.link(ins)
            split_flip_vector(t, yT[:, :, 8:16, :], 8, gain_col(G_ML))
            down_vector(t, 16)
            add_to_x(t, 1.0)

        def sparse_sync(t):
            for i, w in enumerate(SA_W):
                load_cols(t, A["sa_w_in"][0], i * COLS, w)
            for r in range(0, 8, 2):
                load_rows(t, A["sa_w_out"][0], r)

        def sparse_tensor(t):
            pe = t.e
            project_tensor(t, SA_W, hT_k=hT_waits(t))
            all_taken(t)
            flip_tensor(t, lambda k, a: sa[:, a, SA_QI + k * P:SA_QI + (k + 1) * P], 4)
            flip_tensor(t, lambda k, a: sa_kd[:, a, 1, :], 1)
            all_taken(t)
            for h in range(SA_IH):
                b = claim(t)
                r = 64 * (h % 2)
                for a in range(TT):
                    mm = pe.matmul(bank[:, b, a * S:(a + 1) * S], sa_qiT[r:r + 64, h // 2, a * P:(a + 1) * P],
                                   sa_kiT[r:r + 64, 0, :], start=True, stop=True)
                mm.then_inc(full[b], 1)
            flip_tensor(t, lambda k, a: sa[:, a, k * P:(k + 1) * P], 8)
            flip_tensor(t, lambda k, a: sa_kd[:, a, 0, :], 1)
            lo = lambda h: 64 * (h % 2)
            attend_tensor(t, SA_H, lambda h, a: [(sa_qT[lo(h):lo(h) + 64, h // 2, a * P:(a + 1) * P],
                                                  sa_kT[lo(h):lo(h) + 64, 0, :])],
                          lambda h, st: sa[:, st, SA_V:SA_V + SA_D], 64, lo)
            all_taken(t)
            down_tensor(t, hT, 8)

        def pair_of(dst):
            def at(h):
                r = 64 * (h % 2)
                return lambda part: dst[r:r + 64, part, h // 2, :], r, 64
            return at

        def head_views(ap, at, heads, d=64):
            v = ap[:, :, at:at + heads * d].rearrange("p a (h d) -> p a h d", d=d)
            return v

        def index_score(h):
            return sa_rt[:, h % 4, :, S * (h // 4):S * (h // 4 + 1)]

        def sparse_scalar(t):
            tiles = [sa[:, :, i * COLS:i * COLS + w] for i, w in enumerate(SA_W)]
            project_scalar(t, tiles[0:4])
            rms_scalar(t, head_views(sa, 0, SA_H), TT * SA_H, 64)
            project_scalar(t, tiles[4:6])
            rms_scalar(t, sa[:, :, SA_K:SA_K + 64], TT, 64)
            project_scalar(t, tiles[6:])
            flip_scalar(t, sa_qiT, 4)
            flip_scalar(t, sa_kiT, 1)
            t.e.wait_ge(queries_rotated, 1)
            for h in range(SA_IH):
                b = filled(t)
                t.e.activation(index_score(h), halves(b), ACT.Relu).then_inc(taken[b], 1)
            flip_alone_scalar(t, sa_qT, 8)
            flip_alone_scalar(t, sa_kT, 1)
            attend_scalar(t, SA_H, pair_of(hT))
            down_scalar(t, 8, to_x=True)

        def sparse_vector(t):
            dve = t.e
            cos, sin = rope1[:, 0, :, :], rope1[:, 1, :, :]
            rt = squares[:, :].rearrange("p (n a c) -> p n a c", n=4, a=TT)
            project_vector(t, 4)
            all_taken(t)
            rms_vector(t, head_views(sa, 0, SA_H), TT * SA_H, 64, lambda: project_vector(t, 1))
            dve.sem_inc(queries_normed, 1)
            project_vector(t, 1)
            all_taken(t)
            v = head_views(sa, SA_K, 1)
            rms_vector(t, sa[:, :, SA_K:SA_K + 64], TT, 64)
            t.link(dve.tensor_tensor(v, v, rows[:, R_SAK:R_SAK + 64].unsqueeze(1).unsqueeze(1)
                                     .to_broadcast([P, TT, 1, 64]), ALU.mult))
            rotate(t, v[:, :, :, 0:32], v[:, :, :, 32:64], cos, sin, 1, rt)
            project_vector(t, 1)
            all_taken(t)
            for n in range(2):
                ins = dve.tensor_copy(sa_kd[:, :, 0, n * 64:(n + 1) * 64], sa[:, :, SA_K:SA_K + 64])
            t.link(ins)
            for at, n in ((SA_QI, SA_IH), (SA_KI, 1)):
                v = head_views(sa, at, n)
                rotate(t, v[:, :, :, 0:32], v[:, :, :, 32:64], cos, sin, n, rt)
            t.link(dve.tensor_scalar(sa[:, :, SA_WI:SA_WI + SA_IH], sa[:, :, SA_WI:SA_WI + SA_IH],
                                     float(SA_IH) ** -0.5 * float(SA_D) ** -0.5, None, ALU.mult))
            dve.tensor_copy(sa_kd[:, :, 1, 0:64], sa[:, :, SA_KI:SA_KI + 64])
            t.link(dve.tensor_copy(sa_kd[:, :, 1, 64:128], sa[:, :, SA_KI:SA_KI + 64]))
            flip_vector(t, sa_qiT, 4)
            flip_vector(t, sa_kiT, 1)
            caus = const[:, C_CAUS:C_CAUS + TT * S].rearrange("p (a s) -> p a s", a=TT)
            for h in range(SA_IH):
                b = t.banks.take()
                dve.wait_ge(taken[b], t.banks.uses[b])
                for a in range(TT):
                    ins = dve.scalar_tensor_tensor(sa_sc[:, a, :], index_score(h)[:, a, :],
                                                   sa[:, a, SA_WI + h:SA_WI + h + 1],
                                                   caus[:, a, :] if h == 0 else sa_sc[:, a, :], ALU.mult, ALU.add)
                t.link(ins)
            dve.wait_ge(queries_rotated, 1)
            flip_alone_vector(t, 8)
            flip_alone_vector(t, 1)
            for _ in range(TOPK // 8):
                for a in range(TT):
                    ins = dve.max(sa_m8[:, a, :], sa_sc[:, a, :])
                t.link(ins)
                for a in range(TT):
                    ins = dve.match_replace(sa_sc[:, a, :], sa_m8[:, a, :], sa_sc[:, a, :], TAKEN_KEY)
                t.link(ins)
            t.link(dve.tensor_scalar(sa_bias[:, :, :], sa_sc[:, :, :], 0.5 * TAKEN_KEY, NEG, ALU.is_gt, ALU.mult))
            t.link(dve.tensor_tensor(sa_bias[:, :, :], sa_bias[:, :, :], caus, ALU.add))
            attend_vector(t, SA_H, float(SA_D) ** -0.5, lambda h: sa_bias[:, :, :], pair_of(hT))
            down_vector(t, 8)
            add_to_x(t, 1.0)

        def triple_sync(t, l):
            def load_gates(n):
                for i in range(4):
                    load_cols(t, A["w_in_2"][l], Z_GT + n * D + i * COLS)

            for i, w in zip(Z_TILES, Z_W):
                load_cols(t, A["w_in_2"][l], i * COLS, w)
            load_gates(0)
            for r in (0, 2):
                load_rows(t, A["w_br_na_2"][l], r)
            load_gates(1)
            for r in (0, 2):
                load_rows(t, A["w_br_gla_2"][l], r)
            load_rows(t, A["mla_w_uq_2"][l], 0, MLA_H * MLA_QK)
            load_rows(t, A["mla_w_ukv_2"][l], 0)
            load_gates(2)
            for r in (0, 2):
                load_rows(t, A["w_br_mla_2"][l], r)
            for r in range(0, 8, 2):
                load_rows(t, A["w_out_2"][l], r)

        GATE_STEPS = (1, 3, 5, 7)

        def gate_tensor(t):
            return lambda i: project_tensor(t, [COLS]) if i in GATE_STEPS else None

        def gate_scalar(t):
            return lambda i: gate_quarter(t, GATE_STEPS.index(i)) if i in GATE_STEPS else None

        def gate_quarter(t, n):
            project_scalar(t, [gt[:, :, n * COLS:(n + 1) * COLS]], func=ACT.Sigmoid)

        def gate_vector(t):
            return lambda i: project_vector(t, 1) if i in GATE_STEPS else None

        def na_tensor(t, l):
            flip_tensor(t, lambda k, a: z[:, a, Z_NQ + k * P:Z_NQ + (k + 1) * P], 4, order=reverse)
            flip_tensor(t, lambda k, a: z[:, a, Z_NK + k * P:Z_NK + (k + 1) * P], 4)
            lo = lambda h: 64 * (h % 2)
            attend_tensor(t, NA_H, lambda h, a: [(na_qT[lo(h):lo(h) + 64, h // 2, a * P:(a + 1) * P],
                                                  na_kT[lo(h):lo(h) + 64, h // 2, :])],
                          lambda h, st: z[:, st, Z_NV + h * 64:Z_NV + (h + 1) * 64], 64, lo, order=reverse,
                          fill=gate_tensor(t))
            all_taken(t)
            down_tensor(t, brT, 4)

        def na_scalar(t, l):
            flip_scalar(t, na_qT, 4)
            flip_scalar(t, na_kT, 4)
            attend_scalar(t, NA_H, pair_of(brT), gate_scalar(t))
            down_scalar(t, 4)

        def na_vector(t, l):
            dve = t.e
            flip_vector(t, na_qT, 4)
            flip_vector(t, na_kT, 4)
            dve.wait_ge(bias_ready, l + 1)
            attend_vector(t, NA_H, 0.125, lambda h: na_bias[:, h, :, :], pair_of(brT), gate_vector(t))
            branch_vector(t, 0)

        def branch_vector(t, n):
            dve = t.e
            down_vector(t, 4)
            dve.wait_ge(acc_full, t.see(acc_full))
            dst = gt if n else mix
            for a in range(TT):
                if a:
                    dve.wait_ge(piece_done, PARTS + t.piece + 1)
                t.link(dve.tensor_tensor(dst[:, a, :], acc2()[:, a, :], gt[:, a, :], ALU.mult))
                if n:
                    ins = dve.tensor_tensor(mix[:, a, :], mix[:, a, :], gt[:, a, :], ALU.add)
                    if n == 2:
                        ins.then_inc(flip_src, 1)
                    else:
                        t.link(ins)
            dve.sem_inc(acc_taken, 1)
            t.see(acc_taken)
            if n < 2:
                next_lo(t)

        def gla_tensor(t, l):
            pe = t.e
            b = claim(t)
            for d in range(2):
                for a in range(TT):
                    mm = pe.transpose(bank[0:16, b, d * S + a * P:d * S + (a + 1) * P],
                                      z[:, a, Z_GL + 16 * d:Z_GL + 16 * d + 16], ident)
            mm.then_inc(full[b], 1)
            flip_tensor(t, lambda k, a: z[:, a, Z_GQ + k * P:Z_GQ + (k + 1) * P], 2)
            flip_tensor(t, lambda k, a: z[:, a, Z_GK + k * P:Z_GK + (k + 1) * P], 2)
            all_taken(t)
            for d in range(2):
                b = claim(t)
                for a in range(TT):
                    mm = pe.matmul(bank[:, b, a * 256:(a + 1) * 256], glT[:, d, a * P:(a + 1) * P],
                                   gate_up[:, l, d, :], start=True, stop=True)
                mm.then_inc(full[b], 1)
            project_tensor(t, [COLS] * 2)
            pe.wait_ge(dve_operand, t.see(dve_operand))
            for d, incl, rest in ((0, C_LE, C_GT), (1, C_GE, C_LT)):
                b = claim(t)
                for j in range(2):
                    for a in range(TT):
                        mm = pe.matmul(bank[:, b, j * S + a * P:j * S + (a + 1) * P], gg[:, d, a, j * P:(j + 1) * P],
                                       const[:, incl:incl + P], start=True, stop=True)
                mm.then_inc(full[b], 1)
                b = claim(t)
                for a in range(TT):
                    mm = pe.matmul(bank[:, b, a * 256:(a + 1) * 256], const[:, rest:rest + P], gg[:, d, a, :],
                                   start=True, stop=True)
                mm.then_inc(full[b], 1)
            project_tensor(t, [COLS])
            pe.wait_ge(dve_operand, t.see(dve_operand))
            for h in range(GLA_H):
                b = claim(t)
                r, j = 64 * (h % 2), h // 2
                for d in range(2):
                    for a in range(TT):
                        o = (d * TT + a) * P
                        mm = pe.matmul(bank[:, b, o:o + P], em[r:r + 64, d, j, a * P:(a + 1) * P],
                                       ep[r:r + 64, d, j, a * P:(a + 1) * P], start=True, stop=True)
                mm.then_inc(full[b], 1)
            for d in range(2):
                for half in range(2):
                    b = claim(t)
                    r = 64 * half
                    for n in range(3):
                        c = n if d == 0 else 3 - n
                        if c % 2 != half:
                            continue
                        for h in range(GLA_H):
                            o = (h // 2 * 2 + n // 2) * P
                            mm = pe.matmul(bank[64 * (h % 2):64 * (h % 2) + 64, b, o:o + P],
                                           ke[r:r + 64, d, c // 2, h * 64:(h + 1) * 64],
                                           z[r:r + 64, c // 2, Z_GV + h * P:Z_GV + (h + 1) * P], start=True, stop=True)
                    mm.then_inc(full[b], 1)
            pe.wait_ge(dve_operand, t.see(dve_operand))
            for parity in range(2):
                b = claim(t)
                r = 64 * parity
                for j in range(2):
                    h = 2 * j + parity
                    for a in range(TT):
                        o = (j * TT + a) * P
                        pe.matmul(bank[:, b, o:o + P], a_in[:, h, a, :], z[:, a, Z_GV + h * P:Z_GV + (h + 1) * P],
                                  start=True, stop=False, skip_group_check=True)
                        for c in (2 * a, 2 * a + 1):
                            for d in range(2):
                                n = c - 1 if d == 0 else 2 - c
                                if n < 0:
                                    continue
                                mm = pe.matmul(bank[64 * (c % 2):64 * (c % 2) + 64, b, o:o + P],
                                               ep[r:r + 64, d, j, c * 64:(c + 1) * 64], gst[r:r + 64, d, j, n, :],
                                               start=False, stop=False, skip_group_check=True)
                mm.then_inc(full[b], 1)
            project_tensor(t, [COLS])
            flip_tensor(t, lambda k, a: go[:, a, k, :], 4)
            all_taken(t)
            down_tensor(t, brT, 4)

        def gla_scalar(t, l):
            act = t.e
            b = filled(t)
            act.activation(glT[:, :, :], bank[0:16, b, :].rearrange("p (d s) -> p d s", d=2), ACT.Copy)\
                .then_inc(taken[b], 1)
            flip_scalar(t, gqT, 2, float(GLA_DK) ** -0.5)
            flip_scalar(t, gkT, 2)
            t.banks.take(), t.banks.take()
            act.wait_ge(to_act, t.see(to_act))
            t.link(act.activation(ge[:, :, :, :], ge[:, :, :, :], ACT.Exp))
            act.activation(ge[:, :, :, :], ge[:, :, :, :], ACT.Ln, bias=1.0).then_inc(to_dve, 1)
            gate_quarter(t, 0)
            gate_quarter(t, 1)
            tau = 1.0 / 16.0
            for d in range(2):
                b = filled(t)
                act.activation(ep[:, d, :, :], bank_of(b).rearrange("p (j s) -> p j s", j=2), ACT.Exp, scale=tau)
                act.activation(em[:, d, :, :], bank_of(b).rearrange("p (j s) -> p j s", j=2), ACT.Exp, scale=-tau)\
                    .then_inc(taken[b], 1)
                b = filled(t)
                act.activation(ke[:, d, :, :], bank_of(b).rearrange("p (a n) -> p a n", a=TT), ACT.Exp, scale=tau)\
                    .then_inc(taken[b], 1)
            gate_quarter(t, 2)
            for _ in range(8):
                t.banks.take()
            for parity in range(2):
                b = filled(t)
                act.activation(go[:, :, parity::2, :].rearrange("p a j v -> p j a v"),
                               bank_of(b).rearrange("p (j a v) -> p j a v", j=2, a=TT), ACT.Copy).then_inc(taken[b], 1)
            rms_scalar(t, go[:, :, :, :].rearrange("p a h v -> p (a h) v"), TT * GLA_H, P)
            gate_quarter(t, 3)
            split_flip_scalar(t, brT, 4, lambda k: gain[:, G_GLA + l:G_GLA + l + 1])
            down_scalar(t, 4)

        def gla_vector(t, l):
            dve = t.e
            t.banks.take()
            flip_vector(t, gqT, 2, float(GLA_DK) ** -0.5)
            flip_vector(t, gkT, 2)
            for d in range(2):
                b = filled(t)
                bias = rows[:, R_GB + (2 * l + d) * 256:R_GB + (2 * l + d + 1) * 256]
                dve.tensor_tensor(gg[:, d, :, :], bank_of(b).rearrange("p (a n) -> p a n", a=TT),
                                  bias.unsqueeze(1).to_broadcast([P, TT, 256]), ALU.add).then_inc(taken[b], 1)
                dve.wait_ge(taken[b], t.banks.uses[b])
            g3, e3 = z[:, :, 0:512], z[:, :, 512:1024]
            dve.scalar_tensor_tensor(e3, g3, -1.0, g3, ALU.mult, ALU.min)\
                .then_inc(to_act, 1)
            dve.wait_ge(to_dve, t.see(to_dve))
            t.done(dve.scalar_tensor_tensor(g3, g3, 0.0, e3, ALU.min, ALU.subtract), dve_operand)
            project_vector(t, 2)
            for _ in range(4):
                t.banks.take()
            all_taken(t)
            t.link(dve.tensor_copy(gdec[:, 0, :, :], ep[:, 0, :, :].rearrange("p j (c n) -> p j c n", n=64)[:, :, :, 63]))
            t.link(dve.tensor_copy(gdec[:, 1, :, :], ep[:, 1, :, :].rearrange("p j (c n) -> p j c n", n=64)[:, :, :, 0]))
            for d in range(2):
                dve.tensor_tensor(ep[:, d, :, :], ep[:, d, :, :], gqT[:, :, :], ALU.mult)
                dve.tensor_tensor(em[:, d, :, :], em[:, d, :, :], gkT[:, :, :], ALU.mult)
                ins = dve.tensor_tensor(ke[:, d, :, :], ke[:, d, :, :], z[:, :, Z_GK:Z_GK + 256], ALU.mult)
            t.done(ins, dve_operand)
            project_vector(t, 1)
            masks = const[:, C_LE:C_LE + 2 * P].rearrange("p (d n) -> p d n", d=2)
            for h in range(GLA_H):
                b = filled(t)
                dve.tensor_tensor(am[:, :, :, :], bank_of(b).rearrange("p (d a n) -> p d a n", d=2, a=TT),
                                  masks.unsqueeze(2).to_broadcast([P, 2, TT, P]), ALU.mult).then_inc(taken[b], 1)
                dve.wait_ge(taken[b], t.banks.uses[b])
                t.link(dve.tensor_tensor(a_in[:, h, :, :], am[:, 0, :, :], am[:, 1, :, :], ALU.add))
            for d in range(2):
                of_half = [filled(t), filled(t)]
                for n in range(3):
                    c = n if d == 0 else 3 - n
                    for j in range(2):
                        o = (2 * j + n // 2) * P
                        added = bank[:, of_half[c % 2], o:o + P]
                        if n == 0:
                            ins = dve.tensor_copy(gst[:, d, j, 0, :], added)
                        else:
                            ins = dve.scalar_tensor_tensor(gst[:, d, j, n, :], gst[:, d, j, n - 1, :],
                                                           gdec[:, d, j, c:c + 1], added, ALU.mult, ALU.add)
                    if n < 2:
                        t.link(ins)
                ins.then_inc(taken[of_half[c % 2]], 1)
                dve.wait_ge(taken[of_half[c % 2]], t.banks.uses[of_half[c % 2]])
                dve.sem_inc(taken[of_half[1 - c % 2]], 1)
            dve.sem_inc(dve_operand, 1)
            t.banks.take(), t.banks.take()
            all_taken(t)
            rms_vector(t, go[:, :, :, :].rearrange("p a h v -> p (a h) v"), TT * GLA_H, P)
            t.link(dve.tensor_tensor(go[:, :, :, :].rearrange("p a h v -> p a (h v)"),
                                     go[:, :, :, :].rearrange("p a h v -> p a (h v)"),
                                     z[:, :, Z_GR:Z_GR + 512], ALU.mult))
            t.banks.take(by_piece=True)
            split_flip_vector(t, brT, 4, lambda k: gain[:, G_GLA + l:G_GLA + l + 1])
            next_lo(t)
            branch_vector(t, 1)

        def mla_tensor(t, l):
            pe = t.e
            flip_tensor(t, lambda k, a: z[:, a, Z_CQ + k * P:Z_CQ + (k + 1) * P], 2)
            flip_tensor(t, lambda k, a: z[:, a, Z_CKV + k * P:Z_CKV + (k + 1) * P], 2)
            all_taken(t)
            for i, n in enumerate((3, 4)):
                s = arrived(t)
                for c in range(n):
                    b = claim(t, by_piece=(c == n - 1))
                    for a in range(TT):
                        for k in range(2):
                            for p, q in PASSES:
                                mm = pe.matmul(bank[:, b, a * 256:(a + 1) * 256], cT[:, i, p, k, a * P:(a + 1) * P],
                                               slot_rows(s, q, n * 256)[:, k, c * 256:(c + 1) * 256],
                                               start=(k == 0 and p + q == 0), stop=(k == 1 and p == 1))
                    mm.then_inc(piece_done if c == n - 1 else full[b], 1)
            project_tensor(t, [COLS] * 4)
            flip_tensor(t, lambda h, a: lq[:, a, h, 0:P], 4)
            flip_tensor(t, lambda h, a: lq[:, a, h, P:MLA_QK], 4, 64)
            flip_tensor(t, lambda h, a: lk[:, a, h, 0:P], 4)
            flip_tensor(t, lambda h, a: lk[:, a, h, P:MLA_QK], 4, 64)
            attend_tensor(t, MLA_H, lambda h, a: [(lqT[:, h, a * P:(a + 1) * P], lkT[:, h, :]),
                                                  (lqrT[:, h, a * P:(a + 1) * P], lkrT[:, h, :])],
                          lambda h, st: lkv[:, st, h, P:2 * P], P, lambda h: 0)
            all_taken(t)
            down_tensor(t, brT, 4)

        def mla_scalar(t, l):
            act = t.e
            split_flip_scalar(t, cT[:, 0], 2, gain_col(G_CQ + 2 * l))
            split_flip_scalar(t, cT[:, 1], 2, gain_col(G_CKV + 2 * l))
            qf = lq[:, :, :, :].rearrange("p a h d -> p a (h d)")
            kf = lkv[:, :, :, :].rearrange("p a h d -> p a (h d)")
            for n, dst in ((3, qf), (4, kf)):
                for c in range(n):
                    if c == n - 1:
                        b = t.banks.take(by_piece=True)
                        next_hi(t)
                        act.wait_ge(piece_done, through(t))
                    else:
                        b = filled(t)
                    act.activation(dst[:, :, c * 256:(c + 1) * 256], halves(b), ACT.Copy).then_inc(taken[b], 1)
            for first, v in ((0, lq), (2, lk)):
                rms_scalar(t, v, TT * MLA_H, MLA_QK)
                gate_quarter(t, first)
                gate_quarter(t, first + 1)
            flip_scalar(t, lqT, 4)
            flip_scalar(t, lqrT, 4, None, 64)
            flip_scalar(t, lkT, 4)
            flip_scalar(t, lkrT, 4, None, 64)
            attend_scalar(t, MLA_H, lambda h: (lambda part: brT[:, part, h, :], 0, P))
            down_scalar(t, 4, to_x=True)

        def mla_vector(t, l):
            dve = t.e
            split_flip_vector(t, cT[:, 0], 2, gain_col(G_CQ + 2 * l))
            split_flip_vector(t, cT[:, 1], 2, gain_col(G_CKV + 2 * l))
            for n in (3, 4):
                for c in range(n):
                    t.banks.take(by_piece=(c == n - 1))
                next_lo(t)
            all_taken(t)
            dve.tensor_copy(lk[:, :, :, 0:P], lkv[:, :, :, 0:P])
            t.link(dve.tensor_copy(lk[:, :, :, P:MLA_QK],
                                   z[:, :, Z_KR:Z_KR + 64].unsqueeze(2).to_broadcast([P, TT, MLA_H, 64])))
            cos = const[:, C_COS:C_COS + 64].rearrange("p (a c) -> p a c", a=TT)
            sin = const[:, C_SIN:C_SIN + 64].rearrange("p (a c) -> p a c", a=TT)
            for v, g in ((lq, R_MQ), (lk, R_MK)):
                rms_vector(t, v, TT * MLA_H, MLA_QK, lambda: project_vector(t, 1))
                w = rows[:, g + MLA_QK * l:g + MLA_QK * (l + 1)]
                t.link(dve.tensor_tensor(v, v, w.unsqueeze(1).unsqueeze(1).to_broadcast([P, TT, MLA_H, MLA_QK]), ALU.mult))
                rotate(t, v[:, :, :, P:P + 32], v[:, :, :, P + 32:P + 64], cos, sin, MLA_H, z_rt)
                project_vector(t, 1)
            flip_vector(t, lqT, 4)
            flip_vector(t, lqrT, 4, None, 64)
            flip_vector(t, lkT, 4)
            flip_vector(t, lkrT, 4, None, 64)
            attend_vector(t, MLA_H, float(MLA_QK) ** -0.5, None, lambda h: (lambda part: brT[:, part, h, :], 0, P))
            branch_vector(t, 2)

        def triple_tensor(t, l):
            project_tensor(t, Z_W, hT_k=hT_waits(t))
            all_taken(t)
            na_tensor(t, l)
            gla_tensor(t, l)
            mla_tensor(t, l)
            for a, n, k0 in PRE_BANKS:
                if k0 == 0:
                    t.e.wait_ge(flip_src, t.see(flip_src))
                b = claim(t)
                for j in range(n):
                    mm = t.e.transpose(bank[:, b, j * P:(j + 1) * P], mix[:, a, (k0 + j) * P:(k0 + j + 1) * P], ident)
                mm.then_inc(full[b], 1)
            all_taken(t)
            down_tensor(t, hT, KD)

        Z_NORMS = ((3, Z_CQ, 1, 256, None), (5, Z_CKV, 1, 256, None), (9, Z_NQ, NA_H, 64, R_NAQ),
                   (11, Z_NK, NA_H, 64, R_NAK))

        def triple_scalar(t, l):
            def project(lo, hi):
                project_scalar(t, [z[:, :, i * COLS:i * COLS + w] for i, w in zip(Z_TILES[lo:hi], Z_W[lo:hi])])

            done = 0
            for n, at, heads, d, _ in Z_NORMS:
                project(done, n)
                done = n
                if n == 5:
                    for b in range(4):
                        t.e.wait_ge(taken[b], t.banks.uses[b])
                    t.e.activation(z[:, :, Z_GR:Z_GR + 512], z[:, :, Z_GR:Z_GR + 512], ACT.Silu).then_inc(to_dve, 1)
                rms_scalar(t, head_views(z, at, heads, d), TT * heads, d)
            project(done, len(Z_W))
            na_scalar(t, l)
            gla_scalar(t, l)
            mla_scalar(t, l)
            for a, n, k0 in PRE_BANKS:
                b = filled(t)
                t.e.activation(hT[:, 0, k0:k0 + n, a * P:(a + 1) * P],
                               bank[:, b, 0:n * P].rearrange("p (k s) -> p k s", s=P), ACT.Copy).then_inc(flip_hi, 1)
            next_hi(t)
            down_scalar(t, KD, to_x=True)

        def triple_vector(t, l):
            done = 0
            for n, at, heads, d, g in Z_NORMS:
                project_vector(t, n - done)
                done = n
                all_taken(t)
                v = head_views(z, at, heads, d)
                rms_vector(t, v, TT * heads, d)
                if g is not None:
                    t.link(t.e.tensor_tensor(v, v, rows[:, g + d * l:g + d * (l + 1)].unsqueeze(1).unsqueeze(1)
                                             .to_broadcast([P, TT, heads, d]), ALU.mult))
            project_vector(t, len(Z_W) - done)
            all_taken(t)
            t.e.wait_ge(to_dve, t.see(to_dve))
            na_vector(t, l)
            gla_vector(t, l)
            mla_vector(t, l)
            for a, n, k0 in PRE_BANKS:
                b = filled(t)
                t.e.wait_ge(flip_hi, t.see(flip_hi))
                t.e.tensor_tensor(hT[:, 1, k0:k0 + n, a * P:(a + 1) * P],
                                  bank[:, b, 0:n * P].rearrange("p (k s) -> p k s", s=P),
                                  hT[:, 0, k0:k0 + n, a * P:(a + 1) * P].bitcast(F32), ALU.subtract)\
                    .then_inc(taken[b], 1)
            next_lo(t)
            down_vector(t, KD)
            add_to_x(t, 1.0)

        FFNS = [(A["ffn_w_gate"][l, i], A["ffn_w_up"][l, i], A["ffn_w_down"][l, i], G_FFN + 8 * (2 * l + i))
                for l in range(DEPTH) for i in range(2)]
        for l in range(DEPTH):
            FFNS.append((A["ffn1_w1_2"][l], A["ffn1_w3_2"][l], A["ffn1_w2_2"][l], G_FFN1 + 8 * l))
            FFNS.append((A["ffn2_w1_2"][l], A["ffn2_w3_2"][l], A["ffn2_w2_2"][l], G_FFN2 + 8 * l))
        MIXERS = [(G_MIX, hybrid_sync, hybrid_tensor, hybrid_scalar, hybrid_vector, ()),
                  (G_MIX + 8, sparse_sync, sparse_tensor, sparse_scalar, sparse_vector, ())]
        MIXERS += [(G_MIX2 + 8 * l, triple_sync, triple_tensor, triple_scalar, triple_vector, (l,))
                   for l in range(DEPTH)]

        def flip_gains_scalar(t):
            b = filled(t)
            t.e.activation(gain[:, :], bank[:, b, 0:N_GA + N_GB], ACT.Copy).then_inc(taken[b], 1)
            t.e.wait_ge(taken[b], t.banks.uses[b])

        block = ctx.enter_context(nc.Block())

        @block.sync
        def _(sp):
            t = Thread(sp, steps["sp"])
            for n in range(4):
                ffn_sync(t, *FFNS[2 * n][:3])
                MIXERS[n][1](t, *MIXERS[n][5])
                ffn_sync(t, *FFNS[2 * n + 1][:3])
            sp.wait_ge(x_final, 1)
            sp.dma_start(out[0].rearrange("(a p) d -> p a d", p=P), x[:, :, :]).then_inc(out_done, 16)
            sp.wait_ge(out_done, 16)

        smalls = []

        def small(dst, src):
            smalls.append((dst, src))

        small(x[:, :, :], A["x"][0].rearrange("(a p) d -> p a d", p=P))
        small(const[:, :], A["constants"])
        at = 0
        for name in ("ffn_norm", "mix_norm", "ffn1_norm_2", "mix_norm_2", "ffn2_norm_2"):
            v = A[name].rearrange("l i (k p) -> (l i k) p", p=P) if len(A[name].shape) == 3 else \
                A[name].rearrange("l (k p) -> (l k) p", p=P)
            small(gain_rows[at:at + v.shape[0], 0, :], v)
            at += v.shape[0]
        at = 0
        for v in (A["hy_conv_w"][0].rearrange("t (k p) -> (t k) p", p=P),
                  A["hy_conv_b"].rearrange("l (k p) -> (l k) p", p=P),
                  A["hy_ssd_norm"].rearrange("l (k p) -> (l k) p", p=P),
                  A["hy_mlstm_norm"].rearrange("l (k p) -> (l k) p", p=P),
                  A["gla_out_norm_2"],
                  A["mla_cq_norm_2"].rearrange("l (k p) -> (l k) p", p=P),
                  A["mla_ckv_norm_2"].rearrange("l (k p) -> (l k) p", p=P)):
            small(gain_rows[at:at + v.shape[0], 1, :], v)
            at += v.shape[0]
        firsts, smalls = smalls, []
        small(pos_i[:, :], A["positions"][0].rearrange("(a p) -> p a", p=P))
        small(rows[:, R_DSKIP:R_DSKIP + 16], A["hy_d_skip"][0].partition_broadcast(P))
        small(rows[:, R_SAQ:R_SAQ + 64], A["sa_q_norm"][0].partition_broadcast(P))
        small(rows[:, R_SAK:R_SAK + 64], A["sa_k_norm"][0].partition_broadcast(P))
        for l in range(DEPTH):
            small(rows[:, R_NAQ + 64 * l:R_NAQ + 64 * (l + 1)], A["na_q_norm_2"][l].partition_broadcast(P))
            small(rows[:, R_NAK + 64 * l:R_NAK + 64 * (l + 1)], A["na_k_norm_2"][l].partition_broadcast(P))
            small(rows[:, R_MQ + 192 * l:R_MQ + 192 * (l + 1)], A["mla_q_norm_2"][l].partition_broadcast(P))
            small(rows[:, R_MK + 192 * l:R_MK + 192 * (l + 1)], A["mla_k_norm_2"][l].partition_broadcast(P))
            for d, n in enumerate(("gf", "gb")):
                small(rows[:, R_GB + (2 * l + d) * 256:R_GB + (2 * l + d + 1) * 256],
                      A[f"gla_{n}_bias_2"][l].partition_broadcast(P))
                small(gate_up[:, l, d, :], A[f"gla_{n}_up_2"][l])
        small(heads_in[:, 0:1], A["hy_dt_bias"][0].unsqueeze(1))
        small(heads_in[:, 1:2], A["hy_a_log"][0].unsqueeze(1))
        small(heads_in[0:ML_H, 2:3], A["hy_igate_bias"][0].unsqueeze(1))
        small(fg_bias[:, :], A["hy_fgate_bias"][0].unsqueeze(1))
        wg3 = A["hy_w_in"][0].rearrange("(k p) c -> p k c", p=P)
        small(w_gates[:, :, 0:16], wg3[:, :, HY_DT:HY_DT + 16])
        small(w_gates[:, :, 16:24], wg3[:, :, HY_IG:HY_IG + 8])
        ALL_FIRST, ALL_SMALL = 16 * len(firsts), 16 * len(smalls)

        @block.scalar
        def _(act):
            t = Thread(act, steps["act"])
            for dst, src in firsts:
                act.dma_start(dst, src).then_inc(first_in, 16)
            act.wait_ge(first_in, ALL_FIRST)
            flip_gains_scalar(t)
            for n in range(PARTS):
                split_hi(t, n)
            pre_scalar(t, FFNS[0][3])
            act.wait_ge(small_in, ALL_SMALL)
            act.activation(w_gates_s[:, 0, :, :], w_gates[:, :, :], ACT.Copy).then_inc(setup_a, 1)
            act.wait_ge(to_act, t.see(to_act))
            act.activation(rope1[:, 1, :, :].rearrange("p a c -> p (a c)"), rope_t[:, 0, :], ACT.Sin)
            act.activation(rope1[:, 0, :, :].rearrange("p a c -> p (a c)"), rope_t[:, 1, :], ACT.Sin).then_inc(to_dve, 1)
            for n in range(4):
                if n:
                    pre_scalar(t, FFNS[2 * n][3])
                ffn_scalar(t, 2 * n)
                pre_scalar(t, MIXERS[n][0])
                MIXERS[n][3](t, *MIXERS[n][5])
                pre_scalar(t, FFNS[2 * n + 1][3])
                ffn_scalar(t, 2 * n + 1)

        @block.gpsimd
        def _(pool):
            t = Thread(pool, steps["pool"])
            with nc.allow_non_contiguous_dma(reason="one position and one bias per partition"):
                for dst, src in smalls:
                    pool.dma_start(dst, src).then_inc(small_in, 16)
            pool.wait_ge(first_in, ALL_FIRST)
            pool.wait_ge(small_in, ALL_SMALL)
            pool.wait_ge(queries_normed, 1)
            v = head_views(sa, 0, SA_H)
            t.link(pool.tensor_tensor(v, v, rows[:, R_SAQ:R_SAQ + 64].unsqueeze(1).unsqueeze(1)
                                      .to_broadcast([P, TT, SA_H, 64]), ALU.mult))
            rotate(t, v[:, :, :, 0:32], v[:, :, :, 32:64], rope1[:, 0, :, :], rope1[:, 1, :, :], SA_H, sa_rt)
            pool.sem_inc(queries_rotated, 1)
            win = const[:, C_WIN:C_WIN + GRID_W]
            for l in range(DEPTH):
                pool.wait_ge(bias_room, l + 1)
                rpb = A["na_rpb_2"]
                for a in range(TT):
                    for half in range(2):
                        for r in range(ROWS):
                            row = r - (2 * a + half) + WIN_R - 1
                            src = bass.AP(tensor=rpb.tensor,
                                          offset=(l * NA_H * RPB_R + row) * RPB_C + WIN_C - GRID_W,
                                          ap=[[1, GRID_W], [RPB_R * RPB_C, NA_H], [1, GRID_W]])
                            dst = na_bias[half * 64:(half + 1) * 64, :, a, r * GRID_W:(r + 1) * GRID_W]
                            pool.dma_start(dst, src).then_inc(bias_in, 16)
                pool.wait_ge(bias_in, 16 * 4 * ROWS * (l + 1))
                for h in range(NA_H):
                    v = na_bias[:, h, :, :].rearrange("p a (r c) -> p (a r) c", c=GRID_W)
                    t.link(pool.tensor_tensor(v, v, win.unsqueeze(1).to_broadcast([P, TT * ROWS, GRID_W]), ALU.add))
                pool.sem_inc(bias_ready, 1)

        @block.vector
        def _(dve):
            t = Thread(dve, steps["dve"])
            dve.sem_inc(lo_ready, RAW)
            dve.memset(zeros[:, :], 0.0)
            t.done(dve.memset(ones[:, :], 1.0), setup_v)
            dve.wait_ge(first_in, ALL_FIRST)
            dve.sem_inc(norm_src, 2)
            t.see(norm_src, 2)
            t.banks.take()
            all_taken(t)
            for n in range(PARTS):
                split_lo(t, n)
            pre_vector(t, FFNS[0][3])
            dve.wait_ge(small_in, ALL_SMALL)
            dve.wait_ge(setup_a, 1)
            dve.tensor_tensor(w_gates_s[:, 1, :, :], w_gates[:, :, :], w_gates_s[:, 0, :, :].bitcast(F32), ALU.subtract)
            two_pi = 2 * np.pi
            t.link(dve.tensor_copy(pos_f[:, :], pos_i[:, :]))
            inv = const[:, C_INV:C_INV + 32]
            ang, n = rope_t[:, 0, :], rope_t[:, 2, :]
            for a in range(TT):
                t.link(dve.tensor_scalar(rope_t[:, 0, a * 32:(a + 1) * 32], inv, pos_f[:, a:a + 1], None, ALU.mult))
            magic = 1.5 * 2.0 ** 23
            t.link(dve.tensor_scalar(n, ang, 1.0 / two_pi, magic, ALU.mult, ALU.add))
            t.link(dve.tensor_scalar(n, n, magic, None, ALU.subtract))
            c1 = 6.28125
            c2 = float(np.float32(np.floor((two_pi - c1) * 2 ** 24) / 2 ** 24))
            c3 = two_pi - c1 - c2
            for c in (c1, c2, c3):
                t.link(dve.scalar_tensor_tensor(ang, n, -c, ang, ALU.mult, ALU.add))
            t.link(dve.tensor_scalar(rope_t[:, 1, :], ang, np.pi / 2, -two_pi, ALU.is_gt, ALU.mult))
            t.link(dve.scalar_tensor_tensor(rope_t[:, 1, :], ang, np.pi / 2, rope_t[:, 1, :], ALU.add, ALU.add))
            pi_in = 3.1415925
            t.link(dve.tensor_scalar(rope_t[:, 0:2, :], rope_t[:, 0:2, :], pi_in, -pi_in, ALU.min, ALU.max))
            dve.sem_inc(to_act, 1)
            dve.wait_ge(to_dve, t.see(to_dve))
            for n in range(4):
                if n:
                    pre_vector(t, FFNS[2 * n][3])
                ffn_vector(t, 2 * n)
                pre_vector(t, MIXERS[n][0])
                MIXERS[n][4](t, *MIXERS[n][5])
                if n in (1, 2):
                    dve.sem_inc(bias_room, 1)
                pre_vector(t, FFNS[2 * n + 1][3])
                ffn_vector(t, 2 * n + 1)
            dve.sem_inc(x_final, 1)

        @block.tensor
        def _(pe):
            t = Thread(pe, steps["pe"])
            t.acc_uses = 0
            pe.sem_inc(piece_done, PARTS)
            pe.wait_ge(setup_v, 1)
            pe.wait_ge(first_in, ALL_FIRST)
            b = claim(t)
            pe.transpose(bank[:, b, 0:N_GA], gain_rows[0:N_GA, 0, :], const[0:N_GA, C_ID:C_ID + N_GA])
            pe.transpose(bank[:, b, N_GA:N_GA + N_GB], gain_rows[0:N_GB, 1, :], const[0:N_GB, C_ID:C_ID + N_GB])\
                .then_inc(full[b], 1)
            for n in range(4):
                pre_tensor(t, FFNS[2 * n][3])
                ffn_tensor(t, 2 * n)
                pre_tensor(t, MIXERS[n][0])
                MIXERS[n][2](t, *MIXERS[n][5])
                pre_tensor(t, FFNS[2 * n + 1][3])
                ffn_tensor(t, 2 * n + 1)


_INS = ["x", "positions", "ffn_norm", "ffn_w_gate", "ffn_w_up", "ffn_w_down", "mix_norm", "hy_w_in", "hy_conv_w",
        "hy_conv_b", "hy_dt_bias", "hy_a_log", "hy_d_skip", "hy_ssd_norm", "hy_igate_bias", "hy_fgate_bias",
        "hy_mlstm_norm", "hy_w_out", "sa_w_in", "sa_q_norm", "sa_k_norm", "sa_w_out", "ffn1_norm_2", "ffn1_w1_2",
        "ffn1_w3_2", "ffn1_w2_2", "mix_norm_2", "w_in_2", "na_q_norm_2", "na_k_norm_2", "na_rpb_2", "gla_gf_up_2",
        "gla_gf_bias_2", "gla_gb_up_2", "gla_gb_bias_2", "gla_out_norm_2", "mla_cq_norm_2", "mla_ckv_norm_2",
        "mla_w_uq_2", "mla_w_ukv_2", "mla_q_norm_2", "mla_k_norm_2", "w_br_na_2", "w_br_gla_2", "w_br_mla_2",
        "w_out_2", "ffn2_norm_2", "ffn2_w1_2", "ffn2_w3_2", "ffn2_w2_2"]


def kernel(**inputs):
    import concourse.bacc as bacc
    from concourse.bass_utils import run_bass_kernel_spmd

    nc = bacc.Bacc("TRN2", target_bir_lowering=False, num_devices=1)
    arrays, aps = {}, {}
    for name in _INS:
        a = np.ascontiguousarray(inputs[name])
        arrays[f"in_{name}"] = a
        aps[name] = nc.dram_tensor(f"in_{name}", a.shape, mybir.dt.from_np(a.dtype), kind="ExternalInput").ap()
    arrays["in_constants"] = constants()
    aps["constants"] = nc.dram_tensor("in_constants", (P, N_CONST), F32, kind="ExternalInput").ap()
    out = nc.dram_tensor("out_x", (1, S, D), F32, kind="ExternalOutput").ap()
    two_blocks(nc, aps, out)
    r = run_bass_kernel_spmd(nc, [arrays], core_ids=[0])
    return r.results[0]["out_x"]
```
